# Optimizing a Trainium2 kernel written in Bass

```python
import math
import jax, jax.numpy as jnp
from jax import lax
import numpy as np

D_MODEL = 2048
BATCH = 1
SEQ = 256
DEPTH = 2

GDN_HEADS = 8
GDN_HD = 128
GDN_W = GDN_HEADS * GDN_HD
GDN_CONV = 4
GDN_CHUNK = 64
SC_WIDTH = D_MODEL // 2
SC_CONV = 3
NSA_HEADS = 16
NSA_KV = 4
NSA_HD = 128
NSA_Q = NSA_HEADS * NSA_HD
NSA_KVW = NSA_KV * NSA_HD
CMP_LEN = 32
CMP_STRIDE = 16
CMP_HID = 256
SEL_BLOCK = 64
SEL_N = 16
WIN = 512
ATT_QBLK = 128
SEL_QBLK = 32
FORCE_BONUS = 1000.0
ROPE_THETA = 10000.0
D_FF = 5632
FFN_CONV = 3
EPS = 1e-6
NEG = -1e30

AB_COLS = 4 * GDN_W + 2 * GDN_HEADS + 3 * SC_WIDTH
NSA_COLS = NSA_Q + 6 * NSA_KVW + 3 * NSA_HEADS

kernel_name = "hybrid_deltanet_shortconv_nsa_convffn"

def split_cols(t, widths):
    offs = np.cumsum(widths)[:-1].tolist()
    return jnp.split(t, offs, axis=-1)

def rmsnorm(x, w):
    xf = x.astype(jnp.float32)
    y = xf * lax.rsqrt(jnp.mean(xf * xf, axis=-1, keepdims=True) + EPS)
    return (y * w.astype(jnp.float32)).astype(x.dtype)

def l2norm(x):
    return x * lax.rsqrt(jnp.sum(x * x, axis=-1, keepdims=True) + EPS)

def causal_dwconv(x, w):
    K = w.shape[0]
    S = x.shape[1]
    xp = jnp.pad(x, ((0, 0), (K - 1, 0), (0, 0)))
    return sum(xp[:, k:k + S] * w[k] for k in range(K))

def rope_tables(S, dim):
    inv = 1.0 / (ROPE_THETA ** (jnp.arange(0, dim, 2, dtype=jnp.float32) / dim))
    ang = jnp.arange(S, dtype=jnp.float32)[:, None] * inv[None, :]
    return jnp.cos(ang), jnp.sin(ang)

def apply_rope(x, cos, sin):
    x1, x2 = jnp.split(x, 2, axis=-1)
    c = cos[None, :, None, :]
    s = sin[None, :, None, :]
    return jnp.concatenate([x1 * c - x2 * s, x2 * c + x1 * s], axis=-1)

def gated_delta_chunked(q, k, v, g, beta):
    B, H, S, D = q.shape
    C = GDN_CHUNK
    N = S // C
    q = q * (D ** -0.5)
    rs = lambda t: t.reshape((B, H, N, C) + t.shape[3:])
    q, k, v, beta = rs(q), rs(k), rs(v), rs(beta)
    g = jnp.cumsum(rs(g), axis=-1)
    kb = k * beta[..., None]
    vb = v * beta[..., None]
    tril = jnp.tril(jnp.ones((C, C), dtype=bool))
    stril = jnp.tril(jnp.ones((C, C), dtype=bool), -1)
    gdiff = g[..., :, None] - g[..., None, :]
    decay = jnp.where(tril, jnp.exp(jnp.where(tril, gdiff, 0.0)), 0.0)
    Lm = jnp.where(stril, jnp.einsum('bhnid,bhnjd->bhnij', kb, k) * decay, 0.0)
    eye = jnp.eye(C, dtype=jnp.float32)
    T = lax.linalg.triangular_solve(eye + Lm, jnp.broadcast_to(eye, Lm.shape),
                                    left_side=True, lower=True)
    u = T @ vb
    w = T @ (kb * jnp.exp(g)[..., None])
    qk = jnp.where(tril, jnp.einsum('bhnid,bhnjd->bhnij', q, k) * decay, 0.0)

    def step(state, xs):
        qc, kc, uc, wc, gc, ac = xs
        vnew = uc - wc @ state
        o = (qc * jnp.exp(gc)[..., None]) @ state + ac @ vnew
        glast = gc[..., -1]
        kdec = kc * jnp.exp(glast[..., None] - gc)[..., None]
        state = state * jnp.exp(glast)[..., None, None] + jnp.einsum('bhcd,bhce->bhde', kdec, vnew)
        return state, o

    xs = tuple(jnp.moveaxis(t, 2, 0) for t in (q, k, u, w, g, qk))
    s0 = jnp.zeros((B, H, D, D), jnp.float32)
    _, o = lax.scan(step, s0, xs)
    return jnp.moveaxis(o, 0, 2).reshape(B, H, S, D)

def delta_shortconv_mixer(xn, w_in, w_out, conv_qkv, a_log, dt_bias, o_norm, conv_sc):
    B, S, _ = xn.shape
    H, D = GDN_HEADS, GDN_HD
    f32 = jnp.float32
    q, k, v, z, a, b, hb, gb, gc = split_cols(xn @ w_in, [H * D] * 4 + [H] * 2 + [SC_WIDTH] * 3)
    qkv = jax.nn.silu(causal_dwconv(jnp.concatenate([q, k, v], axis=-1), conv_qkv)).astype(f32)
    q, k, v = [t.reshape(B, S, H, D).transpose(0, 2, 1, 3) for t in jnp.split(qkv, 3, axis=-1)]
    g = -jnp.exp(a_log.astype(f32)) * jax.nn.softplus(a.astype(f32) + dt_bias.astype(f32))
    beta = jax.nn.sigmoid(b.astype(f32))
    o = gated_delta_chunked(l2norm(q), l2norm(k), v, g.transpose(0, 2, 1), beta.transpose(0, 2, 1))
    o = rmsnorm(o.transpose(0, 2, 1, 3), o_norm) * jax.nn.silu(z.astype(f32).reshape(B, S, H, D))
    y_a = o.reshape(B, S, H * D).astype(xn.dtype)
    y_b = gb * causal_dwconv(gc * hb, conv_sc)
    return jnp.concatenate([y_a, y_b], axis=-1) @ w_out

def nsa_compress(t, pos, w1, w2):
    B, G, S, D = t.shape
    r = CMP_LEN // CMP_STRIDE
    nc = S // CMP_STRIDE - r + 1
    tr = t.reshape(B, G, S // CMP_STRIDE, CMP_STRIDE, D)
    blocks = jnp.concatenate([tr[:, :, j:j + nc] for j in range(r)], axis=3)
    blocks = (blocks + pos).reshape(B, G, nc, CMP_LEN * D)
    return jax.nn.gelu(blocks @ w1) @ w2

def nsa_compressed_branch(q, kc, vc):
    S = q.shape[3]
    nc = kc.shape[2]
    t = jnp.arange(S)
    valid = (jnp.arange(nc) * CMP_STRIDE + CMP_LEN - 1)[None, :] <= t[:, None]
    s = jnp.einsum('bgrsd,bgcd->bgrsc', q, kc)
    p = jnp.where(valid, jax.nn.softmax(jnp.where(valid, s, NEG), axis=-1), 0.0)
    return jnp.einsum('bgrsc,bgcd->bgrsd', p, vc), p

def nsa_selected_branch(q, k, v, p_cmp):
    B, G, R, S, D = q.shape
    nc = p_cmp.shape[-1]
    ns = S // SEL_BLOCK
    n_sel = min(SEL_N, ns)
    cs = jnp.arange(nc) * CMP_STRIDE
    ss = jnp.arange(ns) * SEL_BLOCK
    ov = jnp.minimum(cs[:, None] + CMP_LEN, ss[None, :] + SEL_BLOCK) - jnp.maximum(cs[:, None], ss[None, :])
    M = (jnp.clip(ov, 0, None) / CMP_STRIDE).astype(jnp.float32)
    score = jnp.einsum('bgrsc,cn->bgsn', p_cmp, M)
    t = jnp.arange(S)
    blk = jnp.arange(ns)
    cur = (t // SEL_BLOCK)[:, None]
    valid = blk[None, :] * SEL_BLOCK <= t[:, None]
    forced = (blk[None, :] == 0) | (blk[None, :] == cur) | (blk[None, :] == cur - 1)
    score = jnp.where(valid, score + jnp.where(forced, FORCE_BONUS, 0.0), NEG)
    _, idx = lax.top_k(score, n_sel)

    kb = k.reshape(B, G, ns, SEL_BLOCK, D)
    vb = v.reshape(B, G, ns, SEL_BLOCK, D)
    nq = S // SEL_QBLK
    q_ch = q.reshape(B, G, R, nq, SEL_QBLK, D).transpose(3, 0, 1, 2, 4, 5)
    i_ch = idx.reshape(B, G, nq, SEL_QBLK, n_sel).transpose(2, 0, 1, 3, 4)
    t_ch = t.reshape(nq, SEL_QBLK)
    bi = jnp.arange(B)[:, None, None, None]
    gi = jnp.arange(G)[None, :, None, None]

    def block(args):
        qb, ib, tb = args
        kg = kb[bi, gi, ib].reshape(B, G, SEL_QBLK, n_sel * SEL_BLOCK, D)
        vg = vb[bi, gi, ib].reshape(B, G, SEL_QBLK, n_sel * SEL_BLOCK, D)
        kpos = (ib[..., None] * SEL_BLOCK + jnp.arange(SEL_BLOCK)).reshape(B, G, SEL_QBLK, n_sel * SEL_BLOCK)
        mask = (kpos <= tb[None, None, :, None])[:, :, None]
        s = jnp.einsum('bgrqd,bgqkd->bgrqk', qb, kg)
        p = jax.nn.softmax(jnp.where(mask, s, NEG), axis=-1)
        return jnp.einsum('bgrqk,bgqkd->bgrqd', p, vg)

    o = lax.map(block, (q_ch, i_ch, t_ch))
    return o.transpose(1, 2, 3, 0, 4, 5).reshape(B, G, R, S, D)

def nsa_window_branch(q, k, v):
    B, G, R, S, D = q.shape
    QB = ATT_QBLK
    KL = WIN + QB
    nb = S // QB
    kp = jnp.pad(k, ((0, 0), (0, 0), (WIN, 0), (0, 0)))
    vp = jnp.pad(v, ((0, 0), (0, 0), (WIN, 0), (0, 0)))
    q_bl = q.reshape(B, G, R, nb, QB, D).transpose(3, 0, 1, 2, 4, 5)

    def block(args):
        qb, i = args
        start = i * QB
        kb = lax.dynamic_slice_in_dim(kp, start, KL, axis=2)
        vb = lax.dynamic_slice_in_dim(vp, start, KL, axis=2)
        tq = start + jnp.arange(QB)
        tk = start - WIN + jnp.arange(KL)
        mask = (tk[None, :] <= tq[:, None]) & (tk[None, :] > tq[:, None] - WIN) & (tk[None, :] >= 0)
        s = jnp.einsum('bgrqd,bgkd->bgrqk', qb, kb)
        p = jax.nn.softmax(jnp.where(mask, s, NEG), axis=-1)
        return jnp.einsum('bgrqk,bgkd->bgrqd', p, vb)

    o = lax.map(block, (q_bl, jnp.arange(nb)))
    return o.transpose(1, 2, 3, 0, 4, 5).reshape(B, G, R, S, D)

def nsa_mixer(xn, w_in, w_out, pos_k, w1_k, w2_k, pos_v, w1_v, w2_v, cos, sin):
    B, S, _ = xn.shape
    H, G, D = NSA_HEADS, NSA_KV, NSA_HD
    R = H // G
    f32 = jnp.float32
    q, kc, vc, ks, vs, kw, vw, gt = split_cols((xn @ w_in).astype(f32), [H * D] + [G * D] * 6 + [3 * H])
    q = apply_rope(q.reshape(B, S, H, D), cos, sin) * (D ** -0.5)
    q = q.reshape(B, S, G, R, D).transpose(0, 2, 3, 1, 4)
    rk = lambda t: apply_rope(t.reshape(B, S, G, D), cos, sin).transpose(0, 2, 1, 3)
    rv = lambda t: t.reshape(B, S, G, D).transpose(0, 2, 1, 3)
    kc, ks, kw = rk(kc), rk(ks), rk(kw)
    vc, vs, vw = rv(vc), rv(vs), rv(vw)
    gates = jax.nn.sigmoid(gt).reshape(B, S, 3, G, R).transpose(2, 0, 3, 4, 1)[..., None]
    kcmp = nsa_compress(kc, pos_k.astype(f32), w1_k.astype(f32), w2_k.astype(f32))
    vcmp = nsa_compress(vc, pos_v.astype(f32), w1_v.astype(f32), w2_v.astype(f32))
    o_cmp, p_cmp = nsa_compressed_branch(q, kcmp, vcmp)
    o_slc = nsa_selected_branch(q, ks, vs, p_cmp)
    o_win = nsa_window_branch(q, kw, vw)
    o = gates[0] * o_cmp + gates[1] * o_slc + gates[2] * o_win
    o = o.transpose(0, 3, 1, 2, 4).reshape(B, S, H * D).astype(xn.dtype)
    return o @ w_out

def conv_ffn(xn, w_gu, conv_w, w_down):
    gate, up = jnp.split(xn @ w_gu, 2, axis=-1)
    return (jax.nn.silu(causal_dwconv(gate, conv_w)) * up) @ w_down

def setup_inputs(seed: int = 0) -> dict:
    key = jax.random.key(seed)
    ks = iter(jax.random.split(key, 32))
    nrm = lambda shape, scale: jax.random.normal(next(ks), shape, jnp.float32) * scale
    NE = (DEPTH + 1) // 2
    NO = DEPTH // 2
    x = nrm((BATCH, SEQ, D_MODEL), 1.0)
    norm_w = 1.0 + nrm((DEPTH, 4, D_MODEL), 0.02)
    ab_w_in = nrm((NE, D_MODEL, AB_COLS), D_MODEL ** -0.5)
    ab_w_out = nrm((NE, GDN_W + SC_WIDTH, D_MODEL), (GDN_W + SC_WIDTH) ** -0.5)
    gdn_conv = nrm((NE, GDN_CONV, 3 * GDN_W), GDN_CONV ** -0.5)
    gdn_a_log = jnp.log(jax.random.uniform(next(ks), (NE, GDN_HEADS), jnp.float32, 1.0, 16.0))
    dt = jnp.exp(jax.random.uniform(next(ks), (NE, GDN_HEADS), jnp.float32, math.log(1e-3), math.log(1e-1)))
    gdn_dt_bias = dt + jnp.log(-jnp.expm1(-dt))
    gdn_norm = 1.0 + nrm((NE, GDN_HD), 0.02)
    sc_conv = nrm((NE, SC_CONV, SC_WIDTH), SC_CONV ** -0.5)
    nsa_w_in = nrm((NO, D_MODEL, NSA_COLS), D_MODEL ** -0.5)
    nsa_w_out = nrm((NO, NSA_Q, D_MODEL), NSA_Q ** -0.5)
    cmp_pos_k = nrm((NO, CMP_LEN, NSA_HD), 0.02)
    cmp_w1_k = nrm((NO, CMP_LEN * NSA_HD, CMP_HID), (CMP_LEN * NSA_HD) ** -0.5)
    cmp_w2_k = nrm((NO, CMP_HID, NSA_HD), CMP_HID ** -0.5)
    cmp_pos_v = nrm((NO, CMP_LEN, NSA_HD), 0.02)
    cmp_w1_v = nrm((NO, CMP_LEN * NSA_HD, CMP_HID), (CMP_LEN * NSA_HD) ** -0.5)
    cmp_w2_v = nrm((NO, CMP_HID, NSA_HD), CMP_HID ** -0.5)
    ffn_w_gu = nrm((DEPTH, D_MODEL, 2 * D_FF), D_MODEL ** -0.5)
    ffn_conv = nrm((DEPTH, FFN_CONV, D_FF), FFN_CONV ** -0.5)
    ffn_w_down = nrm((DEPTH, D_FF, D_MODEL), D_FF ** -0.5)
    return {"x": x, "norm_w": norm_w, "ab_w_in": ab_w_in, "ab_w_out": ab_w_out,
            "gdn_conv": gdn_conv, "gdn_a_log": gdn_a_log, "gdn_dt_bias": gdn_dt_bias,
            "gdn_norm": gdn_norm, "sc_conv": sc_conv, "nsa_w_in": nsa_w_in, "nsa_w_out": nsa_w_out,
            "cmp_pos_k": cmp_pos_k, "cmp_w1_k": cmp_w1_k, "cmp_w2_k": cmp_w2_k,
            "cmp_pos_v": cmp_pos_v, "cmp_w1_v": cmp_w1_v, "cmp_w2_v": cmp_w2_v,
            "ffn_w_gu": ffn_w_gu, "ffn_conv": ffn_conv, "ffn_w_down": ffn_w_down}

def reference(x, norm_w, ab_w_in, ab_w_out, gdn_conv, gdn_a_log, gdn_dt_bias, gdn_norm, sc_conv,
              nsa_w_in, nsa_w_out, cmp_pos_k, cmp_w1_k, cmp_w2_k, cmp_pos_v, cmp_w1_v, cmp_w2_v,
              ffn_w_gu, ffn_conv, ffn_w_down):
    cos, sin = rope_tables(x.shape[1], NSA_HD)
    h = x
    for l in range(DEPTH):
        i = l // 2
        xn = rmsnorm(h, norm_w[l, 0])
        if l % 2 == 0:
            m = delta_shortconv_mixer(xn, ab_w_in[i], ab_w_out[i], gdn_conv[i], gdn_a_log[i],
                                      gdn_dt_bias[i], gdn_norm[i], sc_conv[i])
        else:
            m = nsa_mixer(xn, nsa_w_in[i], nsa_w_out[i], cmp_pos_k[i], cmp_w1_k[i], cmp_w2_k[i],
                          cmp_pos_v[i], cmp_w1_v[i], cmp_w2_v[i], cos, sin)
        h = h + rmsnorm(m, norm_w[l, 1])
        f = conv_ffn(rmsnorm(h, norm_w[l, 2]), ffn_w_gu[l], ffn_conv[l], ffn_w_down[l])
        h = h + rmsnorm(f, norm_w[l, 3])
    return h


_drawn_inputs = setup_inputs


def setup_inputs(seed=0):
    import zlib

    import numpy as np

    out = dict(_drawn_inputs(seed))
    spreads = {}
    factors = {'gdn_norm': 16.08, 'cmp_pos_k': 27.674, 'cmp_pos_v': 4.489}
    for name, (base, spread) in spreads.items():
        noise = np.random.default_rng([zlib.crc32(name.encode()), seed]).standard_normal(out[name].shape)
        drawn = base * np.exp(spread * noise) if base else spread * noise
        out[name] = __import__('jax').numpy.asarray(drawn.astype(out[name].dtype))
    for name, factor in factors.items():
        out[name] = (out[name] * factor).astype(out[name].dtype)
    return out
```

```python
from contextlib import ExitStack

import concourse.bass as bass
from concourse import mybir

F32 = mybir.dt.float32
F32R = mybir.dt.float32r
ACT = mybir.ActivationFunctionType
ALU = mybir.AluOpType
AX = mybir.AxisListType

P = 128
S = 256
D = 2048
KD = D // P
FF = 5632
KF = FF // P
DN_K = KF // 4
HEADS = 8
TT = S // P
LEVELS = 7
NG, NR = 4, 4
WINS = S // 16 - 1
CW = NG * WINS
EPS = 1e-6
NEG = -1e30
SCALE = float(P) ** -0.5

PHASES = ["ab", "qkv", "mix", "out0", "gu0", "dn0", "gate", "kv", "cmp", "q", "out1", "gu1", "dn1"]
N_UNITS = dict(ab=1, qkv=24, mix=32, out0=16, gu0=88, dn0=64, gate=1, kv=24, cmp=8, q=16, out1=16, gu1=88, dn1=64)
N_TILES = dict(N_UNITS, dn0=16, dn1=16, cmp=4)
U0, T0 = {}, {}
_u = _t = 0
for _p in PHASES:
    U0[_p], T0[_p] = _u, _t
    _u += N_UNITS[_p]
    _t += N_TILES[_p]
UNITS = _u

PARAM = {}
_c = 0
for _n, _w in [("norm", 8 * KD), ("gconv", 24 * 4), ("sconv", 8 * 3), ("fconv", 2 * KF * 3), ("gnorm", 1),
               ("alog", 1), ("dtb", 1), ("eps", 1), ("onehot", 2 * HEADS), ("ident", P), ("ones", P)]:
    PARAM[_n] = (_c, _w)
    _c += _w
N_PARAM = _c
L0C = {"triu": (0, P), "level": (P, LEVELS * P)}
N_L0C = P + LEVELS * P
L1C = {}
_c = 0
for _n, _w in [("cos", S), ("sin", S), ("causal", S), ("cmask", TT * WINS), ("cvalid", TT * WINS),
               ("posk", 32), ("posv", 32), ("w2k", 2 * P), ("w2v", 2 * P)]:
    L1C[_n] = (_c, _w)
    _c += _w
N_L1C = _c


class Unit:

    def __init__(self, phase, j, i=0, per=4):
        off = U0[phase] + j
        self.n = off + per * i
        self.raw = off % 4
        self.half = off % 2
        self.loads = 16 * (off // 4 + 1) + 16 * (per // 4) * i


class Tile:

    def __init__(self, phase, j, i=0, per=4, bank=None):
        off = T0[phase] + j
        self.n = off + per * i
        self.bank = off % 4 if bank is None else bank


class Steps:

    def __init__(self, sem):
        self.sem, self.base, self.k, self.i, self.per = sem, 0, 0, None, 0

    def enter(self, i, per, first=0):
        self.base += self.k - first * per
        self.k, self.i, self.per = 0, i, per

    def leave(self, end):
        assert self.k == self.per, (self.k, self.per)
        self.base += end * self.per
        self.k, self.i = 0, None

    def mark(self, ins):
        ins.then_inc(self.sem, 1)
        self.k += 1
        return self.base + self.k + (self.i * self.per if self.i is not None else 0)


def after(eng, sem, value):
    if not isinstance(value, int) or value > 0:
        eng.wait_ge(sem, value)


def build(nc, A, out):
    ctx = ExitStack()
    base0 = (nc.sbuf_base + 63) // 64 * 64

    def at(name, offset, shape, dt=F32):
        return nc.alloc_sbuf_tensor_at(name, shape, dt, offset=base0 + offset)

    KB = 1024
    with ctx:
        def sem(name):
            return ctx.enter_context(nc.semaphore(name))

        raw = [at(f"raw{i}", i * 8 * KB, [P, KD, P]) for i in range(4)]
        hi = [at(f"hi{i}", (32 + 8 * i) * KB, [P, KD, P], F32R) for i in range(2)]
        lo = [at(f"lo{i}", (48 + 8 * i) * KB, [P, KD, P], F32R) for i in range(2)]
        XO = 64 * KB
        xhl = at("xhl", XO, [P, KD, 2, S], F32R)
        mout = at("mout", XO, [P, KD, S])
        hold = at("hold", XO + 16 * KB, [P, KD, S])
        MO = 96 * KB
        mid = at("mid", MO, [P, KF, 2, S], F32R)
        yhl = at("yhl", MO, [P, KD, 2, S], F32R)
        hnew = at("hnew", MO + 72 * KB, [P, KD, S])
        sq4 = [at(f"sq4_{i}", MO + 40 * KB + 4 * KB * i, [P, 4, S]) for i in range(2)]
        xf4 = [at(f"xf4_{i}", MO + 48 * KB + 4 * KB * i, [P, 4, S]) for i in range(2)]
        WO = MO + 88 * KB

        qkv = at("qkv", MO + 32 * KB, [P, 3, 4, 2, S])
        G = MO + 56 * KB
        rs = at("rs", G, [P, 2, 2, S])
        X = at("X", G, [P, 4, P])
        PT = at("PT", G + 2 * KB, [P, 4, P])
        dt_ = at("dt_", G + 4 * KB, [P, 4, P])
        yb_ = at("yb_", G + 4 * KB, [P, 4, P])
        bc = at("bc", G + 6 * KB, [P, 2, 2, S])
        nt = [at(f"nt{i}", G + 6 * KB + 2 * KB * i, [P, 4, P]) for i in range(2)]
        nr = at("nr", G + 10 * KB, [P, 2, 2, S])
        vb = at("vb", G + 10 * KB, [P, 4, P])
        kdec = at("kdec", G + 12 * KB, [P, 2, P])
        kbg = at("kbg", G + 13 * KB, [P, 2, P])
        kb = at("kb", G + 14 * KB, [P, 2, S])
        vn0 = at("vn0", G + 14 * KB, [P, 2, P])
        vn1 = at("vn1", G + 15 * KB, [P, 2, P])
        qn = at("qn", G + 16 * KB, [P, 2, S])
        ot = at("ot", G + 18 * KB, [P, 2, S])
        vw = at("vw", G + 20 * KB, [P, 2, S])
        ez = at("ez", G + 20 * KB, [P, 2, S])
        osq = at("osq", G + 20 * KB, [P, 2, S])
        lt = at("lt", G + 22 * KB, [P, 4, P])
        orn = at("orn", G + 22 * KB, [P, 2, S])
        kn = at("kn", G + 24 * KB, [P, 2, S])
        wt = at("wt", G + 24 * KB, [P, 2, P])
        s1 = at("s1", G + 25 * KB, [P, 2, P])
        qg = at("qg", G + 26 * KB, [P, 2, P])
        eg = at("eg", G + 27 * KB, [P, 2, P])
        att = at("att", G + 28 * KB, [P, 4, P])
        zs = at("zs", G + 30 * KB, [P, 2, S])

        kt = at("kt", MO + 32 * KB, [P, 3, NG, S])
        vk = at("vk", MO + 44 * KB, [P, 3, NG, TT, P])
        l1c = at("l1c", MO + 56 * KB, [P, N_L1C])
        xc = [at(f"xc{k}", MO + 15 * KB * k, [P, 32, 2, CW], F32R) for k in range(2)]
        assert N_L1C * 4 <= 7 * KB
        B1 = MO + 63 * KB
        h1 = at("h1", B1, [P, 4, CW])
        kc_ = at("kc_", B1 + 1024, [P, NG, WINS])
        vc_ = at("vc_", B1 + 1280, [P, NG, P])
        sig = at("sig", B1 + 3328, [P, TT, 3, 16])
        gt = at("gt", B1 + 3712, [P, 16, 6])
        B2 = MO + 68 * KB
        vst = at("vst", B2, [P, NG, S])
        xct = at("xct", B2 + 4 * KB, [P, 32, NG, WINS])
        gts = at("gts", B2 + 12 * KB, [P, S])
        qs = at("qs", B2, [P, NR, S])
        sm1 = at("sm1", B2 + 4 * KB, [P, 2, S])
        sm0 = at("sm0", B2 + 6 * KB, [P, 2, P])
        smc = at("smc", B2 + 7 * KB, [P, TT, 16])
        soft = at("soft", B2 + 7 * KB + 128, [P, 32])
        pt = at("pt", B2 + 8 * KB, [P, 2, 3 * P])
        ptc = at("ptc", B2 + 11 * KB, [P, S])
        vs = at("vs", B2 + 12 * KB, [P, 2, TT, P])
        vcs = at("vcs", B2 + 14 * KB, [P, P])
        of = [at(f"of{k}", B2 + 15 * KB + KB * k, [P, S]) for k in range(2)]
        C1 = {n: l1c[:, c:c + w] for n, (c, w) in L1C.items()}

        o = WO
        def small(name, shape, dt=F32):
            nonlocal o
            n = 4
            for s_ in shape[1:]:
                n *= s_
            t = at(name, o, shape, dt)
            o += (n + 31) // 32 * 32
            return t

        prm = small("prm", [P, N_PARAM])
        half = [small(f"half{i}", [P, S]) for i in range(4)]
        cbuf = [small(f"cbuf{i}", [P, 3 + S]) for i in range(2)]
        cv = [small(f"cv{i}", [P, S]) for i in range(2)]
        up = [small(f"up{i}", [P, S]) for i in range(2)]
        ssq = small("ssq", [P, S])
        sqd = [small(f"sqd{i}", [P, S]) for i in range(2)]
        rstd = small("rstd", [P, S])
        tiny = small("tiny", [P, 64])
        wend = o
        sil = [small(f"sil{i}", [P, S]) for i in range(2)]
        mf = [small(f"mf{i}", [P, S]) for i in range(2)]
        o = wend
        l0c = small("l0c", [P, N_L0C])
        R = small("R", [P, S])
        abf = small("abf", [P, S])
        at4 = [at(f"at{i}", G + i * KB, [P, S]) for i in range(8)]
        ones256 = at("ones256", G + 8 * KB, [P, S])

        def prm_(name, *dims):
            c, w = PARAM[name]
            return prm[:, c:c + w]

        normw = prm_("norm").rearrange("p (l c) -> p l c", l=8)
        gconv = prm_("gconv").rearrange("p (c k) -> p c k", k=4)
        sconv = prm_("sconv").rearrange("p (i a k) -> p i a k", a=2, k=3)
        fconv = prm_("fconv").rearrange("p (l c k) -> p l c k", l=2, k=3)
        onehot = prm_("onehot").rearrange("p (i a k) -> p i a k", a=2, k=2)
        gnorm, alog, dtb, eps = prm_("gnorm"), prm_("alog"), prm_("dtb"), prm_("eps")
        ident, ones = prm_("ident"), prm_("ones")
        triu = l0c[:, 0:P]
        level = l0c[:, P:].rearrange("p (l j) -> p l j", l=LEVELS)

        lin = [ctx.enter_context(nc.psum_tensor(f"lin{i}", [P, 512], F32)) for i in range(4)]
        aux = [ctx.enter_context(nc.psum_tensor(f"aux{i}", [P, 512], F32)) for i in range(4)]

        s_prm = sem("s_prm")
        s_l0c = sem("s_l0c")
        s_w = [sem(f"s_w{i}") for i in range(4)]
        s_hi = sem("s_hi")
        s_lo = sem("s_lo")
        s_wh = sem("s_wh")
        s_unit = sem("s_unit")
        s_half = sem("s_half")
        s_free = sem("s_free")
        v_ = Steps(sem("s_dve"))
        a_ = Steps(sem("s_act"))
        s_hload = sem("s_hload")
        s_out = sem("s_out")
        s_hstore = sem("s_hstore")
        s_hn = sem("s_hn")
        s_sq4 = sem("s_sq4")
        s_nps = sem("s_nps")
        s_root = sem("s_root")
        s_xf = sem("s_xf")
        s_xhi = sem("s_xhi")
        s_xlo = sem("s_xlo")
        s_msq = sem("s_msq")
        s_ssq = sem("s_ssq")
        s_conv = sem("s_conv")
        s_silu = sem("s_silu")
        s_mid = sem("s_mid")
        s_midhi = sem("s_midhi")
        s_midlo = sem("s_midlo")
        s_yf = sem("s_yf")
        s_yhi = sem("s_yhi")
        s_ylo = sem("s_ylo")
        a_names = "gt gtp sg ge gn vt vk vk_ xck xch xcl ge2 h1 k2 kc swap rope sc sm mx ex p tp pta ptd pv oc cp xcw".split()
        ns = {x: sem("n_" + x) for x in a_names}
        s_l1c = sem("s_l1c")
        s_post = sem("s_post")
        g_names = ("ab rt rs bc bcc sq ss nr vw kn kb dt de eg qg dm kd tp vb kk lt at xi nt y yb z xp uw vn0 s1 s1c "
                   "v1 v1c o oc on orn ez zadd zs hb").split()
        g = {n: sem("g_" + n) for n in g_names}

        block = ctx.enter_context(nc.Block())

        @block.sync
        def _(sp):
            sp.dma_start(hnew[:, :, :], A["x"]).then_inc(s_hload, 16)
            sp.dma_start(prm[:, :], A["params"]).then_inc(s_prm, 16)

            def load(u, src, nk=KD):
                after(sp, s_lo, u.n - 3)
                sp.dma_start(raw[u.raw][:, 0:nk, :], src).then_inc(s_w[u.raw], 16)

            w = A["w_in0"]
            for j in range(4):
                load(Unit("ab", j), w[j])
            sp.dma_start(l0c[:, :], A["l0c"]).then_inc(s_l0c, 16)
            load(Unit("ab", 4), w[4])
            with sp.Fori(0, 13) as i:
                for j in range(4):
                    load(Unit("ab", 5 + j, i), w[i * 4 + 5 + j])

            def loads(phase, w, nk=KD):
                with sp.Fori(1, N_UNITS[phase] // 4) as i:
                    for j in range(4):
                        load(Unit(phase, j, i), w[i * 4 + j], nk)

            def first(phase, w, nk=KD):
                for j in range(4):
                    load(Unit(phase, j), w[j], nk)

            def residual(j, phase):
                sp.wait_ge(s_unit, U0[phase])
                if j > 1:
                    sp.wait_ge(s_hstore, 16 * (j - 1))
                sp.dma_start(hold[:, :, :], A["x"] if j == 1 else A["residual"]).then_inc(s_hload, 16)

            def store(j):
                sp.wait_ge(s_hn, 4 * j)
                sp.wait_ge(s_hload, 16 * (j + 1))
                sp.dma_start(A["residual"], hnew[:, :, :]).then_inc(s_hstore, 16)

            first("out0", A["w_out0"])
            loads("out0", A["w_out0"])
            residual(1, "out0")
            first("gu0", A["w_gu0"])
            store(1)
            loads("gu0", A["w_gu0"])
            first("dn0", A["w_dn0"], DN_K)
            loads("dn0", A["w_dn0"], DN_K)
            residual(2, "dn0")
            w = A["w_in1"]
            for j in range(4):
                load(Unit("gate", j), w[j])
            sp.wait_ge(s_unit, U0["gate"])
            sp.dma_start(l1c[:, :], A["l1c"]).then_inc(s_l1c, 16)
            store(2)
            load(Unit("gate", 4), w[4])
            with sp.Fori(0, 5) as i:
                for j in range(4):
                    load(Unit("gate", 5 + j, i), w[i * 4 + 5 + j])
            for j in range(8):
                load(Unit("cmp", j), A["w_cmp"][j])
            for j in range(16):
                load(Unit("q", j), w[25 + j])
            first("out1", A["w_out1"])
            loads("out1", A["w_out1"])
            residual(3, "out1")
            first("gu1", A["w_gu1"])
            store(3)
            loads("gu1", A["w_gu1"])
            first("dn1", A["w_dn1"], DN_K)
            loads("dn1", A["w_dn1"], DN_K)
            residual(4, "dn1")
            for q in range(4):
                sp.wait_ge(s_hn, 16 - 3 + q)
                sp.dma_start(out[:, 4 * q:4 * q + 4, :], hnew[:, 4 * q:4 * q + 4, :]).then_inc(s_out, 16)
            sp.wait_ge(s_out, 64)

        @block.tensor
        def _(pe):
            def passes(u, bank, rhs2, rhs1, nk, start, stop, width=S, ready=None, slot=None):
                pe.wait_ge(s_hi, u.n + 1)
                for k in range(nk):
                    if ready is not None:
                        ready(k)
                    m = pe.matmul(bank[:, 0:2 * width], hi[u.half][:, k, :], rhs2(k),
                                  start=start and k == 0, stop=False, skip_group_check=True)
                    if k == nk - 1:
                        m.then_inc(s_wh, 1)
                    if slot is not None:
                        slot(k)
                pe.wait_ge(s_lo, u.n + 1)
                for k in range(nk):
                    m = pe.matmul(bank[:, 0:width], lo[u.half][:, k, :], rhs1(k),
                                  start=False, stop=stop and k == nk - 1, skip_group_check=True)
                m.then_inc(s_unit, 1)
                if slot is not None:
                    slot(nk)

            def x_unit(u, t, norm=None, slot=None):
                after(pe, s_free, t.n - 3)
                def ready(k):
                    if norm is not None and k % 4 == 0:
                        pe.wait_ge(s_xlo, 4 * norm + k // 4 + 1)
                passes(u, lin[t.bank], lambda k: xhl[:, k, :, :], lambda k: xhl[:, k, 0, :], KD, True, True,
                       ready=ready, slot=slot)

            def sum_squares(norm):
                for c in range(KD):
                    if c % 4 == 0:
                        pe.wait_ge(s_sq4, 4 * norm + c // 4 + 1)
                    m = pe.matmul(aux[0][:, 0:S], ones, sq4[(c // 4) % 2][:, c % 4, :],
                                  start=c == 0, stop=c == KD - 1)
                    if c % 4 == 3:
                        m.then_inc(s_nps, 1)

            pe.wait_ge(s_prm, 16)
            sum_squares(0)
            x_unit(Unit("ab", 0), Tile("ab", 0), norm=0)
            for j in range(4):
                x_unit(Unit("qkv", j), Tile("qkv", j))
            with pe.Fori(1, 6) as i:
                for j in range(4):
                    x_unit(Unit("qkv", j, i), Tile("qkv", j, i))
            pe.wait_ge(g["ab"], 1)
            for t in range(TT):
                m = pe.transpose(aux[t][:, 0:P], R[:, t * P:(t + 1) * P], ident)
            m.then_inc(g["rt"], 1)

            def mix(i):
                n = i + 1

                def spread():
                    pe.wait_ge(g["rs"], n)
                    for k in range(2):
                        pe.matmul(aux[k][:, :], ones, rs[:, k, :, :], start=True, stop=True).then_inc(g["bc"], 1)
                    pe.wait_ge(g["sq"], n)
                    for k in range(2):
                        pe.matmul(aux[2 + k][:, :], ones, nr[:, k, :, :], start=True, stop=True).then_inc(g["ss"], 1)

                def turn():
                    pe.wait_ge(g["kn"], n)
                    pe.wait_ge(g["vw"], n)
                    for q in range(4):
                        pe.transpose(aux[2][:, q * P:(q + 1) * P], kn[:, q // 2, (q % 2) * P:(q % 2 + 1) * P], ident)
                    for q in range(4):
                        m = pe.transpose(aux[3][:, q * P:(q + 1) * P], vw[:, q // 2, (q % 2) * P:(q % 2 + 1) * P], ident)
                    m.then_inc(g["tp"], 1)

                def grams():
                    pe.wait_ge(g["kb"], n)
                    for bank, rhs in ((aux[0], kb), (aux[1], qn)):
                        for q in range(4):
                            sl = slice((q % 2) * P, (q % 2 + 1) * P)
                            m = pe.matmul(bank[:, q * P:(q + 1) * P], kn[:, q // 2, sl], rhs[:, q // 2, sl],
                                          start=True, stop=True, skip_group_check=True)
                    m.then_inc(g["kk"], 1)

                def inv_a(l):
                    pe.wait_ge(g["nt"], i * LEVELS + l + 1)
                    if l == 0:
                        pe.wait_ge(g["xi"], n)
                        pe.wait_ge(g["vb"], n)
                    else:
                        pe.wait_ge(g["xp"], i * LEVELS + l)
                    for q in range(4):
                        m = pe.matmul(aux[2][:, q * P:(q + 1) * P], nt[l % 2][:, q, :], X[:, q, :],
                                      start=True, stop=True, skip_group_check=True)
                    m.then_inc(g["y"], 1)

                def inv_b(l):
                    pe.wait_ge(g["yb"], i * LEVELS + l + 1)
                    s_ = 1 << l
                    for q in range(4):
                        yq = yb_[:, q, :].rearrange("p (b h s) -> p b h s", h=2, s=s_)
                        pq = PT[:, q, :].rearrange("p (b h s) -> p b h s", h=2, s=s_)
                        pe.matmul(aux[3][:, q * 64:(q + 1) * 64], PT[:, q, :], yq[:, :, 0, :],
                                  start=True, stop=True, skip_group_check=True)
                        m = pe.matmul(aux[3][:, 256 + q * 64:256 + (q + 1) * 64], yb_[:, q, :], pq[:, :, 1, :],
                                      start=True, stop=True, skip_group_check=True)
                    m.then_inc(g["z"], 1)

                def first_v():
                    pe.wait_ge(g["xp"], (i + 1) * LEVELS)
                    pe.wait_ge(g["at"], n)
                    for h in range(2):
                        pe.matmul(aux[0][:, h * P:(h + 1) * P], PT[:, 2 * h, :], vb[:, 2 * h, :],
                                  start=True, stop=True, skip_group_check=True)
                        m = pe.matmul(aux[0][:, 256 + h * P:256 + (h + 1) * P], kbg[:, h, :], PT[:, 2 * h + 1, :],
                                      start=True, stop=True, skip_group_check=True)
                    m.then_inc(g["uw"], 1)

                def state():
                    pe.wait_ge(g["vn0"], n)
                    for h in range(2):
                        m = pe.matmul(aux[1][:, h * P:(h + 1) * P], kdec[:, h, :], vn0[:, h, :],
                                      start=True, stop=True, skip_group_check=True)
                    m.then_inc(g["s1"], 1)

                def second_v():
                    pe.wait_ge(g["s1c"], n)
                    for h in range(2):
                        pe.matmul(aux[2][:, h * P:(h + 1) * P], PT[:, 2 * h + 1, :], vb[:, 2 * h + 1, :],
                                  start=True, stop=False, skip_group_check=True)
                        m = pe.matmul(aux[2][:, h * P:(h + 1) * P], wt[:, h, :], s1[:, h, :],
                                      start=False, stop=True, skip_group_check=True)
                    m.then_inc(g["v1"], 1)

                def outputs():
                    pe.wait_ge(g["v1c"], n)
                    pe.wait_ge(g["qg"], n)
                    for h in range(2):
                        pe.matmul(aux[3][:, h * S:h * S + P], vn0[:, h, :], att[:, 2 * h, :],
                                  start=True, stop=True, skip_group_check=True)
                        pe.matmul(aux[3][:, h * S + P:(h + 1) * S], vn1[:, h, :], att[:, 2 * h + 1, :],
                                  start=True, stop=False, skip_group_check=True)
                        m = pe.matmul(aux[3][:, h * S + P:(h + 1) * S], s1[:, h, :], qg[:, h, :],
                                      start=False, stop=True, skip_group_check=True)
                    m.then_inc(g["o"], 1)

                def out_norm():
                    pe.wait_ge(g["oc"], n)
                    pe.matmul(aux[0][:, :], ones, osq[:, :, :], start=True, stop=True).then_inc(g["on"], 1)

                plan = {0: [spread], 2: [turn], 4: [grams], 19: [first_v], 20: [state], 21: [second_v],
                        22: [outputs], 23: [out_norm]}
                for l in range(LEVELS):
                    plan[5 + 2 * l] = [lambda l=l: inv_a(l)]
                    plan[6 + 2 * l] = [lambda l=l: inv_b(l)]
                for j in range(8):
                    x_unit(Unit("mix", j, i, 8), Tile("mix", j, i, 8),
                           slot=lambda k, j=j: [f() for f in plan.get(3 * j + {7: 0, 15: 1, 16: 2}.get(k, 99), [])])

            with pe.Fori(0, 4) as i:
                mix(i)

            def out_phase(phase):
                def tiles(i):
                    for j in range(4):
                        t = Tile(phase, j, i)
                        after(pe, s_free, t.n - 3)
                        passes(Unit(phase, j, i), lin[t.bank], lambda k: yhl[:, k, :, :],
                               lambda k: yhl[:, k, 0, :], KD, True, True)
                pe.wait_ge(s_ylo, 12 if phase == "out0" else 28)
                with pe.Fori(0, 4) as i:
                    tiles(i)

            def up_phase(phase, norm):
                with pe.Fori(0, 22) as i:
                    for j in range(4):
                        x_unit(Unit(phase, j, i), Tile(phase, j, i), norm=norm if j == 0 else None)

            def down_phase(phase, layer):
                pe.wait_ge(s_midlo, KF * (layer + 1))
                with pe.Fori(0, 8) as i:
                    for a in range(2):
                        t = Tile(phase, a, i, 2)
                        pe.wait_ge(s_free, t.n - 1)
                        for q in range(4):
                            passes(Unit(phase, 4 * a + q, i, 8), lin[t.bank],
                                   lambda k: mid[:, DN_K * q + k, :, :], lambda k: mid[:, DN_K * q + k, 0, :],
                                   DN_K, q == 0, q == 3)

            def junction(j, norm=True):
                pe.wait_ge(s_ssq, 17 * j)
                pe.matmul(aux[1][:, 0:S], ones, ssq[:, :], start=True, stop=True).then_inc(s_post, 1)
                if norm:
                    sum_squares(j)

            out_phase("out0")
            junction(1)
            up_phase("gu0", 1)
            down_phase("dn0", 0)
            junction(2)

            x_unit(Unit("gate", 0), Tile("gate", 0), norm=2)

            def kv(i):
                for j in range(8):
                    x_unit(Unit("kv", j, i, 8), Tile("kv", j, i, 8))
                    if j == 0 and isinstance(i, int):
                        pe.wait_ge(s_free, T0["gate"] + 1)
                        for t in range(TT):
                            m = pe.transpose(aux[1][:, t * P:(t + 1) * P], gts[:, t * P:(t + 1) * P], ident)
                        m.then_inc(ns["gtp"], 1)
                    if j >= 5:
                        turn_v(i, j - 5)
                turn_v(i, 3)

            def turn_v(i, g_):
                pe.wait_ge(s_free, Tile("kv", 4 + g_, i, 8).n + 1)
                after(pe, ns["vk"], 4 * i + g_ - 1)
                for t in range(TT):
                    m = pe.transpose(aux[2 + g_ % 2][:, t * P:(t + 1) * P], vst[:, g_, t * P:(t + 1) * P], ident)
                m.then_inc(ns["vk_"], 1)

            kv(0)
            with pe.Fori(1, 3) as i:
                kv(i)
            for kind in range(2):
                pe.wait_ge(ns["xcl"], kind + 1)
                for ht in range(2):
                    t = Tile("cmp", 2 * kind + ht)
                    pe.wait_ge(s_free, t.n - 3)
                    for q in range(2):
                        passes(Unit("cmp", 4 * kind + 2 * ht + q), lin[t.bank],
                               lambda k: xc[kind][:, 16 * q + k, :, :], lambda k: xc[kind][:, 16 * q + k, 0, :],
                               KD, q == 0, q == 1, width=CW)
            for j in range(4):
                x_unit(Unit("q", j), Tile("q", j))
                if j == 0:
                    pe.wait_ge(ns["h1"], 2)
                    for ht in range(2):
                        pe.matmul(aux[0][:, 0:CW], C1["w2k"].rearrange("p (a d) -> p a d", a=2)[:, ht, :],
                                  h1[:, ht, :], start=ht == 0, stop=ht == 1)
                    for g_ in range(NG):
                        for ht in range(2):
                            m = pe.matmul(aux[1][0:WINS, g_ * P:(g_ + 1) * P], h1[:, 2 + ht, g_ * WINS:(g_ + 1) * WINS],
                                          C1["w2v"].rearrange("p (a d) -> p a d", a=2)[:, ht, :],
                                          start=ht == 0, stop=ht == 1, skip_group_check=True)
                    m.then_inc(ns["k2"], 1)

            def scores(g_, r):
                h = 4 * g_ + r
                pe.wait_ge(ns["rope"], 12 + h + 1)
                after(pe, ns["oc"], h)
                after(pe, ns["ptd"], h)
                pe.matmul(aux[3][:, 0:WINS], qs[:, r, 0:P], kc_[:, g_, :], start=True, stop=True,
                          skip_group_check=True)
                pe.matmul(aux[3][:, 16:16 + WINS], qs[:, r, P:S], kc_[:, g_, :], start=True, stop=True,
                          skip_group_check=True)
                pe.matmul(aux[0][:, 0:S], qs[:, r, 0:P], kt[:, 1:3, g_, 0:P], start=True, stop=True)
                pe.matmul(aux[1][:, :], qs[:, r, P:S], kt[:, 1:3, g_, :], start=True, stop=True).then_inc(ns["sc"], 1)

            def turn_p(g_, r):
                h = 4 * g_ + r
                pe.wait_ge(ns["p"], h + 1)
                after(pe, ns["pta"], h)
                for b in range(2):
                    pe.transpose(aux[2][:, b * P:(b + 1) * P], sm0[:, b, :], ident)
                for t in range(TT):
                    pe.transpose(aux[2][0:WINS, (2 + t) * P:(3 + t) * P], smc[:, t, 0:WINS], ident)
                for b in range(2):
                    for k in range(2):
                        m = pe.transpose(aux[3][:, (2 * b + k) * P:(2 * b + k + 1) * P], sm1[:, b, k * P:(k + 1) * P],
                                         ident)
                m.then_inc(ns["tp"], 1)

            def values(g_, r):
                h = 4 * g_ + r
                pe.wait_ge(ns["pta"], h + 1)
                pe.wait_ge(ns["ptd"], h + 1)
                pe.wait_ge(ns["cp"], g_ + 1)
                o_ = aux[0]
                for b in range(2):
                    pe.matmul(o_[:, 0:S], vs[:, b, 0, :], pt[:, b, 0:S], start=b == 0, stop=False, skip_group_check=True)
                    pe.matmul(o_[:, P:S], vs[:, b, 1, :], pt[:, b, S:S + P], start=False, stop=False,
                              skip_group_check=True)
                pe.matmul(o_[:, 0:S], vcs[0:WINS, :], ptc[0:WINS, :], start=False, stop=True,
                          skip_group_check=True).then_inc(ns["pv"], 1)

            pe.wait_ge(ns["kc"], 1)
            with pe.Fori(1, 4) as i:
                g_ = i - 1
                for j in range(4):
                    def slot(k, j=j):
                        if j > 0 and k == 3:
                            turn_p(g_, j - 1)
                        if j > 0 and k == 8:
                            values(g_, j - 1)
                        if k == 12:
                            scores(g_, j)
                    x_unit(Unit("q", j, i), Tile("q", j, i), slot=slot)
                turn_p(g_, 3)
                values(g_, 3)
            for r in range(4):
                scores(3, r)
                turn_p(3, r)
                values(3, r)
            out_phase("out1")
            junction(3)
            up_phase("gu1", 3)
            down_phase("dn1", 1)
            junction(4, norm=False)

        @block.scalar
        def _(act):
            def split(u, nk=KD, lo_done=True):
                act.wait_ge(s_w[u.raw], u.loads)
                after(act, s_wh, u.n - 1)
                after(act, s_lo, u.n - 1)
                act.activation(hi[u.half][:, 0:nk, :], raw[u.raw][:, 0:nk, :], ACT.Copy).then_inc(s_hi, 1)

            def take(t, u_done, width=S):
                act.wait_ge(s_unit, u_done + 1)
                act.activation(half[t.bank][:, 0:width], lin[t.bank][:, width:2 * width], ACT.Copy).then_inc(s_half, 1)

            def norm_squares(norm, n_root):
                for q in range(4):
                    if norm == 0:
                        if q == 0:
                            act.wait_ge(s_hload, 16)
                    else:
                        act.wait_ge(s_hn, 4 * (norm - 1) + q + 1)
                    if q >= 2:
                        act.wait_ge(s_nps, 4 * norm + q - 1)
                    act.activation(sq4[q % 2][:, :, :], hnew[:, 4 * q:4 * q + 4, :], ACT.Square).then_inc(s_sq4, 1)
                act.wait_ge(s_nps, 4 * norm + 4)
                act.activation(rstd[:, :], aux[0][:, 0:S], ACT.Sqrt, bias=eps, scale=1.0 / D).then_inc(s_root, 1)

            def norm_high(norm):
                for q in range(4):
                    act.wait_ge(s_xf, 4 * norm + q + 1)
                    act.activation(xhl[:, 4 * q:4 * q + 4, 0, :], xf4[q % 2][:, :, :], ACT.Copy).then_inc(s_xhi, 1)

            act.wait_ge(s_prm, 16)
            norm_squares(0, 0)
            split(Unit("ab", 0))
            split(Unit("ab", 1))
            norm_high(0)
            t = Tile("ab", 0)
            take(t, 0)
            split(Unit("ab", 2))

            def qkv_tiles(i):
                for j in range(4):
                    u, t = Unit("qkv", j, i), Tile("qkv", j, i)
                    take(t, u.n)
                    split(Unit("qkv", j + 2, i))
                    c = i * 4 + j
                    act.wait_ge(s_conv, c + 1)
                    act.activation(qkv[:, :, :, :, :].rearrange("p a b c t -> p (a b c) t")[:, c, :],
                                   cv[j % 2][:, :], ACT.Silu).then_inc(s_silu, 1)

            qkv_tiles(0)
            with act.Fori(1, 6) as i:
                qkv_tiles(i)

            act.wait_ge(g["hb"], 1)
            a0, a1, a2, a3, a4 = [x[0:8, :] for x in at4[0:5]]
            r = a_.mark(act.activation(a1, a0, ACT.Abs))
            act.wait_ge(a_.sem, r)
            r = a_.mark(act.activation(a1, a1, ACT.Exp, scale=-1.0))
            r = a_.mark(act.activation(R[32:40, :], abf[32:40, :], ACT.Exp, scale=-1.0))
            r = a_.mark(act.activation(tiny[0:8, 0:1], alog[0:8, :], ACT.Exp))
            act.wait_ge(a_.sem, r)
            act.activation(a2, a1, ACT.Ln, bias=1.0).then_inc(g["eg"], 1)
            act.wait_ge(g["kd"], 1)
            act.activation(tiny[:, 40:48], tiny[:, 24:32], ACT.Exp).then_inc(g["kd"], 1)

            def mix(i):
                n = i + 1
                act.activation(nr[:, 0, :, :], qkv[:, 0, i, :, :], ACT.Square)
                act.activation(nr[:, 1, :, :], qkv[:, 1, i, :, :], ACT.Square).then_inc(g["sq"], 1)
                act.activation(vw[:, :, :], qkv[:, 2, i, :, :], ACT.Copy).then_inc(g["vw"], 1)

                def spread():
                    act.wait_ge(g["bc"], 2 * n)
                    act.activation(bc[:, 0, :, :], aux[0][:, :], ACT.Copy)
                    act.activation(bc[:, 1, :, :], aux[1][:, :], ACT.Copy).then_inc(g["bcc"], 1)
                    act.wait_ge(g["ss"], 2 * n)
                    for k in range(2):
                        act.activation(nr[:, k, :, :], aux[2 + k][:, :], ACT.Sqrt, bias=eps).then_inc(g["nr"], 1)

                def exps():
                    act.wait_ge(g["dt"], n)
                    act.activation(dt_[:, :, :], dt_[:, :, :], ACT.Exp).then_inc(g["de"], 1)
                    act.activation(eg[:, :, :], bc[:, 0, :, P:S], ACT.Exp)
                    act.activation(tiny[:, 50:52], tiny[:, 48:50], ACT.Exp).then_inc(g["eg"], 1)

                def zexp():
                    act.wait_ge(s_free, Tile("mix", 1, i, 8).n + 1)
                    act.activation(ez[:, :, :], zs[:, :, :], ACT.Exp, scale=-1.0).then_inc(g["ez"], 1)

                def yev(l):
                    if l == 0:
                        act.wait_ge(g["at"], n)
                    act.wait_ge(g["y"], i * LEVELS + l + 1)
                    act.activation(yb_[:, :, :], aux[2][:, :], ACT.Copy).then_inc(g["yb"], 1)

                def v0():
                    act.wait_ge(g["uw"], n)
                    act.activation(vn0[:, :, :], aux[0][:, 0:256], ACT.Copy)
                    act.activation(wt[:, :, :], aux[0][:, 256:512], ACT.Copy, scale=-1.0).then_inc(g["vn0"], 1)

                def s1c():
                    act.wait_ge(g["s1"], n)
                    act.activation(s1[:, :, :], aux[1][:, 0:256], ACT.Copy).then_inc(g["s1c"], 1)

                def v1():
                    act.wait_ge(g["v1"], n)
                    act.activation(vn1[:, :, :], aux[2][:, 0:256], ACT.Copy).then_inc(g["v1c"], 1)

                def oev():
                    act.wait_ge(g["o"], n)
                    act.activation(ot[:, :, :], aux[3][:, :], ACT.Copy)
                    act.activation(osq[:, :, :], aux[3][:, :], ACT.Square).then_inc(g["oc"], 1)

                def oroot():
                    act.wait_ge(g["on"], n)
                    act.activation(orn[:, :, :], aux[0][:, :], ACT.Sqrt, bias=eps, scale=1.0 / P).then_inc(g["orn"], 1)

                def high(a):
                    act.wait_ge(s_yf, 3 * i + a + 1)
                    act.activation(y4[:, i + 4, a, 0, :], cv[a][:, :], ACT.Copy).then_inc(s_yhi, 1)

                plan = {0: [spread], 3: [exps], 9: [zexp], 19: [v0], 20: [s1c], 21: [v1], 22: [oev], 23: [oroot],
                        16: [lambda: high(0)]}
                for l in range(LEVELS):
                    plan.setdefault(5 + 2 * l, []).append(lambda l=l: yev(l))
                for j in range(8):
                    for s_ in range(3):
                        for f in plan.get(3 * j + s_, []):
                            f()
                    u, t = Unit("mix", j, i, 8), Tile("mix", j, i, 8)
                    take(t, u.n)
                    split(Unit("mix", j + 2, i, 8))
                high(1)
                act.wait_ge(s_yf, 3 * i + 3)
                act.activation(y4[:, i, :, 0, :], ot[:, :, :], ACT.Copy).then_inc(s_yhi, 1)

            y4 = yhl[:, :, :, :].rearrange("p (i a) l t -> p i a l t", a=2)
            n_last = 4
            with act.Fori(0, n_last) as i:
                mix(i)

            def look(phase, j, i=0, per=4):
                if isinstance(i, int):
                    off = U0[phase] + j + per * i + 2
                    if off >= UNITS:
                        return
                    nk = DN_K if any(U0[x] <= off < U0[x] + N_UNITS[x] for x in ("dn0", "dn1")) else KD
                else:
                    nk = DN_K if phase[:2] == "dn" else KD
                split(Unit(phase, j + 2, i, per), nk)

            def square(m, j, b):
                act.wait_ge(s_ssq, 17 * (j - 1) + 1 + m)
                act.activation(sqd[b][:, :], mout[:, m, :], ACT.Square).then_inc(s_msq, 1)

            def out_phase(phase, jn):
                with act.Fori(0, 4) as i:
                    for j in range(4):
                        u, t = Unit(phase, j, i), Tile(phase, j, i)
                        take(t, u.n)
                        look(phase, j, i)
                        act.wait_ge(s_free, t.n + 1)
                        square(4 * i + j, jn, j % 2)

            def up_phase(phase, layer):
                def pairs(i):
                    for a in range(2):
                        c = 2 * i + a
                        take(Tile(phase, 2 * a, i), Unit(phase, 2 * a, i).n)
                        look(phase, 2 * a, i)
                        take(Tile(phase, 2 * a + 1, i), Unit(phase, 2 * a + 1, i).n)
                        act.wait_ge(s_conv, 24 + KF * layer + c + 1)
                        after(act, s_mid, KF * layer + c - 1)
                        act.activation(sil[a][:, :], cv[a][:, :], ACT.Silu).then_inc(s_silu, 1)
                        look(phase, 2 * a + 1, i)
                        act.wait_ge(s_mid, KF * layer + c + 1)
                        act.activation(mid[:, c, 0, :], mf[a][:, :], ACT.Copy).then_inc(s_midhi, 1)
                act.wait_ge(s_hstore, 16 * (2 * layer + 1))
                pairs(0)
                with act.Fori(1, 21) as i:
                    pairs(i)
                pairs(21)

            def down_phase(phase, jn):
                def tiles(i):
                    for a in range(2):
                        for q in range(4):
                            j = 4 * a + q
                            u, t = Unit(phase, j, i, 8), Tile(phase, a, i, 2)
                            if q == 3:
                                take(t, u.n)
                            look(phase, j, i, 8)
                        act.wait_ge(s_free, t.n + 1)
                        square(2 * i + a, jn, a)
                with act.Fori(0, 7) as i:
                    tiles(i)
                tiles(7)

            def junction(j, norm=True):
                act.wait_ge(s_post, j)
                act.activation(rstd[:, :], aux[1][:, 0:S], ACT.Sqrt, bias=eps, scale=1.0 / D).then_inc(s_root, 1)
                if norm:
                    norm_squares(j, 0)
                    norm_high(j)

            out_phase("out0", 1)
            junction(1)
            up_phase("gu0", 0)
            down_phase("dn0", 2)
            junction(2)

            take(Tile("gate", 0), U0["gate"])
            look("gate", 0)

            def swap(j):
                act.activation(up[j][0:64, :], cv[j][64:128, :], ACT.Copy)
                act.activation(up[j][64:128, :], cv[j][0:64, :], ACT.Copy).then_inc(ns["swap"], 1)

            def kv(i):
                for j in range(8):
                    u, t = Unit("kv", j, i, 8), Tile("kv", j, i, 8)
                    take(t, u.n)
                    if j < 4:
                        act.wait_ge(s_free, t.n + 1)
                        after(act, ns["rope"], 4 * i + j - 1)
                        swap(j % 2)
                    look("kv", j, i, 8)
                    if j >= 5:
                        out_v(i, j - 5)
                    if j == 0 and isinstance(i, int):
                        act.wait_ge(ns["gtp"], 1)
                        act.activation(sig[:, :, :, :].rearrange("p t b h -> p t (b h)"),
                                       aux[1][:, 0:S].rearrange("p (t c) -> p t c", t=TT)[:, :, 0:48],
                                       ACT.Exp, scale=-1.0).then_inc(ns["sg"], 1)
                out_v(i, 3)

            def out_v(i, g_):
                act.wait_ge(ns["vk_"], 4 * i + g_ + 1)
                act.activation(vk[:, i, g_, :, :], aux[2 + g_ % 2][:, 0:S], ACT.Copy).then_inc(ns["vk"], 1)

            kv(0)
            for kind in range(2):
                act.wait_ge(ns["xcw"], kind + 1)
                act.activation(xc[kind][:, :, 0, :], xct[:, :, :, :].rearrange("p l g c -> p l (g c)"),
                               ACT.Copy).then_inc(ns["xch"], 1)
            with act.Fori(1, 3) as i:
                kv(i)
            for kind in range(2):
                for ht in range(2):
                    for q in range(2):
                        j = 4 * kind + 2 * ht + q
                        if q == 1:
                            take(Tile("cmp", 2 * kind + ht), U0["cmp"] + j, CW)
                        look("cmp", j)
                act.wait_ge(s_free, T0["cmp"] + 2 * kind + 2)
                act.activation(h1[:, 2 * kind:2 * kind + 2, :], h1[:, 2 * kind:2 * kind + 2, :],
                               ACT.Gelu_apprx_tanh).then_inc(ns["h1"], 1)

            def query(j, i):
                t = Tile("q", j, i)
                take(t, Unit("q", j, i).n)
                act.wait_ge(s_free, t.n + 1)
                act.wait_ge(ns["rope"], 12 + 4 * i + j - 1)
                swap(j % 2)

            def exps(g_, r):
                h = 4 * g_ + r
                act.wait_ge(ns["mx"], h + 1)
                for b in range(2):
                    act.activation(sm0[:, b, :], sm0[:, b, :], ACT.Exp, bias=soft[:, 8 + b:9 + b], scale=SCALE,
                                   accum_out=soft[:, 16 + b:17 + b])
                    act.activation(sm1[:, b, :], sm1[:, b, :], ACT.Exp, bias=soft[:, 10 + b:11 + b], scale=SCALE,
                                   accum_out=soft[:, 18 + b:19 + b])
                    m = act.activation(smc[:, b, 0:WINS], smc[:, b, 0:WINS], ACT.Exp, bias=soft[:, 12 + b:13 + b],
                                       scale=SCALE, accum_out=soft[:, 20 + b:21 + b])
                m.then_inc(ns["ex"], 1)

            def take_p(g_, r):
                h = 4 * g_ + r
                act.wait_ge(ns["tp"], h + 1)
                act.activation(pt[:, :, 0:P], aux[2][:, 0:S].rearrange("p (b t) -> p b t", b=2), ACT.Copy)
                act.activation(ptc[0:WINS, :], aux[2][0:WINS, S:2 * S], ACT.Copy).then_inc(ns["pta"], 1)

            def take_o(g_, r):
                h = 4 * g_ + r
                act.wait_ge(ns["pv"], h + 1)
                after(act, s_ylo, 12 + h - 1)
                act.activation(of[r % 2][:, :], aux[0][:, 0:S], ACT.Copy)
                act.activation(yhl[:, h, 0, :], aux[0][:, 0:S], ACT.Copy).then_inc(ns["oc"], 1)

            def group(g_):
                after(act, ns["pv"], 4 * g_)
                act.activation(vs[:, :, :, :], vk[:, 1:3, g_, :, :], ACT.Copy)
                act.activation(vcs[0:WINS, :], vc_[0:WINS, g_, :], ACT.Copy).then_inc(ns["cp"], 1)

            for j in range(4):
                query(j, 0)
                look("q", j, 0)
                if j == 0:
                    act.wait_ge(ns["k2"], 1)
                    act.activation(kc_[:, :, :], aux[0][:, 0:CW], ACT.Copy)
                    act.activation(vc_[0:WINS, :, :], aux[1][0:WINS, :], ACT.Copy).then_inc(ns["kc"], 1)
            with act.Fori(1, 4) as i:
                g_ = i - 1
                group(g_)
                for j in range(4):
                    if j > 0:
                        take_p(g_, j - 1)
                        take_o(g_, j - 1)
                    exps(g_, j)
                    query(j, i)
                    look("q", j, i)
                take_p(g_, 3)
                take_o(g_, 3)
            group(3)
            for r in range(4):
                exps(3, r)
                take_p(3, r)
                take_o(3, r)
            out_phase("out1", 3)
            junction(3)
            up_phase("gu1", 1)
            down_phase("dn1", 4)
            junction(4, norm=False)

        @block.vector
        def _(dve):
            def split(u, nk=KD):
                dve.wait_ge(s_hi, u.n + 1)
                after(dve, s_unit, u.n - 1)
                dve.tensor_tensor(lo[u.half][:, 0:nk, :], raw[u.raw][:, 0:nk, :],
                                  hi[u.half][:, 0:nk, :].bitcast(F32), ALU.subtract).then_inc(s_lo, 1)

            def take(t, dst, width=S):
                dve.wait_ge(s_half, t.n + 1)
                dve.tensor_tensor(dst, lin[t.bank][:, 0:width], half[t.bank][:, 0:width], ALU.add).then_inc(s_free, 1)
                dve.wait_ge(s_free, t.n + 1)

            def step(ins):
                dve.wait_ge(v_.sem, v_.mark(ins))

            def norm_rest(norm):
                w = normw[:, 2 * norm, :]
                dve.wait_ge(s_root, 2 * norm + 1)
                step(dve.reciprocal(rstd[:, :], rstd[:, :]))
                for q in range(4):
                    if q >= 2:
                        dve.wait_ge(s_xhi, 4 * norm + q - 1)
                    for c in range(4):
                        ins = dve.scalar_tensor_tensor(xf4[q % 2][:, c, :], hnew[:, 4 * q + c, :],
                                                       w[:, 4 * q + c:4 * q + c + 1], rstd[:, :],
                                                       ALU.mult, ALU.mult)
                    ins.then_inc(s_xf, 1)
                    dve.wait_ge(s_xhi, 4 * norm + q + 1)
                    dve.tensor_tensor(xhl[:, 4 * q:4 * q + 4, 1, :], xf4[q % 2][:, :, :],
                                      xhl[:, 4 * q:4 * q + 4, 0, :].bitcast(F32), ALU.subtract).then_inc(s_xlo, 1)

            for b in range(2):
                dve.memset(cbuf[b][:, :], 0.0)
            step(dve.memset(R[:, :], 0.0))
            dve.wait_ge(s_prm, 16)
            norm_rest(0)
            split(Unit("ab", 0))
            split(Unit("ab", 1))
            take(Tile("ab", 0), abf[:, :])
            split(Unit("ab", 2))

            def conv(dst, src, w, taps, last):
                step(dve.tensor_scalar(dst, src[:, 0:S], w(0), None, ALU.mult))
                for k in range(1, taps):
                    ins = dve.scalar_tensor_tensor(dst, src[:, k:k + S], w(k), dst, ALU.mult, ALU.add)
                    if k < taps - 1:
                        step(ins)
                    elif last is not None:
                        ins.then_inc(last, 1)
                    else:
                        step(ins)

            def qkv_tiles(i):
                for j in range(4):
                    t = Tile("qkv", j, i)
                    c = i * 4 + j
                    take(t, cbuf[j % 2][:, 3:3 + S])
                    after(dve, s_silu, c - 1)
                    conv(cv[j % 2][:, :], cbuf[j % 2], lambda k: gconv[:, c, k:k + 1], 4, s_conv)
                    split(Unit("qkv", j + 2, i))

            qkv_tiles(0)
            with dve.Fori(1, 6) as i:
                v_.enter(i, 12, first=1)
                qkv_tiles(i)
                v_.leave(6)

            a0, a1, a2, a3, a4 = [x[0:8, :] for x in at4[0:5]]
            dve.tensor_scalar(a0, abf[0:8, :], dtb[0:8, :], None, ALU.add).then_inc(g["hb"], 1)
            dve.memset(ones256[:, :], 1.0)
            dve.wait_ge(g["eg"], 1)
            step(dve.tensor_scalar(a3, a1, 1.0, None, ALU.add))
            step(dve.scalar_tensor_tensor(a4, a3, -1.0, a1, ALU.add, ALU.subtract))
            step(dve.reciprocal(a3, a3))
            step(dve.tensor_tensor(a4, a4, a3, ALU.mult))
            step(dve.tensor_tensor(a2, a2, a4, ALU.subtract))
            step(dve.scalar_tensor_tensor(a2, a0, 0.0, a2, ALU.max, ALU.add))
            step(dve.tensor_scalar(a2, a2, tiny[0:8, 0:1], -1.0, ALU.mult, ALU.mult))
            for t in range(TT):
                sl = slice(t * P, (t + 1) * P)
                step(dve.tensor_tensor_scan(R[0:8, sl], ones256[0:8, sl], a2[:, sl], 0.0, ALU.mult, ALU.add))
            step(dve.tensor_scalar(R[32:40, :], R[32:40, :], 1.0, None, ALU.add))
            dve.reciprocal(R[32:40, :], R[32:40, :]).then_inc(g["ab"], 1)
            dve.wait_ge(g["rt"], 1)
            dve.tensor_copy(tiny[:, 8:16], aux[0][:, 0:8])
            dve.tensor_copy(tiny[:, 16:24], aux[1][:, 0:8])
            dve.tensor_copy(tiny[:, 24:32], aux[1][:, 0:8]).then_inc(g["kd"], 1)
            dve.tensor_copy(tiny[:, 52:60], aux[0][:, 32:40])
            step(dve.tensor_copy(tiny[:, 32:40], aux[1][:, 32:40]))
            dve.wait_ge(g["kd"], 2)
            step(dve.tensor_tensor(tiny[:, 40:48], tiny[:, 40:48], tiny[:, 32:40], ALU.mult))

            gcol = tiny[:, 8:24].rearrange("p (t i a) -> p t i a", t=2, a=2)
            bcol = [tiny[:, 52:60].rearrange("p (i a) -> p i a", a=2), tiny[:, 32:40].rearrange("p (i a) -> p i a", a=2)]
            bge = tiny[:, 40:48].rearrange("p (i a) -> p i a", a=2)
            y4 = yhl[:, :, :, :].rearrange("p (i a) l t -> p i a l t", a=2)

            def mix(i):
                n = i + 1
                for k in range(2):
                    for h in range(2):
                        ins = dve.tensor_scalar(rs[:, k, h, :], R[:, :], onehot[:, i, h, k:k + 1], None, ALU.mult)
                ins.then_inc(g["rs"], 1)

                def qk_norm():
                    dve.wait_ge(g["bcc"], n)
                    for t in range(2):
                        for h in range(2):
                            dve.tensor_scalar(dt_[:, 2 * h + t, :], bc[:, 0, h, t * P:(t + 1) * P],
                                              gcol[:, t, i, h:h + 1], 0.0, ALU.subtract, ALU.min)
                    for h in range(2):
                        ins = dve.tensor_scalar(tiny[:, 48 + h:49 + h], bc[:, 0, h, P - 1:P],
                                                gcol[:, 0, i, h:h + 1], None, ALU.subtract)
                    ins.then_inc(g["dt"], 1)
                    dve.wait_ge(g["nr"], 2 * n)
                    step(dve.reciprocal(nr[:, :, :, :], nr[:, :, :, :]))
                    dve.scalar_tensor_tensor(qn[:, :, :], qkv[:, 0, i, :, :], SCALE, nr[:, 0, :, :], ALU.mult, ALU.mult)
                    dve.tensor_tensor(kn[:, :, :], qkv[:, 1, i, :, :], nr[:, 1, :, :], ALU.mult).then_inc(g["kn"], 1)
                    dve.wait_ge(g["kn"], n)
                    dve.tensor_tensor(kb[:, :, :], kn[:, :, :], bc[:, 1, :, :], ALU.mult).then_inc(g["kb"], 1)
                    dve.wait_ge(g["eg"], n + 1)
                    dve.tensor_tensor(qg[:, :, :], qn[:, :, P:S], eg[:, :, :], ALU.mult).then_inc(g["qg"], 1)

                def vbs():
                    dve.wait_ge(g["tp"], n)
                    for h in range(2):
                        for t in range(2):
                            q = 2 * h + t
                            dve.tensor_scalar(vb[:, q, :], aux[3][:, q * P:(q + 1) * P], bcol[t][:, i, h:h + 1],
                                              None, ALU.mult)
                        dve.tensor_scalar(kdec[:, h, :], aux[2][:, 2 * h * P:(2 * h + 1) * P],
                                          tiny[:, 50 + h:51 + h], None, ALU.mult)
                        ins = dve.tensor_scalar(kbg[:, h, :], aux[2][:, (2 * h + 1) * P:(2 * h + 2) * P],
                                                bge[:, i, h:h + 1], None, ALU.mult)
                    ins.then_inc(g["vb"], 1)

                def masks():
                    dve.wait_ge(g["kk"], n)
                    dve.wait_ge(g["dm"], n)
                    dve.tensor_tensor(lt[:, :, :], aux[0][:, :].rearrange("p (q j) -> p q j", q=4), dt_[:, :, :],
                                      ALU.mult).then_inc(g["lt"], 1)
                    dve.tensor_tensor(att[:, :, :], aux[1][:, :].rearrange("p (q j) -> p q j", q=4), dt_[:, :, :],
                                      ALU.mult).then_inc(g["at"], 1)

                def inv(l):
                    dve.wait_ge(g["z"], i * LEVELS + l + 1)
                    s_ = 1 << l
                    for k, m in ((0, X), (1, PT)):
                        v = m[:, :, :].rearrange("p q (b h s) -> p (q b) h s", h=2, s=s_)[:, :, k, :]
                        z = aux[3][:, 256 * k:256 * (k + 1)].rearrange("p (b s) -> p b s", s=s_)
                        ins = dve.tensor_tensor(v, v, z, ALU.subtract)
                    ins.then_inc(g["xp"], 1)

                def zsilu():
                    dve.wait_ge(g["ez"], n)
                    step(dve.tensor_scalar(ez[:, :, :], ez[:, :, :], 1.0, None, ALU.add))
                    step(dve.reciprocal(ez[:, :, :], ez[:, :, :]))
                    step(dve.tensor_tensor(zs[:, :, :], zs[:, :, :], ez[:, :, :], ALU.mult))

                def low(a):
                    dve.wait_ge(s_yhi, 3 * i + a + 1)
                    dve.tensor_tensor(y4[:, i + 4, a, 1, :], cv[a][:, :], y4[:, i + 4, a, 0, :].bitcast(F32),
                                      ALU.subtract).then_inc(s_ylo, 1)

                plan = {1: [qk_norm], 2: [vbs], 4: [masks], 10: [zsilu], 17: [lambda: low(0)]}
                for l in range(LEVELS):
                    plan.setdefault(6 + 2 * l, []).append(lambda l=l: inv(l))
                for j in range(8):
                    for s_ in range(3):
                        for f in plan.get(3 * j + s_, []):
                            f()
                    t = Tile("mix", j, i, 8)
                    if j < 2:
                        dst = zs[:, j, :]
                    else:
                        a, w = (j - 2) // 3, (j - 2) % 3
                        dst = [up[0][:, :], up[1][:, :], up[0][:, :]][w]
                    take(t, dst)
                    if j >= 2 and w == 1:
                        step(dve.tensor_tensor(cbuf[a][:, 3:3 + S], up[0][:, :], up[1][:, :], ALU.mult))
                        conv(cv[a][:, :], cbuf[a][:, 1:3 + S], lambda k: sconv[:, i, a, k:k + 1], 3, None)
                    if j >= 2 and w == 2:
                        dve.tensor_tensor(cv[a][:, :], cv[a][:, :], up[0][:, :], ALU.mult).then_inc(s_yf, 1)
                    split(Unit("mix", j + 2, i, 8))
                low(1)
                dve.wait_ge(g["orn"], n)
                step(dve.reciprocal(orn[:, :, :], orn[:, :, :]))
                step(dve.scalar_tensor_tensor(ot[:, :, :], ot[:, :, :], gnorm, orn[:, :, :], ALU.mult, ALU.mult))
                dve.tensor_tensor(ot[:, :, :], ot[:, :, :], zs[:, :, :], ALU.mult).then_inc(s_yf, 1)
                dve.wait_ge(s_yhi, 3 * i + 3)
                dve.tensor_tensor(y4[:, i, :, 1, :], ot[:, :, :], y4[:, i, :, 0, :].bitcast(F32),
                                  ALU.subtract).then_inc(s_ylo, 1)

            MIX_STEPS = 14
            with dve.Fori(0, 4) as i:
                v_.enter(i, MIX_STEPS)
                mix(i)
                v_.leave(4)

            def look(phase, j, i=0, per=4):
                if isinstance(i, int):
                    off = U0[phase] + j + per * i + 2
                    if off >= UNITS:
                        return
                    nk = DN_K if any(U0[x] <= off < U0[x] + N_UNITS[x] for x in ("dn0", "dn1")) else KD
                else:
                    nk = DN_K if phase[:2] == "dn" else KD
                split(Unit(phase, j + 2, i, per), nk)

            def add_square(m, j, b):
                dve.wait_ge(s_msq, 16 * (j - 1) + m + 1)
                dve.wait_ge(s_ssq, 17 * (j - 1) + 1 + m)
                dve.tensor_tensor(ssq[:, :], ssq[:, :], sqd[b][:, :], ALU.add).then_inc(s_ssq, 1)

            def out_phase(phase, jn):
                dve.memset(ssq[:, :], 0.0).then_inc(s_ssq, 1)
                with dve.Fori(0, 4) as i:
                    for j in range(4):
                        take(Tile(phase, j, i), mout[:, 4 * i + j, :])
                        look(phase, j, i)
                        add_square(4 * i + j, jn, j % 2)

            def up_phase(phase, layer):
                def pairs(i):
                    for a in range(2):
                        c = 2 * i + a
                        take(Tile(phase, 2 * a, i), cbuf[a][:, 3:3 + S])
                        dve.wait_ge(s_silu, 24 + KF * layer + c - 1)
                        conv(cv[a][:, :], cbuf[a][:, 1:3 + S], lambda k: fconv[:, layer, c, k:k + 1], 3, s_conv)
                        look(phase, 2 * a, i)
                        take(Tile(phase, 2 * a + 1, i), up[a][:, :])
                        dve.wait_ge(s_silu, 24 + KF * layer + c + 1)
                        after(dve, s_midhi, KF * layer + c - 1)
                        dve.tensor_tensor(mf[a][:, :], sil[a][:, :], up[a][:, :], ALU.mult).then_inc(s_mid, 1)
                        look(phase, 2 * a + 1, i)
                        dve.wait_ge(s_midhi, KF * layer + c + 1)
                        dve.tensor_tensor(mid[:, c, 1, :], mf[a][:, :], mid[:, c, 0, :].bitcast(F32),
                                          ALU.subtract).then_inc(s_midlo, 1)
                pairs(0)
                with dve.Fori(1, 21) as i:
                    v_.enter(i, 4, first=1)
                    pairs(i)
                    v_.leave(21)
                pairs(21)

            def down_phase(phase, jn):
                dve.memset(ssq[:, :], 0.0).then_inc(s_ssq, 1)
                def tiles(i):
                    for a in range(2):
                        for q in range(4):
                            if q == 3:
                                take(Tile(phase, a, i, 2), mout[:, 2 * i + a, :])
                            look(phase, 4 * a + q, i, 8)
                        add_square(2 * i + a, jn, a)
                with dve.Fori(0, 7) as i:
                    tiles(i)
                tiles(7)

            def junction(j, norm=True):
                w = normw[:, 2 * j - 1, :]
                dve.wait_ge(s_root, 2 * j)
                step(dve.reciprocal(rstd[:, :], rstd[:, :]))
                dve.wait_ge(s_hload, 16 * (j + 1))
                for q in range(4):
                    m4 = mout[:, 4 * q:4 * q + 4, :]
                    step(dve.tensor_tensor(m4, m4, rstd[:, :].unsqueeze(1).broadcast_to([P, 4, S]), ALU.mult))
                    for c in range(4 * q, 4 * q + 4):
                        ins = dve.scalar_tensor_tensor(hnew[:, c, :], mout[:, c, :], w[:, c:c + 1], hold[:, c, :],
                                                       ALU.mult, ALU.add)
                    ins.then_inc(s_hn, 1)
                if norm:
                    dve.wait_ge(s_hn, 4 * j)
                    norm_rest(j)

            out_phase("out0", 1)
            junction(1)
            up_phase("gu0", 0)
            down_phase("dn0", 2)
            junction(2)

            dve.wait_ge(s_hstore, 32)
            dve.wait_ge(s_l1c, 16)
            take(Tile("gate", 0), gts[:, :])
            look("gate", 0)

            def rotary(b, dst, count):
                dve.wait_ge(ns["swap"], count)
                step(dve.tensor_tensor(cv[b][:, :], cv[b][:, :], C1["cos"], ALU.mult))
                step(dve.tensor_tensor(up[b][:, :], up[b][:, :], C1["sin"], ALU.mult))
                dve.tensor_tensor(dst, cv[b][:, :], up[b][:, :], ALU.add).then_inc(ns["rope"], 1)

            def kv(i):
                for j in range(8):
                    t = Tile("kv", j, i, 8)
                    if j < 4:
                        take(t, cv[j % 2][:, :])
                        rotary(j % 2, kt[:, i, j, :], 4 * i + j + 1)
                    else:
                        after(dve, ns["vk_"], 4 * (i - 1) + j - 3)
                        take(t, vst[:, j - 4, :])
                    look("kv", j, i, 8)
                    if j == 0 and isinstance(i, int):
                        dve.wait_ge(ns["sg"], 1)
                        sg = sig[:, :, :, :].rearrange("p t b h -> p (t b h)")
                        step(dve.tensor_scalar(sg, sg, 1.0, None, ALU.add))
                        step(dve.reciprocal(sg, sg))
                        for t_ in range(TT):
                            dve.tensor_copy(gt[:, :, 2 * t_:2 * t_ + 2], sig[:, t_, 1:3, :].rearrange("p b h -> p h b"))
                            ins = dve.tensor_copy(gt[:, :, 4 + t_:5 + t_], sig[:, t_, 0:1, :].rearrange("p b h -> p h b"))
                        step(ins)

            kv(0)
            for kind in range(2):
                pos = C1["posv" if kind else "posk"].rearrange("p (a b) -> p a b", a=2)
                src = (vst[:, :, :] if kind else kt[:, 0, :, :]).rearrange("p g (w b) -> p g w b", b=16)
                dve.wait_ge(ns["rope"], 4)
                if kind:
                    dve.wait_ge(ns["xcl"], 1)
                for a in range(2):
                    ins = dve.tensor_tensor(xct[:, 16 * a:16 * a + 16, :, :],
                                            src[:, :, a:a + WINS, :].rearrange("p g w b -> p b g w"),
                                            pos[:, a, :].unsqueeze(2).unsqueeze(3).broadcast_to([P, 16, NG, WINS]),
                                            ALU.add)
                ins.then_inc(ns["xcw"], 1)
                dve.wait_ge(ns["xch"], kind + 1)
                dve.tensor_tensor(xc[kind][:, :, 1, :], xct[:, :, :, :].rearrange("p l g c -> p l (g c)"),
                                  xc[kind][:, :, 0, :].bitcast(F32), ALU.subtract).then_inc(ns["xcl"], 1)
            with dve.Fori(1, 3) as i:
                v_.enter(i, 8, first=1)
                kv(i)
                v_.leave(3)
            for kind in range(2):
                for ht in range(2):
                    for q in range(2):
                        if q == 1:
                            take(Tile("cmp", 2 * kind + ht), h1[:, 2 * kind + ht, :], CW)
                        look("cmp", 4 * kind + 2 * ht + q)

            def query(j, i):
                take(Tile("q", j, i), cv[j % 2][:, :])
                after(dve, ns["sc"], 4 * (i - 1) + j + 1)
                rotary(j % 2, qs[:, j, :], 12 + 4 * i + j + 1)

            def maxima(g_, r):
                h = 4 * g_ + r
                dve.wait_ge(ns["sc"], h + 1)
                after(dve, ns["tp"], h)
                dve.tensor_tensor(smc[:, :, 0:WINS], aux[3][:, 0:32].rearrange("p (t c) -> p t c", t=2)[:, :, 0:WINS],
                                  C1["cmask"].rearrange("p (t c) -> p t c", t=2), ALU.add)
                dve.tensor_tensor(sm0[:, :, :], aux[0][:, 0:S].rearrange("p (b k) -> p b k", b=2),
                                  C1["causal"][:, P:S].unsqueeze(1).broadcast_to([P, 2, P]), ALU.add)
                step(dve.tensor_tensor(sm1[:, :, :], aux[1][:, :].rearrange("p (b k) -> p b k", b=2),
                                       C1["causal"][:, 0:S].unsqueeze(1).broadcast_to([P, 2, S]), ALU.add))
                dve.tensor_reduce(soft[:, 0:2], sm0[:, :, :], AX.X, ALU.max)
                dve.tensor_reduce(soft[:, 2:4], sm1[:, :, :], AX.X, ALU.max)
                step(dve.tensor_reduce(soft[:, 4:6], smc[:, :, 0:WINS], AX.X, ALU.max))
                dve.tensor_scalar(soft[:, 8:14], soft[:, 0:6], -SCALE, None, ALU.mult).then_inc(ns["mx"], 1)

            def weigh(g_, r):
                h = 4 * g_ + r
                dve.wait_ge(ns["ex"], h + 1)
                step(dve.reciprocal(soft[:, 24:30], soft[:, 16:22]))
                step(dve.tensor_tensor(soft[:, 24:30], soft[:, 24:30], gt[:, h, :], ALU.mult))
                for b in range(2):
                    dve.tensor_scalar(sm0[:, b, :], sm0[:, b, :], soft[:, 24 + b:25 + b], None, ALU.mult)
                    dve.tensor_scalar(sm1[:, b, :], sm1[:, b, :], soft[:, 26 + b:27 + b], None, ALU.mult)
                    ins = dve.scalar_tensor_tensor(smc[:, b, 0:WINS], smc[:, b, 0:WINS], soft[:, 28 + b:29 + b],
                                                   C1["cvalid"].rearrange("p (t c) -> p t c", t=2)[:, b, :],
                                                   ALU.mult, ALU.mult)
                ins.then_inc(ns["p"], 1)

            def take_p(g_, r):
                dve.wait_ge(ns["tp"], 4 * g_ + r + 1)
                dve.tensor_copy(pt[:, :, P:3 * P], aux[3][:, :].rearrange("p (b t) -> p b t", b=2)).then_inc(ns["ptd"], 1)

            def low(g_, r):
                h = 4 * g_ + r
                dve.wait_ge(ns["oc"], h + 1)
                dve.tensor_tensor(yhl[:, h, 1, :], of[r % 2][:, :], yhl[:, h, 0, :].bitcast(F32),
                                  ALU.subtract).then_inc(s_ylo, 1)

            for j in range(4):
                query(j, 0)
                look("q", j, 0)
            with dve.Fori(1, 4) as i:
                g_ = i - 1
                v_.enter(i, 24, first=1)
                for j in range(4):
                    if j > 0:
                        take_p(g_, j - 1)
                        low(g_, j - 1)
                    maxima(g_, j)
                    weigh(g_, j)
                    query(j, i)
                    look("q", j, i)
                take_p(g_, 3)
                low(g_, 3)
                v_.leave(4)
            for r in range(4):
                maxima(3, r)
                weigh(3, r)
                take_p(3, r)
                low(3, r)
            out_phase("out1", 3)
            junction(3)
            up_phase("gu1", 1)
            down_phase("dn1", 4)
            junction(4, norm=False)

        @block.gpsimd
        def _(pool):
            pool.wait_ge(s_prm, 16)
            pool.wait_ge(s_l0c, 16)
            l_ = level
            with pool.Fori(0, 4) as i:
                n = i + 1
                pool.wait_ge(g["de"], n)
                for q in range(4):
                    ins = pool.tensor_tensor(dt_[:, q, :], dt_[:, q, :], triu, ALU.mult)
                ins.then_inc(g["dm"], 1)
                pool.wait_ge(g["bc"], 2 * n)
                for q in range(4):
                    pool.tensor_tensor(X[:, q, :], ident, ident, ALU.mult)
                    ins = pool.tensor_tensor(PT[:, q, :], ident, ident, ALU.mult)
                ins.then_inc(g["xi"], 1)
                pool.wait_ge(g["lt"], n)
                for l in range(LEVELS):
                    if l >= 2:
                        pool.wait_ge(g["y"], i * LEVELS + l - 1)
                    for q in range(4):
                        ins = pool.tensor_tensor(nt[l % 2][:, q, :], lt[:, q, :], level[:, l, :], ALU.mult)
                    ins.then_inc(g["nt"], 1)


def layouts(np, a):
    f = np.float32

    def chunks(v):
        v = v.reshape(v.shape[:-1] + (v.shape[-1] // P, P))
        return np.moveaxis(v, -1, 0)

    def units(w, cols):
        k = w.shape[0] // P
        return np.ascontiguousarray(w.reshape(k, P, w.shape[1])[:, :, cols].reshape(k, P, -1, P).transpose(2, 1, 0, 3))

    r = {}
    r["x"] = np.ascontiguousarray(a["x"][0].T.reshape(KD, P, S).transpose(1, 0, 2))
    w0 = a["ab_w_in"][0]
    ab = np.zeros((D, P), w0.dtype)
    ab[:, 0:8] = w0[:, 4096:4104]
    ab[:, 32:40] = w0[:, 4104:4112]
    cols = list(range(3072))
    z, hb, gb, gc = 3072, 4112, 5136, 6160
    for i in range(4):
        for s_, t in ((z, 0), (z, 1), (hb, 0), (gc, 0), (gb, 0), (hb, 1), (gc, 1), (gb, 1)):
            c = s_ + (2 * i + t) * P
            cols += list(range(c, c + P))
    r["w_in0"] = np.concatenate([units(ab, np.arange(P)), units(w0, np.array(cols))], 0)
    prm = np.zeros((P, N_PARAM), f)

    def put(name, v):
        c, w = PARAM[name]
        prm[:, c:c + w] = v.reshape(P, w)

    put("norm", chunks(a["norm_w"].reshape(8, D)))
    put("gconv", chunks(a["gdn_conv"][0]).transpose(0, 2, 1))
    put("sconv", chunks(a["sc_conv"][0]).transpose(0, 2, 1))
    put("fconv", chunks(a["ffn_conv"]).transpose(0, 1, 3, 2))
    put("gnorm", a["gdn_norm"][0][:, None])
    v = np.zeros((P, 1), f)
    v[0:8, 0] = a["gdn_a_log"][0]
    put("alog", v)
    v = np.zeros((P, 1), f)
    v[0:8, 0] = a["gdn_dt_bias"][0]
    put("dtb", v)
    put("eps", np.full((P, 1), EPS, f))
    oh = np.zeros((P, 8, 2), f)
    for h in range(8):
        oh[h, h, 0] = 1
        oh[32 + h, h, 1] = 1
    put("onehot", oh)
    put("ident", np.eye(P, dtype=f))
    put("ones", np.ones((P, P), f))
    r["params"] = prm
    j, i = np.arange(P)[:, None], np.arange(P)[None, :]
    l0 = [(i >= j).astype(f)]
    for l in range(LEVELS):
        s_ = 1 << l
        l0.append(((i // (2 * s_) == j // (2 * s_)) & (j // s_ % 2 == 0) & (i // s_ % 2 == 1)).astype(f))
    r["l0c"] = np.concatenate(l0, 1)
    every = np.arange(D)
    r["w_out0"] = units(a["ab_w_out"][0], every)
    r["w_out1"] = units(a["nsa_w_out"][0], every)
    for l in range(2):
        gu = a["ffn_w_gu"][l]
        cols = np.arange(2 * FF).reshape(2, KF, P).transpose(1, 0, 2).ravel()
        r[f"w_gu{l}"] = units(gu, cols)
        dn = units(a["ffn_w_down"][l], every)
        r[f"w_dn{l}"] = np.ascontiguousarray(dn.reshape(KD, P, 4, DN_K, P).transpose(0, 2, 1, 3, 4)).reshape(64, P, DN_K, P)
    w1 = a["nsa_w_in"][0]
    gates = np.zeros((D, P), w1.dtype)
    gates[:, 0:48] = w1[:, 5120:5168]
    r["w_in1"] = np.concatenate([units(gates, np.arange(P)), units(w1, np.arange(2048, 5120)), units(w1, every)], 0)
    c = []
    for name in ("cmp_w1_k", "cmp_w1_v"):
        c.append(a[name][0].reshape(2, 16, P, 2, P).transpose(3, 0, 2, 1, 4).reshape(4, P, 16, P))
    r["w_cmp"] = np.ascontiguousarray(np.concatenate(c, 0))
    l1 = np.zeros((P, N_L1C), f)

    def put1(name, v):
        c, w = L1C[name]
        l1[:, c:c + w] = v.reshape(P, w)

    inv = 1.0 / (10000.0 ** (np.arange(0, P, 2, dtype=f) / f(P)))
    ang = (np.arange(S, dtype=f)[:, None] * inv[None, :].astype(f)).astype(f)
    put1("cos", np.concatenate([np.cos(ang).T, np.cos(ang).T], 0))
    put1("sin", np.concatenate([-np.sin(ang).T, np.sin(ang).T], 0))
    causal = np.where(np.arange(P)[None, :] <= np.arange(P)[:, None], 0, NEG).astype(f)
    put1("causal", np.concatenate([np.zeros((P, P), f), causal], 1))
    tok = np.arange(S).reshape(TT, P).T[:, :, None]
    ok = np.arange(WINS)[None, None, :] * 16 + 31 <= tok
    put1("cmask", np.where(ok | (tok < 31), 0, NEG).astype(f))
    put1("cvalid", ok.astype(f))
    put1("posk", a["cmp_pos_k"][0].T)
    put1("posv", a["cmp_pos_v"][0].T)
    for n, k in (("w2k", "cmp_w2_k"), ("w2v", "cmp_w2_v")):
        put1(n, a[k][0].reshape(2, P, P).transpose(1, 0, 2))
    r["l1c"] = l1
    return r



def kernel(**inputs):
    import numpy as np
    import concourse.bacc as bacc
    from concourse.bass_utils import run_bass_kernel_spmd

    nc = bacc.Bacc("TRN2", target_bir_lowering=False, num_devices=1)
    arrays = {"in_" + k: v for k, v in layouts(np, {k: np.asarray(v) for k, v in inputs.items()}).items()}
    A = {k[3:]: nc.dram_tensor(k, v.shape, F32, kind="ExternalInput").ap() for k, v in arrays.items()}
    A["residual"] = nc.dram_tensor("residual", (P, KD, S), F32, kind="Internal").ap()
    out = nc.dram_tensor("out", (P, KD, S), F32, kind="ExternalOutput").ap()
    build(nc, A, out)
    got = run_bass_kernel_spmd(nc, [arrays], core_ids=[0]).results[0]["out"]
    return np.ascontiguousarray(got.transpose(1, 0, 2).reshape(D, S).T[None])
```

```python
from contextlib import ExitStack

import concourse.bass as bass
from concourse import mybir

F32 = mybir.dt.float32
F32R = mybir.dt.float32r
ACT = mybir.ActivationFunctionType
ALU = mybir.AluOpType
AX = mybir.AxisListType

P = 128
S = 256
D = 2048
KD = D // P
FF = 5632
KF = FF // P
DN_K = KF // 4
HEADS = 8
TT = S // P
LEVELS = 7
NG, NR = 4, 4
WINS = S // 16 - 1
CW = NG * WINS
EPS = 1e-6
NEG = -1e30
SCALE = float(P) ** -0.5

PHASES = ["ab", "qkv", "mix", "out0", "gu0", "dn0", "gate", "kv", "cmp", "q", "out1", "gu1", "dn1"]
N_UNITS = dict(ab=1, qkv=24, mix=32, out0=16, gu0=88, dn0=64, gate=1, kv=24, cmp=8, q=16, out1=16, gu1=88, dn1=64)
N_TILES = dict(N_UNITS, dn0=16, dn1=16, cmp=4)
U0, T0 = {}, {}
_u = _t = 0
for _p in PHASES:
    U0[_p], T0[_p] = _u, _t
    _u += N_UNITS[_p]
    _t += N_TILES[_p]
UNITS = _u

PARAM = {}
_c = 0
for _n, _w in [("norm", 8 * KD), ("gconv", 24 * 4), ("sconv", 8 * 3), ("fconv", 2 * KF * 3), ("gnorm", 1),
               ("alog", 1), ("dtb", 1), ("eps", 1), ("onehot", 2 * HEADS), ("ident", P), ("ones", P)]:
    PARAM[_n] = (_c, _w)
    _c += _w
N_PARAM = _c
L0C = {"triu": (0, P), "level": (P, LEVELS * P)}
N_L0C = P + LEVELS * P
L1C = {}
_c = 0
for _n, _w in [("cos", S), ("sin", S), ("causal", S), ("cmask", TT * WINS), ("cvalid", TT * WINS),
               ("posk", 32), ("posv", 32), ("w2k", 2 * P), ("w2v", 2 * P)]:
    L1C[_n] = (_c, _w)
    _c += _w
N_L1C = _c


class Unit:

    def __init__(self, phase, j, i=0, per=4):
        off = U0[phase] + j
        self.n = off + per * i
        self.raw = off % 4
        self.half = off % 2
        self.loads = 16 * (off // 4 + 1) + 16 * (per // 4) * i


class Tile:

    def __init__(self, phase, j, i=0, per=4, bank=None):
        off = T0[phase] + j
        self.n = off + per * i
        self.bank = off % 4 if bank is None else bank


class Steps:

    def __init__(self, sem):
        self.sem, self.base, self.k, self.i, self.per = sem, 0, 0, None, 0

    def enter(self, i, per, first=0):
        self.base += self.k - first * per
        self.k, self.i, self.per = 0, i, per

    def leave(self, end):
        assert self.k == self.per, (self.k, self.per)
        self.base += end * self.per
        self.k, self.i = 0, None

    def mark(self, ins):
        ins.then_inc(self.sem, 1)
        self.k += 1
        return self.base + self.k + (self.i * self.per if self.i is not None else 0)


def after(eng, sem, value):
    if not isinstance(value, int) or value > 0:
        eng.wait_ge(sem, value)


def build(nc, A, out):
    ctx = ExitStack()
    base0 = (nc.sbuf_base + 63) // 64 * 64

    def at(name, offset, shape, dt=F32):
        return nc.alloc_sbuf_tensor_at(name, shape, dt, offset=base0 + offset)

    KB = 1024
    with ctx:
        def sem(name):
            return ctx.enter_context(nc.semaphore(name))

        raw = [at(f"raw{i}", i * 8 * KB, [P, KD, P]) for i in range(4)]
        hi = [at(f"hi{i}", (32 + 8 * i) * KB, [P, KD, P], F32R) for i in range(2)]
        lo = [at(f"lo{i}", (48 + 8 * i) * KB, [P, KD, P], F32R) for i in range(2)]
        XO = 64 * KB
        xhl = at("xhl", XO, [P, KD, 2, S], F32R)
        mh = at("mh", XO, [P, KD, 2, S])
        mout, hold = mh[:, :, 0, :], mh[:, :, 1, :]
        MO = 96 * KB
        mid = at("mid", MO, [P, KF, 2, S], F32R)
        yhl = at("yhl", MO, [P, KD, 2, S], F32R)
        hnew = at("hnew", MO + 72 * KB, [P, KD, S])
        sq4 = [at(f"sq4_{i}", MO + 40 * KB + 4 * KB * i, [P, 4, S]) for i in range(2)]
        WO = MO + 88 * KB

        qkv = at("qkv", MO + 32 * KB, [P, 3, 4, 2, S])
        G = MO + 56 * KB
        rs = at("rs", G, [P, 2, 2, S])
        X = at("X", G, [P, 4, P])
        PT = at("PT", G + 2 * KB, [P, 4, P])
        dt_ = at("dt_", G + 4 * KB, [P, 4, P])
        yb_ = at("yb_", G + 4 * KB, [P, 4, P])
        bc = at("bc", G + 6 * KB, [P, 2, 2, S])
        nt = [at(f"nt{i}", G + 6 * KB + 2 * KB * i, [P, 4, P]) for i in range(2)]
        nr = at("nr", G + 10 * KB, [P, 2, 2, S])
        dqk = at("dqk", G + 10 * KB, [P, 8, P])
        vb = at("vb", G + 10 * KB, [P, 4, P])
        kdec = at("kdec", G + 12 * KB, [P, 2, P])
        kbg = at("kbg", G + 13 * KB, [P, 2, P])
        kb = at("kb", G + 14 * KB, [P, 2, S])
        vn0 = at("vn0", G + 14 * KB, [P, 2, P])
        vn1 = at("vn1", G + 15 * KB, [P, 2, P])
        qn = at("qn", G + 16 * KB, [P, 2, S])
        ot = at("ot", G + 18 * KB, [P, 2, S])
        vw = at("vw", G + 20 * KB, [P, 2, S])
        osq = at("osq", G + 20 * KB, [P, 2, S])
        lt = at("lt", G + 22 * KB, [P, 4, P])
        do_ = at("do_", G + 22 * KB, [P, 4, P])
        kn = at("kn", G + 24 * KB, [P, 2, S])
        wt = at("wt", G + 24 * KB, [P, 2, P])
        s1 = at("s1", G + 25 * KB, [P, 2, P])
        qg = at("qg", G + 26 * KB, [P, 2, P])
        eg = at("eg", G + 27 * KB, [P, 2, P])
        att = at("att", G + 28 * KB, [P, 4, P])
        zs = at("zs", G + 30 * KB, [P, 2, S])

        kt = at("kt", MO + 32 * KB, [P, 3, NG, S])
        vk = at("vk", MO + 44 * KB, [P, 3, NG, TT, P])
        l1c = at("l1c", MO + 56 * KB, [P, N_L1C])
        xc = [at(f"xc{k}", MO + 15 * KB * k, [P, 32, 2, CW], F32R) for k in range(2)]
        assert N_L1C * 4 <= 7 * KB
        B1 = MO + 63 * KB
        h1 = at("h1", B1, [P, 4, CW])
        kc_ = at("kc_", B1 + 1024, [P, NG, WINS])
        vc_ = at("vc_", B1 + 1280, [P, NG, P])
        sig = at("sig", B1 + 3328, [P, TT, 3, 16])
        gt = at("gt", B1 + 3712, [P, 16, 6])
        B2 = MO + 68 * KB
        vst = at("vst", B2, [P, NG, S])
        xct = at("xct", B2 + 4 * KB, [P, 32, NG, WINS])
        gts = at("gts", B2 + 12 * KB, [P, S])
        qs = at("qs", B2, [P, NR, S])
        sm1 = at("sm1", B2 + 4 * KB, [P, 2, S])
        sm0 = at("sm0", B2 + 6 * KB, [P, 2, P])
        smc = at("smc", B2 + 7 * KB, [P, TT, 16])
        soft = at("soft", B2 + 7 * KB + 128, [P, 32])
        pt = at("pt", B2 + 8 * KB, [P, 2, 3 * P])
        ptc = at("ptc", B2 + 11 * KB, [P, S])
        vs = at("vs", B2 + 12 * KB, [P, 2, TT, P])
        vcs = at("vcs", B2 + 14 * KB, [P, P])
        of = [at(f"of{k}", B2 + 15 * KB + KB * k, [P, S]) for k in range(2)]
        C1 = {n: l1c[:, c:c + w] for n, (c, w) in L1C.items()}

        o = WO
        def small(name, shape, dt=F32):
            nonlocal o
            n = 4
            for s_ in shape[1:]:
                n *= s_
            t = at(name, o, shape, dt)
            o += (n + 31) // 32 * 32
            return t

        prm = small("prm", [P, N_PARAM])
        half = [small(f"half{i}", [P, CW]) for i in range(2)]
        cbuf = [small(f"cbuf{i}", [P, 3 + S]) for i in range(2)]
        cv = [small(f"cv{i}", [P, S]) for i in range(2)]
        up = [small(f"up{i}", [P, S]) for i in range(2)]
        ssq = small("ssq", [P, S])
        sqd = [small(f"sqd{i}", [P, S]) for i in range(2)]
        rstd = small("rstd", [P, S])
        tiny = small("tiny", [P, 96])
        diag = [x[:, :].rearrange("p (t j) -> p t j", t=TT) for x in sqd]
        wend = o
        sil = [small(f"sil{i}", [P, S]) for i in range(2)]
        mf = [small(f"mf{i}", [P, S]) for i in range(2)]
        o = wend
        l0c = small("l0c", [P, N_L0C])
        R = small("R", [P, S])
        abf = small("abf", [P, S])
        at4 = [at(f"at{i}", G + i * KB, [P, S]) for i in range(8)]
        ones256 = at("ones256", G + 8 * KB, [P, S])

        def prm_(name, *dims):
            c, w = PARAM[name]
            return prm[:, c:c + w]

        normw = prm_("norm").rearrange("p (l c) -> p l c", l=8)
        norm1 = prm_("norm").rearrange("p (l c o) -> p l c o", l=8, o=1)
        gconv = prm_("gconv").rearrange("p (c k) -> p c k", k=4)
        sconv = prm_("sconv").rearrange("p (i a k) -> p i a k", a=2, k=3)
        fconv = prm_("fconv").rearrange("p (l c k) -> p l c k", l=2, k=3)
        onehot = prm_("onehot").rearrange("p (i a k) -> p i a k", a=2, k=2)
        gnorm, alog, dtb, eps = prm_("gnorm"), prm_("alog"), prm_("dtb"), prm_("eps")
        ident, ones = prm_("ident"), prm_("ones")
        triu = l0c[:, 0:P]
        level = l0c[:, P:].rearrange("p (l j) -> p l j", l=LEVELS)

        lin = [ctx.enter_context(nc.psum_tensor(f"lin{i}", [P, 512], F32)) for i in range(4)]
        aux = [ctx.enter_context(nc.psum_tensor(f"aux{i}", [P, 512], F32)) for i in range(4)]

        s_prm = sem("s_prm")
        s_l0c = sem("s_l0c")
        s_w = [sem(f"s_w{i}") for i in range(4)]
        s_hi = sem("s_hi")
        s_lo = sem("s_lo")
        s_wh = sem("s_wh")
        s_unit = sem("s_unit")
        s_half = sem("s_half")
        s_free = sem("s_free")
        v_ = Steps(sem("s_dve"))
        a_ = Steps(sem("s_act"))
        s_hload = sem("s_hload")
        s_out = sem("s_out")
        s_hstore = sem("s_hstore")
        s_hn = sem("s_hn")
        s_sq4 = sem("s_sq4")
        s_nps = sem("s_nps")
        s_root = sem("s_root")
        s_x = [sem(f"s_x{i}") for i in range(4)]
        s_col = sem("s_col")
        s_bc = sem("s_bc")
        s_rs = sem("s_rs")
        s_xhi = sem("s_xhi")
        s_xlo = sem("s_xlo")
        s_msq = sem("s_msq")
        s_ssq = sem("s_ssq")
        s_conv = sem("s_conv")
        s_silu = sem("s_silu")
        s_mid = sem("s_mid")
        s_midhi = sem("s_midhi")
        s_midlo = sem("s_midlo")
        s_yf = sem("s_yf")
        s_yhi = sem("s_yhi")
        s_ylo = sem("s_ylo")
        a_names = "gt gtp sg ge gn vt vk vk_ xck xch xcl ge2 h1 k2 kc swap rope sc sm mx ex p tp pta ptd pv oc cp xcw".split()
        ns = {x: sem("n_" + x) for x in a_names}
        s_l1c = sem("s_l1c")
        s_post = sem("s_post")
        s_pbc2 = sem("s_pbc2")
        s_pbc = sem("s_pbc")
        g_names = ("ab rt rs bc bcc sq ss nr vw kn kb dt de eg qg dm kd tp vb kk lt at xi nt y yb z xp uw vn0 s1 s1c "
                   "v1 v1c o oc on orn zs hb dq qb do ob zs2").split()
        g = {n: sem("g_" + n) for n in g_names}

        block = ctx.enter_context(nc.Block())

        @block.sync
        def _(sp):
            sp.dma_start(prm[:, :], A["params"]).then_inc(s_prm, 16)

            def x_group(q):
                sp.dma_start(hnew[:, 4 * q:4 * q + 4, :], A["x"][:, 4 * q:4 * q + 4, :]).then_inc(s_x[q], 16)

            x_group(0)

            def load(u, src, nk=KD):
                after(sp, s_lo, u.n - 3)
                sp.dma_start(raw[u.raw][:, 0:nk, :], src).then_inc(s_w[u.raw], 16)

            w = A["w_in0"]
            load(Unit("ab", 0), w[0])
            for q in range(1, 4):
                x_group(q)
            for j in range(1, 4):
                load(Unit("ab", j), w[j])
            sp.dma_start(l0c[:, :], A["l0c"]).then_inc(s_l0c, 16)
            load(Unit("ab", 4), w[4])
            with sp.Fori(0, 13) as i:
                for j in range(4):
                    load(Unit("ab", 5 + j, i), w[i * 4 + 5 + j])

            def loads(phase, w, nk=KD):
                with sp.Fori(1, N_UNITS[phase] // 4) as i:
                    for j in range(4):
                        load(Unit(phase, j, i), w[i * 4 + j], nk)

            def first(phase, w, nk=KD):
                for j in range(4):
                    load(Unit(phase, j), w[j], nk)

            def residual(j, phase):
                sp.wait_ge(s_unit, U0[phase])
                if j > 1:
                    sp.wait_ge(s_hstore, 16 * (j - 1))
                sp.dma_start(hold, A["x"] if j == 1 else A["residual"]).then_inc(s_hload, 16)

            def store(j):
                sp.wait_ge(s_hn, 4 * j)
                sp.wait_ge(s_hload, 16 * j)
                sp.dma_start(A["residual"], hnew[:, :, :]).then_inc(s_hstore, 16)

            first("out0", A["w_out0"])
            loads("out0", A["w_out0"])
            residual(1, "out0")
            first("gu0", A["w_gu0"])
            store(1)
            loads("gu0", A["w_gu0"])
            first("dn0", A["w_dn0"], DN_K)
            loads("dn0", A["w_dn0"], DN_K)
            residual(2, "dn0")
            w = A["w_in1"]
            for j in range(4):
                load(Unit("gate", j), w[j])
            sp.wait_ge(s_unit, U0["gate"])
            sp.dma_start(l1c[:, :], A["l1c"]).then_inc(s_l1c, 16)
            store(2)
            load(Unit("gate", 4), w[4])
            with sp.Fori(0, 5) as i:
                for j in range(4):
                    load(Unit("gate", 5 + j, i), w[i * 4 + 5 + j])
            for j in range(8):
                load(Unit("cmp", j), A["w_cmp"][j])
            for j in range(16):
                load(Unit("q", j), w[25 + j])
            first("out1", A["w_out1"])
            loads("out1", A["w_out1"])
            residual(3, "out1")
            first("gu1", A["w_gu1"])
            store(3)
            loads("gu1", A["w_gu1"])
            first("dn1", A["w_dn1"], DN_K)
            loads("dn1", A["w_dn1"], DN_K)
            residual(4, "dn1")
            for q in range(4):
                sp.wait_ge(s_hn, 16 - 3 + q)
                sp.dma_start(out[:, 4 * q:4 * q + 4, :], hnew[:, 4 * q:4 * q + 4, :]).then_inc(s_out, 16)
            sp.wait_ge(s_out, 64)

        @block.tensor
        def _(pe):
            def passes(u, bank, hi_, lo_, nk, start, stop, ready=None, slot=None):
                pe.wait_ge(s_hi, u.n + 1)
                for k in range(nk):
                    if ready is not None:
                        ready(k)
                    pe.matmul(bank[:, 0:S], hi[u.half][:, k, :], hi_(k), start=start and k == 0, stop=False,
                              skip_group_check=True)
                    m = pe.matmul(bank[:, 0:S], hi[u.half][:, k, :], lo_(k), start=False, stop=False,
                                  skip_group_check=True)
                    if k == nk - 1:
                        m.then_inc(s_wh, 1)
                    if slot is not None:
                        slot(k)
                pe.wait_ge(s_lo, u.n + 1)
                for k in range(nk):
                    m = pe.matmul(bank[:, 0:S], lo[u.half][:, k, :], hi_(k), start=False, stop=stop and k == nk - 1,
                                  skip_group_check=True)
                m.then_inc(s_unit, 1)
                if slot is not None:
                    slot(nk)

            def x_unit(u, t, norm=None, slot=None):
                after(pe, s_free, t.n - 3)

                def ready(k):
                    if norm is not None and k % 4 == 0:
                        sum_squares(norm, k // 4)
                        pe.wait_ge(s_xlo, 4 * norm + k // 4 + 1)

                def spread(k):
                    if k == KD:
                        pe.wait_ge(s_col, norm + 1)
                        pe.matmul(aux[0][:, 0:S], ones, diag[1], start=True, stop=True).then_inc(s_bc, 1)

                passes(u, lin[t.bank], lambda k: xhl[:, k, 0, :], lambda k: xhl[:, k, 1, :], KD, True, True,
                       ready=ready, slot=slot if norm is None else spread)

            def sum_squares(norm, q):
                pe.wait_ge(s_sq4, 4 * norm + q + 1)
                for c in range(4):
                    for t in range(TT):
                        m = pe.matmul(aux[0][:, t:t + 1], sq4[q % 2][:, c, t * P:(t + 1) * P], ones[:, 0:1],
                                      start=q == 0 and c == 0 and t == 0, stop=q == 3 and c == 3,
                                      skip_group_check=True)
                m.then_inc(s_nps, 1)

            pe.wait_ge(s_prm, 16)
            x_unit(Unit("ab", 0), Tile("ab", 0), norm=0)
            for j in range(4):
                x_unit(Unit("qkv", j), Tile("qkv", j))
            with pe.Fori(1, 6) as i:
                for j in range(4):
                    x_unit(Unit("qkv", j, i), Tile("qkv", j, i))
            pe.wait_ge(g["ab"], 1)
            for t in range(TT):
                m = pe.transpose(aux[t][:, 0:P], R[:, t * P:(t + 1) * P], ident)
            m.then_inc(g["rt"], 1)

            def mix(i):
                n = i + 1

                def spread():
                    pe.wait_ge(g["rs"], n)
                    for k in range(2):
                        pe.matmul(aux[k][:, :], ones, rs[:, k, :, :], start=True, stop=True).then_inc(g["bc"], 1)
                    pe.wait_ge(g["sq"], n)
                    for q in range(8):
                        m = pe.matmul(aux[2][:, q:q + 1], nr[:, q // 4, q // 2 % 2, (q % 2) * P:(q % 2 + 1) * P],
                                      ones[:, 0:1], start=True, stop=True, skip_group_check=True)
                    m.then_inc(g["ss"], 1)

                def norms():
                    pe.wait_ge(g["dq"], n)
                    for k in range(2):
                        m = pe.matmul(aux[2 + k][:, :], ones, dqk[:, 4 * k:4 * k + 4, :], start=True, stop=True)
                    m.then_inc(g["qb"], 1)

                def turn():
                    pe.wait_ge(g["kn"], n)
                    pe.wait_ge(g["vw"], n)
                    for q in range(4):
                        pe.transpose(aux[2][:, q * P:(q + 1) * P], kn[:, q // 2, (q % 2) * P:(q % 2 + 1) * P], ident)
                    for q in range(4):
                        m = pe.transpose(aux[3][:, q * P:(q + 1) * P], vw[:, q // 2, (q % 2) * P:(q % 2 + 1) * P], ident)
                    m.then_inc(g["tp"], 1)

                def grams():
                    pe.wait_ge(g["qg"], n)
                    for bank, rhs in ((aux[0], kb), (aux[1], qn)):
                        for q in range(4):
                            sl = slice((q % 2) * P, (q % 2 + 1) * P)
                            m = pe.matmul(bank[:, q * P:(q + 1) * P], kn[:, q // 2, sl], rhs[:, q // 2, sl],
                                          start=True, stop=True, skip_group_check=True)
                    m.then_inc(g["kk"], 1)

                def inv_a(l):
                    pe.wait_ge(g["nt"], i * LEVELS + l + 1)
                    if l == 0:
                        pe.wait_ge(g["xi"], n)
                        pe.wait_ge(g["vb"], n)
                    else:
                        pe.wait_ge(g["xp"], i * LEVELS + l)
                    for q in range(4):
                        m = pe.matmul(aux[2][:, q * P:(q + 1) * P], nt[l % 2][:, q, :], X[:, q, :],
                                      start=True, stop=True, skip_group_check=True)
                    m.then_inc(g["y"], 1)

                def inv_b(l):
                    pe.wait_ge(g["yb"], i * LEVELS + l + 1)
                    s_ = 1 << l
                    for q in range(4):
                        yq = yb_[:, q, :].rearrange("p (b h s) -> p b h s", h=2, s=s_)
                        pq = PT[:, q, :].rearrange("p (b h s) -> p b h s", h=2, s=s_)
                        pe.matmul(aux[3][:, q * 64:(q + 1) * 64], PT[:, q, :], yq[:, :, 0, :],
                                  start=True, stop=True, skip_group_check=True)
                        m = pe.matmul(aux[3][:, 256 + q * 64:256 + (q + 1) * 64], yb_[:, q, :], pq[:, :, 1, :],
                                      start=True, stop=True, skip_group_check=True)
                    m.then_inc(g["z"], 1)

                def first_v():
                    pe.wait_ge(g["xp"], (i + 1) * LEVELS)
                    pe.wait_ge(g["at"], n)
                    for h in range(2):
                        pe.matmul(aux[0][:, h * P:(h + 1) * P], PT[:, 2 * h, :], vb[:, 2 * h, :],
                                  start=True, stop=True, skip_group_check=True)
                        m = pe.matmul(aux[0][:, 256 + h * P:256 + (h + 1) * P], kbg[:, h, :], PT[:, 2 * h + 1, :],
                                      start=True, stop=True, skip_group_check=True)
                    m.then_inc(g["uw"], 1)

                def state():
                    pe.wait_ge(g["vn0"], n)
                    for h in range(2):
                        m = pe.matmul(aux[1][:, h * P:(h + 1) * P], kdec[:, h, :], vn0[:, h, :],
                                      start=True, stop=True, skip_group_check=True)
                    m.then_inc(g["s1"], 1)

                def second_v():
                    pe.wait_ge(g["s1c"], n)
                    for h in range(2):
                        pe.matmul(aux[2][:, h * P:(h + 1) * P], PT[:, 2 * h + 1, :], vb[:, 2 * h + 1, :],
                                  start=True, stop=False, skip_group_check=True)
                        m = pe.matmul(aux[2][:, h * P:(h + 1) * P], wt[:, h, :], s1[:, h, :],
                                      start=False, stop=True, skip_group_check=True)
                    m.then_inc(g["v1"], 1)

                def outputs():
                    pe.wait_ge(g["v1c"], n)
                    pe.wait_ge(g["qg"], n)
                    for h in range(2):
                        pe.matmul(aux[3][:, h * S:h * S + P], vn0[:, h, :], att[:, 2 * h, :],
                                  start=True, stop=True, skip_group_check=True)
                        pe.matmul(aux[3][:, h * S + P:(h + 1) * S], vn1[:, h, :], att[:, 2 * h + 1, :],
                                  start=True, stop=False, skip_group_check=True)
                        m = pe.matmul(aux[3][:, h * S + P:(h + 1) * S], s1[:, h, :], qg[:, h, :],
                                      start=False, stop=True, skip_group_check=True)
                    m.then_inc(g["o"], 1)

                def out_norm():
                    pe.wait_ge(g["oc"], n)
                    for q in range(4):
                        m = pe.matmul(aux[0][:, q:q + 1], osq[:, q // 2, (q % 2) * P:(q % 2 + 1) * P], ones[:, 0:1],
                                      start=True, stop=True, skip_group_check=True)
                    m.then_inc(g["on"], 1)

                def out_scale():
                    pe.wait_ge(g["do"], n)
                    pe.matmul(aux[0][:, :], ones, do_[:, :, :], start=True, stop=True).then_inc(g["ob"], 1)

                plan = {0: [spread], 1: [norms], 2: [turn], 3: [grams], 18: [first_v], 19: [state], 20: [second_v],
                        21: [outputs], 22: [out_norm], 23: [out_scale]}
                for l in range(LEVELS):
                    plan[4 + 2 * l] = [lambda l=l: inv_a(l)]
                    plan[5 + 2 * l] = [lambda l=l: inv_b(l)]
                for j in range(8):
                    x_unit(Unit("mix", j, i, 8), Tile("mix", j, i, 8),
                           slot=lambda k, j=j: [f() for f in plan.get(3 * j + {7: 0, 15: 1, 16: 2}.get(k, 99), [])])

            with pe.Fori(0, 4) as i:
                mix(i)

            def out_phase(phase):
                def tiles(i):
                    for j in range(4):
                        t = Tile(phase, j, i)
                        after(pe, s_free, t.n - 3)
                        passes(Unit(phase, j, i), lin[t.bank], lambda k: yhl[:, k, 0, :],
                               lambda k: yhl[:, k, 1, :], KD, True, True)
                pe.wait_ge(s_ylo, 12 if phase == "out0" else 28)
                with pe.Fori(0, 4) as i:
                    tiles(i)

            def up_phase(phase, norm):
                for j in range(4):
                    x_unit(Unit(phase, j), Tile(phase, j), norm=norm if j == 0 else None)
                with pe.Fori(1, 22) as i:
                    for j in range(4):
                        x_unit(Unit(phase, j, i), Tile(phase, j, i))

            def down_phase(phase, layer):
                pe.wait_ge(s_midlo, KF * (layer + 1))
                with pe.Fori(0, 8) as i:
                    for a in range(2):
                        t = Tile(phase, a, i, 2)
                        pe.wait_ge(s_free, t.n - 1)
                        for q in range(4):
                            passes(Unit(phase, 4 * a + q, i, 8), lin[t.bank],
                                   lambda k: mid[:, DN_K * q + k, 0, :], lambda k: mid[:, DN_K * q + k, 1, :],
                                   DN_K, q == 0, q == 3)

            def junction(j):
                pe.wait_ge(s_ssq, 17 * j)
                for t in range(TT):
                    m = pe.matmul(aux[1][:, t:t + 1], ssq[:, t * P:(t + 1) * P], ones[:, 0:1],
                                  start=True, stop=True, skip_group_check=True)
                m.then_inc(s_post, 1)
                pe.wait_ge(s_pbc2, j)
                pe.matmul(aux[1][:, 0:S], ones, diag[0], start=True, stop=True).then_inc(s_pbc, 1)

            out_phase("out0")
            junction(1)
            up_phase("gu0", 1)
            down_phase("dn0", 0)
            junction(2)

            x_unit(Unit("gate", 0), Tile("gate", 0), norm=2)

            def kv(i):
                for j in range(8):
                    x_unit(Unit("kv", j, i, 8), Tile("kv", j, i, 8))
                    if j == 0 and isinstance(i, int):
                        pe.wait_ge(s_free, T0["gate"] + 1)
                        for t in range(TT):
                            m = pe.transpose(aux[1][:, t * P:(t + 1) * P], gts[:, t * P:(t + 1) * P], ident)
                        m.then_inc(ns["gtp"], 1)
                    if j >= 5:
                        turn_v(i, j - 5)
                turn_v(i, 3)

            def turn_v(i, g_):
                pe.wait_ge(s_free, Tile("kv", 4 + g_, i, 8).n + 1)
                after(pe, ns["vk"], 4 * i + g_ - 1)
                for t in range(TT):
                    m = pe.transpose(aux[2 + g_ % 2][:, t * P:(t + 1) * P], vst[:, g_, t * P:(t + 1) * P], ident)
                m.then_inc(ns["vk_"], 1)

            kv(0)
            with pe.Fori(1, 3) as i:
                kv(i)
            for kind in range(2):
                pe.wait_ge(ns["xcl"], kind + 1)
                for ht in range(2):
                    t = Tile("cmp", 2 * kind + ht)
                    pe.wait_ge(s_free, t.n - 3)
                    for q in range(2):
                        u = Unit("cmp", 4 * kind + 2 * ht + q)
                        pe.wait_ge(s_hi, u.n + 1)
                        for k in range(KD):
                            m = pe.matmul(lin[t.bank][:, 0:2 * CW], hi[u.half][:, k, :], xc[kind][:, 16 * q + k, :, :],
                                          start=q == 0 and k == 0, stop=False, skip_group_check=True)
                        m.then_inc(s_wh, 1)
                        pe.wait_ge(s_lo, u.n + 1)
                        for k in range(KD):
                            m = pe.matmul(lin[t.bank][:, 0:CW], lo[u.half][:, k, :], xc[kind][:, 16 * q + k, 0, :],
                                          start=False, stop=q == 1 and k == KD - 1, skip_group_check=True)
                        m.then_inc(s_unit, 1)
            def compressed():
                pe.wait_ge(ns["h1"], 2)
                for ht in range(2):
                    pe.matmul(aux[0][:, 0:CW], C1["w2k"].rearrange("p (a d) -> p a d", a=2)[:, ht, :],
                              h1[:, ht, :], start=ht == 0, stop=ht == 1)
                for g_ in range(NG):
                    for ht in range(2):
                        m = pe.matmul(aux[1][0:WINS, g_ * P:(g_ + 1) * P], h1[:, 2 + ht, g_ * WINS:(g_ + 1) * WINS],
                                      C1["w2v"].rearrange("p (a d) -> p a d", a=2)[:, ht, :],
                                      start=ht == 0, stop=ht == 1, skip_group_check=True)
                m.then_inc(ns["k2"], 1)
                pe.wait_ge(ns["kc"], 1)

            def scores(h, g_, r):
                pe.wait_ge(ns["rope"], 12 + h + 1)
                after(pe, ns["mx"], h)
                for t in range(TT):
                    pe.matmul(aux[0][:, S + 16 * t:S + 16 * t + WINS], qs[:, r, t * P:(t + 1) * P], kc_[:, g_, :],
                              start=True, stop=True, skip_group_check=True)
                pe.matmul(aux[0][:, 0:S], qs[:, r, 0:P], kt[:, 1:3, g_, 0:P], start=True, stop=True,
                          skip_group_check=True)
                pe.matmul(aux[1][:, :], qs[:, r, P:S], kt[:, 1:3, g_, :], start=True, stop=True).then_inc(ns["sc"], 1)

            def turn_p(h):
                pe.wait_ge(ns["p"], h + 1)
                after(pe, ns["pta"], h)
                for b in range(2):
                    pe.transpose(aux[2][:, b * P:(b + 1) * P], sm0[:, b, :], ident)
                for t in range(TT):
                    pe.transpose(aux[2][0:WINS, (2 + t) * P:(3 + t) * P], smc[:, t, 0:WINS], ident)
                for b in range(2):
                    for k in range(2):
                        m = pe.transpose(aux[3][:, (2 * b + k) * P:(2 * b + k + 1) * P], sm1[:, b, k * P:(k + 1) * P],
                                         ident)
                m.then_inc(ns["tp"], 1)

            def values(h, g_, r):
                pe.wait_ge(ns["pta"], h + 1)
                pe.wait_ge(ns["cp"], g_ + 1)
                after(pe, ns["oc"], h - 1)
                o_ = lin[2 + r % 2]
                for b in range(2):
                    pe.matmul(o_[:, 0:S], vs[:, b, 0, :], pt[:, b, 0:S], start=b == 0, stop=False, skip_group_check=True)
                    pe.matmul(o_[:, P:S], vs[:, b, 1, :], pt[:, b, S:S + P], start=False, stop=False,
                              skip_group_check=True)
                pe.matmul(o_[:, 0:S], vcs[0:WINS, :], ptc[0:WINS, :], start=False, stop=True,
                          skip_group_check=True).then_inc(ns["pv"], 1)

            def queries(i):
                for j in range(4):
                    def slot(k, j=j):
                        if k == 3 and (j > 1 or not isinstance(i, int)):
                            turn_p(4 * i + j - 2)
                        if k == 8 and (j > 0 or not isinstance(i, int)):
                            scores(4 * i + j - 1, i if j > 0 else i - 1, (j - 1) % 4)
                        if k == 13 and (j > 1 or not isinstance(i, int)):
                            values(4 * i + j - 2, i if j > 1 else i - 1, (j - 2) % 4)
                    t = Tile("q", j, i, bank=j % 2)
                    pe.wait_ge(s_free, t.n - 1)
                    passes(Unit("q", j, i), lin[t.bank], lambda k: xhl[:, k, 0, :], lambda k: xhl[:, k, 1, :],
                           KD, True, True, slot=slot)
                    if j == 0 and isinstance(i, int):
                        compressed()

            queries(0)
            with pe.Fori(1, 4) as i:
                queries(i)
            scores(15, 3, 3)
            turn_p(14)
            values(14, 3, 2)
            turn_p(15)
            values(15, 3, 3)
            out_phase("out1")
            junction(3)
            up_phase("gu1", 3)
            down_phase("dn1", 1)
            junction(4)

        @block.scalar
        def _(act):
            def split(u, nk=KD, lo_done=True):
                act.wait_ge(s_w[u.raw], u.loads)
                after(act, s_wh, u.n - 1)
                after(act, s_lo, u.n - 1)
                act.activation(hi[u.half][:, 0:nk, :], raw[u.raw][:, 0:nk, :], ACT.Copy).then_inc(s_hi, 1)

            def norm(nn, group):
                w = normw[:, 2 * nn, :]
                for q in range(4):
                    group(q)
                    for c in range(4 * q, 4 * q + 4):
                        m = act.activation(xhl[:, c, 0, :], hnew[:, c, :], ACT.Copy, scale=w[:, c:c + 1])
                    m.then_inc(s_xhi, 1)
                    after(act, s_nps, 4 * nn + q - 1)
                    act.activation(sq4[q % 2][:, :, :], hnew[:, 4 * q:4 * q + 4, :], ACT.Square).then_inc(s_sq4, 1)
                act.wait_ge(s_nps, 4 * nn + 4)
                act.activation(tiny[:, 0:2], aux[0][:, 0:2], ACT.Sqrt, bias=eps, scale=1.0 / D).then_inc(s_root, 1)

            def factors(nn):
                act.wait_ge(s_bc, nn + 1)
                act.activation(rstd[:, :], aux[0][:, 0:S], ACT.Copy).then_inc(s_rs, 1)

            act.wait_ge(s_prm, 16)
            split(Unit("ab", 0))
            norm(0, lambda q: act.wait_ge(s_x[q], 16))
            split(Unit("ab", 1))
            factors(0)
            split(Unit("ab", 2))

            def qkv_tiles(i):
                for j in range(4):
                    split(Unit("qkv", j + 2, i))
                    c = i * 4 + j
                    act.wait_ge(s_conv, c + 1)
                    act.activation(qkv[:, :, :, :, :].rearrange("p a b c t -> p (a b c) t")[:, c, :],
                                   cv[j % 2][:, :], ACT.Silu).then_inc(s_silu, 1)

            qkv_tiles(0)
            with act.Fori(1, 6) as i:
                qkv_tiles(i)

            act.wait_ge(g["hb"], 1)
            a0, a1, a2, a3, a4 = [x[0:8, :] for x in at4[0:5]]
            r = a_.mark(act.activation(a1, a0, ACT.Abs))
            act.wait_ge(a_.sem, r)
            r = a_.mark(act.activation(a1, a1, ACT.Exp, scale=-1.0))
            r = a_.mark(act.activation(R[32:40, :], abf[32:40, :], ACT.Exp, scale=-1.0))
            r = a_.mark(act.activation(tiny[0:8, 0:1], alog[0:8, :], ACT.Exp))
            act.wait_ge(a_.sem, r)
            act.activation(a2, a1, ACT.Ln, bias=1.0).then_inc(g["eg"], 1)
            act.wait_ge(g["kd"], 1)
            act.activation(tiny[:, 40:48], tiny[:, 24:32], ACT.Exp).then_inc(g["kd"], 1)

            def mix(i):
                n = i + 1
                act.activation(nr[:, 0, :, :], qkv[:, 0, i, :, :], ACT.Square)
                act.activation(nr[:, 1, :, :], qkv[:, 1, i, :, :], ACT.Square).then_inc(g["sq"], 1)
                act.activation(vw[:, :, :], qkv[:, 2, i, :, :], ACT.Copy).then_inc(g["vw"], 1)

                def spread():
                    act.wait_ge(g["bc"], 2 * n)
                    act.activation(bc[:, 0, :, :], aux[0][:, :], ACT.Copy)
                    act.activation(bc[:, 1, :, :], aux[1][:, :], ACT.Copy).then_inc(g["bcc"], 1)
                    act.wait_ge(g["ss"], n)
                    act.activation(tiny[:, 64:72], aux[2][:, 0:8], ACT.Sqrt, bias=eps).then_inc(g["nr"], 1)

                def exps():
                    act.wait_ge(g["dt"], n)
                    act.activation(dt_[:, :, :], dt_[:, :, :], ACT.Exp).then_inc(g["de"], 1)
                    act.activation(eg[:, :, :], bc[:, 0, :, P:S], ACT.Exp)
                    act.activation(tiny[:, 50:52], tiny[:, 48:50], ACT.Exp).then_inc(g["eg"], 1)

                def zsilu():
                    act.wait_ge(s_free, Tile("mix", 1, i, 8).n + 1)
                    act.activation(zs[:, :, :], zs[:, :, :], ACT.Silu).then_inc(g["zs2"], 1)

                def yev(l):
                    if l == 0:
                        act.wait_ge(g["at"], n)
                    act.wait_ge(g["y"], i * LEVELS + l + 1)
                    act.activation(yb_[:, :, :], aux[2][:, :], ACT.Copy).then_inc(g["yb"], 1)

                def v0():
                    act.wait_ge(g["uw"], n)
                    act.activation(vn0[:, :, :], aux[0][:, 0:256], ACT.Copy)
                    act.activation(wt[:, :, :], aux[0][:, 256:512], ACT.Copy, scale=-1.0).then_inc(g["vn0"], 1)

                def s1c():
                    act.wait_ge(g["s1"], n)
                    act.activation(s1[:, :, :], aux[1][:, 0:256], ACT.Copy).then_inc(g["s1c"], 1)

                def v1():
                    act.wait_ge(g["v1"], n)
                    act.activation(vn1[:, :, :], aux[2][:, 0:256], ACT.Copy).then_inc(g["v1c"], 1)

                def oev():
                    act.wait_ge(g["o"], n)
                    act.activation(ot[:, :, :], aux[3][:, :], ACT.Copy)
                    act.activation(osq[:, :, :], aux[3][:, :], ACT.Square).then_inc(g["oc"], 1)

                def oroot():
                    act.wait_ge(g["on"], n)
                    act.activation(tiny[:, 72:76], aux[0][:, 0:4], ACT.Sqrt, bias=eps, scale=1.0 / P).then_inc(g["orn"], 1)

                def high(a):
                    act.wait_ge(s_yf, 3 * i + a + 1)
                    act.activation(y4[:, i + 4, a, 0, :], cv[a][:, :], ACT.Copy).then_inc(s_yhi, 1)

                plan = {0: [spread, exps], 8: [zsilu], 18: [v0], 19: [s1c], 20: [v1], 21: [oev], 22: [oroot],
                        16: [lambda: high(0)]}
                for l in range(LEVELS):
                    plan.setdefault(4 + 2 * l, []).append(lambda l=l: yev(l))
                for j in range(8):
                    for s_ in range(3):
                        for f in plan.get(3 * j + s_, []):
                            f()
                    split(Unit("mix", j + 2, i, 8))
                high(1)
                act.wait_ge(s_yf, 3 * i + 3)
                act.activation(y4[:, i, :, 0, :], ot[:, :, :], ACT.Copy).then_inc(s_yhi, 1)

            y4 = yhl[:, :, :, :].rearrange("p (i a) l t -> p i a l t", a=2)
            n_last = 4
            with act.Fori(0, n_last) as i:
                mix(i)

            def look(phase, j, i=0, per=4):
                if isinstance(i, int):
                    off = U0[phase] + j + per * i + 2
                    if off >= UNITS:
                        return
                    nk = DN_K if any(U0[x] <= off < U0[x] + N_UNITS[x] for x in ("dn0", "dn1")) else KD
                else:
                    nk = DN_K if phase[:2] == "dn" else KD
                split(Unit(phase, j + 2, i, per), nk)

            def take_out(t, u, m, j, b):
                act.wait_ge(s_unit, u.n + 1)
                act.wait_ge(s_ssq, 17 * (j - 1) + 1 + m)
                act.activation(sqd[b][:, :], lin[t.bank][:, 0:S], ACT.Square).then_inc(s_msq, 1)
                act.activation(mout[:, m, :], lin[t.bank][:, 0:S], ACT.Copy, scale=norm1[:, 2 * j - 1, m, :]).then_inc(s_free, 1)

            def out_phase(phase, jn):
                with act.Fori(0, 4) as i:
                    for j in range(4):
                        u, t = Unit(phase, j, i), Tile(phase, j, i)
                        take_out(t, u, 4 * i + j, jn, j % 2)
                        look(phase, j, i)

            def up_phase(phase, layer):
                def pairs(i):
                    for a in range(2):
                        c = 2 * i + a
                        look(phase, 2 * a, i)
                        act.wait_ge(s_conv, 24 + KF * layer + c + 1)
                        after(act, s_mid, KF * layer + c - 1)
                        act.activation(sil[a][:, :], cv[a][:, :], ACT.Silu).then_inc(s_silu, 1)
                        look(phase, 2 * a + 1, i)
                        act.wait_ge(s_mid, KF * layer + c + 1)
                        act.activation(mid[:, c, 0, :], mf[a][:, :], ACT.Copy).then_inc(s_midhi, 1)
                factors(2 * layer + 1)
                act.wait_ge(s_hstore, 16 * (2 * layer + 1))
                pairs(0)
                with act.Fori(1, 21) as i:
                    pairs(i)
                pairs(21)

            def down_phase(phase, jn):
                def tiles(i):
                    for a in range(2):
                        for q in range(4):
                            j = 4 * a + q
                            u, t = Unit(phase, j, i, 8), Tile(phase, a, i, 2)
                            if q == 3:
                                take_out(t, u, 2 * i + a, jn, a)
                            look(phase, j, i, 8)
                with act.Fori(0, 7) as i:
                    tiles(i)
                tiles(7)

            def junction(j):
                act.wait_ge(s_post, j)
                act.activation(tiny[:, 2:4], aux[1][:, 0:2], ACT.Sqrt, bias=eps, scale=1.0 / D).then_inc(s_root, 1)
                if j < 4:
                    norm(j, lambda q: act.wait_ge(s_hn, 4 * (j - 1) + q + 1))

            out_phase("out0", 1)
            junction(1)
            up_phase("gu0", 0)
            down_phase("dn0", 2)
            junction(2)

            factors(2)
            look("gate", 0)

            def swap(t, u, b):
                act.wait_ge(s_unit, u.n + 1)
                act.activation(up[b][0:64, :], lin[t.bank][64:128, 0:S], ACT.Copy)
                act.activation(up[b][64:128, :], lin[t.bank][0:64, 0:S], ACT.Copy).then_inc(ns["swap"], 1)

            def kv(i):
                for j in range(8):
                    if j < 4:
                        after(act, ns["rope"], 4 * i + j - 1)
                        swap(Tile("kv", j, i, 8), Unit("kv", j, i, 8), j % 2)
                    look("kv", j, i, 8)
                    if j >= 5:
                        out_v(i, j - 5)
                    if j == 0 and isinstance(i, int):
                        act.wait_ge(ns["gtp"], 1)
                        act.activation(sig[:, :, :, :].rearrange("p t b h -> p t (b h)"),
                                       aux[1][:, 0:S].rearrange("p (t c) -> p t c", t=TT)[:, :, 0:48],
                                       ACT.Exp, scale=-1.0).then_inc(ns["sg"], 1)
                out_v(i, 3)

            def out_v(i, g_):
                act.wait_ge(ns["vk_"], 4 * i + g_ + 1)
                act.activation(vk[:, i, g_, :, :], aux[2 + g_ % 2][:, 0:S], ACT.Copy).then_inc(ns["vk"], 1)

            kv(0)
            for kind in range(2):
                act.wait_ge(ns["xcw"], kind + 1)
                act.activation(xc[kind][:, :, 0, :], xct[:, :, :, :].rearrange("p l g c -> p l (g c)"),
                               ACT.Copy).then_inc(ns["xch"], 1)
            with act.Fori(1, 3) as i:
                kv(i)
            for kind in range(2):
                for ht in range(2):
                    for q in range(2):
                        j = 4 * kind + 2 * ht + q
                        if q == 1:
                            t = Tile("cmp", 2 * kind + ht)
                            act.wait_ge(s_unit, U0["cmp"] + j + 1)
                            act.activation(half[ht][:, :], lin[t.bank][:, CW:2 * CW], ACT.Copy).then_inc(s_half, 1)
                        look("cmp", j)
                act.wait_ge(s_free, T0["cmp"] + 2 * kind + 2)
                act.activation(h1[:, 2 * kind:2 * kind + 2, :], h1[:, 2 * kind:2 * kind + 2, :],
                               ACT.Gelu_apprx_tanh).then_inc(ns["h1"], 1)

            def query(j, i):
                act.wait_ge(ns["rope"], 12 + 4 * i + j - 1)
                swap(Tile("q", j, i, bank=j % 2), Unit("q", j, i), j % 2)

            def exps(h):
                act.wait_ge(ns["mx"], h + 1)
                for b in range(2):
                    act.activation(sm0[:, b, :], sm0[:, b, :], ACT.Exp, bias=soft[:, 8 + b:9 + b], scale=SCALE,
                                   accum_out=soft[:, 16 + b:17 + b])
                    act.activation(sm1[:, b, :], sm1[:, b, :], ACT.Exp, bias=soft[:, 10 + b:11 + b], scale=SCALE,
                                   accum_out=soft[:, 18 + b:19 + b])
                    m = act.activation(smc[:, b, 0:WINS], smc[:, b, 0:WINS], ACT.Exp, bias=soft[:, 12 + b:13 + b],
                                       scale=SCALE, accum_out=soft[:, 20 + b:21 + b])
                m.then_inc(ns["ex"], 1)

            def take_p(h):
                act.wait_ge(ns["tp"], h + 1)
                act.activation(pt[:, :, 0:P], aux[2][:, 0:S].rearrange("p (b t) -> p b t", b=2), ACT.Copy)
                act.activation(ptc[0:WINS, :], aux[2][0:WINS, S:2 * S], ACT.Copy)
                act.activation(pt[:, :, P:3 * P], aux[3][:, :].rearrange("p (b t) -> p b t", b=2),
                               ACT.Copy).then_inc(ns["pta"], 1)

            def take_o(h, r):
                act.wait_ge(ns["pv"], h + 1)
                after(act, s_ylo, 12 + h - 1)
                act.activation(of[r % 2][:, :], lin[2 + r % 2][:, 0:S], ACT.Copy)
                act.activation(yhl[:, h, 0, :], lin[2 + r % 2][:, 0:S], ACT.Copy).then_inc(ns["oc"], 1)

            def group(g_):
                after(act, ns["pv"], 4 * g_)
                act.activation(vs[:, :, :, :], vk[:, 1:3, g_, :, :], ACT.Copy)
                act.activation(vcs[0:WINS, :], vc_[0:WINS, g_, :], ACT.Copy).then_inc(ns["cp"], 1)

            def queries(i):
                for j in range(4):
                    if j > 1 or not isinstance(i, int):
                        take_p(4 * i + j - 2)
                    if j > 0 or not isinstance(i, int):
                        split(Unit("q", j + 1, i))
                        exps(4 * i + j - 1)
                    if j > 1 or not isinstance(i, int):
                        take_o(4 * i + j - 2, (j - 2) % 4)
                    if j == 1:
                        group(i)
                    query(j, i)
                    if j == 0 and isinstance(i, int):
                        act.wait_ge(ns["k2"], 1)
                        act.activation(kc_[:, :, :], aux[0][:, 0:CW], ACT.Copy)
                        act.activation(vc_[0:WINS, :, :], aux[1][0:WINS, :], ACT.Copy).then_inc(ns["kc"], 1)

            queries(0)
            with act.Fori(1, 4) as i:
                queries(i)
            exps(15)
            take_p(14)
            take_o(14, 2)
            split(Unit("q", 17))
            take_p(15)
            take_o(15, 3)
            out_phase("out1", 3)
            junction(3)
            up_phase("gu1", 1)
            down_phase("dn1", 4)
            junction(4)

        @block.vector
        def _(dve):
            def split(u, nk=KD):
                dve.wait_ge(s_hi, u.n + 1)
                after(dve, s_unit, u.n - 1)
                dve.tensor_tensor(lo[u.half][:, 0:nk, :], raw[u.raw][:, 0:nk, :],
                                  hi[u.half][:, 0:nk, :].bitcast(F32), ALU.subtract).then_inc(s_lo, 1)

            def take(u, t, dst, factor):
                dve.wait_ge(s_unit, u.n + 1)
                dve.tensor_tensor(dst, lin[t.bank][:, 0:S], factor, ALU.mult).then_inc(s_free, 1)
                dve.wait_ge(s_free, t.n + 1)

            def step(ins):
                dve.wait_ge(v_.sem, v_.mark(ins))

            def norm_low(nn, q):
                w = normw[:, 2 * nn, :]
                dve.wait_ge(s_xhi, 4 * nn + q + 1)
                for c in range(4 * q, 4 * q + 4):
                    ins = dve.scalar_tensor_tensor(xhl[:, c, 1, :], hnew[:, c, :], w[:, c:c + 1],
                                                   xhl[:, c, 0, :].bitcast(F32), ALU.mult, ALU.subtract)
                ins.then_inc(s_xlo, 1)

            def diagonal(cols, dst, roots, count, done):
                dve.wait_ge(roots, count)
                step(dve.reciprocal(cols, cols))
                for t in range(dst.shape[1]):
                    ins = dve.tensor_scalar(dst[:, t, :], ident, cols[:, t:t + 1], None, ALU.mult)
                ins.then_inc(done, 1)

            for b in range(2):
                dve.memset(cbuf[b][:, :], 0.0)
            step(dve.memset(R[:, :], 0.0))
            dve.wait_ge(s_prm, 16)
            for q in range(4):
                dve.wait_ge(s_x[q], 16)
                norm_low(0, q)
                if q == 0:
                    split(Unit("ab", 0))
            diagonal(tiny[:, 0:2], diag[1], s_root, 1, s_col)
            split(Unit("ab", 1))
            dve.wait_ge(s_rs, 1)
            take(Unit("ab", 0), Tile("ab", 0), abf[:, :], rstd[:, :])
            step(dve.tensor_tensor(sqd[0][:, :], rstd[:, :], rstd[:, :], ALU.mult))
            split(Unit("ab", 2))

            def conv(dst, src, w, taps, last):
                step(dve.tensor_scalar(dst, src[:, 0:S], w(0), None, ALU.mult))
                for k in range(1, taps):
                    ins = dve.scalar_tensor_tensor(dst, src[:, k:k + S], w(k), dst, ALU.mult, ALU.add)
                    if k < taps - 1:
                        step(ins)
                    elif last is not None:
                        ins.then_inc(last, 1)
                    else:
                        step(ins)

            def qkv_tiles(i):
                for j in range(4):
                    t = Tile("qkv", j, i)
                    c = i * 4 + j
                    take(Unit("qkv", j, i), t, cbuf[j % 2][:, 3:3 + S], rstd[:, :])
                    after(dve, s_silu, c - 1)
                    conv(cv[j % 2][:, :], cbuf[j % 2], lambda k: gconv[:, c, k:k + 1], 4, s_conv)
                    split(Unit("qkv", j + 2, i))

            qkv_tiles(0)
            with dve.Fori(1, 6) as i:
                v_.enter(i, 12, first=1)
                qkv_tiles(i)
                v_.leave(6)

            a0, a1, a2, a3, a4 = [x[0:8, :] for x in at4[0:5]]
            dve.tensor_scalar(a0, abf[0:8, :], dtb[0:8, :], None, ALU.add).then_inc(g["hb"], 1)
            dve.memset(ones256[:, :], 1.0)
            dve.wait_ge(g["eg"], 1)
            step(dve.tensor_scalar(a3, a1, 1.0, None, ALU.add))
            step(dve.scalar_tensor_tensor(a4, a3, -1.0, a1, ALU.add, ALU.subtract))
            step(dve.reciprocal(a3, a3))
            step(dve.tensor_tensor(a4, a4, a3, ALU.mult))
            step(dve.tensor_tensor(a2, a2, a4, ALU.subtract))
            step(dve.scalar_tensor_tensor(a2, a0, 0.0, a2, ALU.max, ALU.add))
            step(dve.tensor_scalar(a2, a2, tiny[0:8, 0:1], -1.0, ALU.mult, ALU.mult))
            for t in range(TT):
                sl = slice(t * P, (t + 1) * P)
                step(dve.tensor_tensor_scan(R[0:8, sl], ones256[0:8, sl], a2[:, sl], 0.0, ALU.mult, ALU.add))
            step(dve.tensor_scalar(R[32:40, :], R[32:40, :], 1.0, None, ALU.add))
            dve.reciprocal(R[32:40, :], R[32:40, :]).then_inc(g["ab"], 1)
            dve.wait_ge(g["rt"], 1)
            dve.tensor_copy(tiny[:, 8:16], aux[0][:, 0:8])
            dve.tensor_copy(tiny[:, 16:24], aux[1][:, 0:8])
            dve.tensor_copy(tiny[:, 24:32], aux[1][:, 0:8]).then_inc(g["kd"], 1)
            dve.tensor_copy(tiny[:, 52:60], aux[0][:, 32:40])
            step(dve.tensor_copy(tiny[:, 32:40], aux[1][:, 32:40]))
            dve.wait_ge(g["kd"], 2)
            step(dve.tensor_tensor(tiny[:, 40:48], tiny[:, 40:48], tiny[:, 32:40], ALU.mult))

            gcol = tiny[:, 8:24].rearrange("p (t i a) -> p t i a", t=2, a=2)
            bcol = [tiny[:, 52:60].rearrange("p (i a) -> p i a", a=2), tiny[:, 32:40].rearrange("p (i a) -> p i a", a=2)]
            bge = tiny[:, 40:48].rearrange("p (i a) -> p i a", a=2)
            y4 = yhl[:, :, :, :].rearrange("p (i a) l t -> p i a l t", a=2)

            def mix(i):
                n = i + 1
                for k in range(2):
                    for h in range(2):
                        ins = dve.tensor_scalar(rs[:, k, h, :], R[:, :], onehot[:, i, h, k:k + 1], None, ALU.mult)
                ins.then_inc(g["rs"], 1)

                def qk_norm():
                    dve.wait_ge(g["bcc"], n)
                    diagonal(tiny[:, 64:72], dqk, g["nr"], n, g["dq"])
                    for t in range(2):
                        for h in range(2):
                            dve.tensor_scalar(dt_[:, 2 * h + t, :], bc[:, 0, h, t * P:(t + 1) * P],
                                              gcol[:, t, i, h:h + 1], 0.0, ALU.subtract, ALU.min)
                    for h in range(2):
                        ins = dve.tensor_scalar(tiny[:, 48 + h:49 + h], bc[:, 0, h, P - 1:P],
                                                gcol[:, 0, i, h:h + 1], None, ALU.subtract)
                    ins.then_inc(g["dt"], 1)
                    dve.wait_ge(g["qb"], n)
                    dve.scalar_tensor_tensor(qn[:, :, :], qkv[:, 0, i, :, :], SCALE,
                                             aux[2][:, :].rearrange("p (h t) -> p h t", h=2), ALU.mult, ALU.mult)
                    dve.tensor_tensor(kn[:, :, :], qkv[:, 1, i, :, :], aux[3][:, :].rearrange("p (h t) -> p h t", h=2),
                                      ALU.mult).then_inc(g["kn"], 1)
                    dve.wait_ge(g["kn"], n)
                    dve.tensor_tensor(kb[:, :, :], kn[:, :, :], bc[:, 1, :, :], ALU.mult).then_inc(g["kb"], 1)
                    dve.wait_ge(g["eg"], n + 1)
                    dve.tensor_tensor(qg[:, :, :], qn[:, :, P:S], eg[:, :, :], ALU.mult).then_inc(g["qg"], 1)

                def vbs():
                    dve.wait_ge(g["tp"], n)
                    for h in range(2):
                        for t in range(2):
                            q = 2 * h + t
                            dve.tensor_scalar(vb[:, q, :], aux[3][:, q * P:(q + 1) * P], bcol[t][:, i, h:h + 1],
                                              None, ALU.mult)
                        dve.tensor_scalar(kdec[:, h, :], aux[2][:, 2 * h * P:(2 * h + 1) * P],
                                          tiny[:, 50 + h:51 + h], None, ALU.mult)
                        ins = dve.tensor_scalar(kbg[:, h, :], aux[2][:, (2 * h + 1) * P:(2 * h + 2) * P],
                                                bge[:, i, h:h + 1], None, ALU.mult)
                    ins.then_inc(g["vb"], 1)

                def masks():
                    dve.wait_ge(g["kk"], n)
                    dve.wait_ge(g["dm"], n)
                    dve.tensor_tensor(lt[:, :, :], aux[0][:, :].rearrange("p (q j) -> p q j", q=4), dt_[:, :, :],
                                      ALU.mult).then_inc(g["lt"], 1)
                    dve.tensor_tensor(att[:, :, :], aux[1][:, :].rearrange("p (q j) -> p q j", q=4), dt_[:, :, :],
                                      ALU.mult).then_inc(g["at"], 1)

                def inv(l):
                    dve.wait_ge(g["z"], i * LEVELS + l + 1)
                    s_ = 1 << l
                    for k, m in ((0, X), (1, PT)):
                        v = m[:, :, :].rearrange("p q (b h s) -> p (q b) h s", h=2, s=s_)[:, :, k, :]
                        z = aux[3][:, 256 * k:256 * (k + 1)].rearrange("p (b s) -> p b s", s=s_)
                        ins = dve.tensor_tensor(v, v, z, ALU.subtract)
                    ins.then_inc(g["xp"], 1)

                def out_diag():
                    diagonal(tiny[:, 72:76], do_, g["orn"], n, g["do"])

                def low(a):
                    dve.wait_ge(s_yhi, 3 * i + a + 1)
                    dve.tensor_tensor(y4[:, i + 4, a, 1, :], cv[a][:, :], y4[:, i + 4, a, 0, :].bitcast(F32),
                                      ALU.subtract).then_inc(s_ylo, 1)

                plan = {1: [qk_norm], 2: [vbs], 3: [masks], 17: [lambda: low(0)], 22: [out_diag]}
                for l in range(LEVELS):
                    plan.setdefault(5 + 2 * l, []).append(lambda l=l: inv(l))
                for j in range(8):
                    for s_ in range(3):
                        for f in plan.get(3 * j + s_, []):
                            f()
                    u, t = Unit("mix", j, i, 8), Tile("mix", j, i, 8)
                    a, w = (j - 2) // 3, (j - 2) % 3
                    if j < 2:
                        take(u, t, zs[:, j, :], rstd[:, :])
                    elif w == 0:
                        take(u, t, up[0][:, :], sqd[0][:, :])
                    elif w == 1:
                        take(u, t, cbuf[a][:, 3:3 + S], up[0][:, :])
                        conv(cv[a][:, :], cbuf[a][:, 1:3 + S], lambda k: sconv[:, i, a, k:k + 1], 3, None)
                    else:
                        take(u, t, up[0][:, :], rstd[:, :])
                        dve.tensor_tensor(cv[a][:, :], cv[a][:, :], up[0][:, :], ALU.mult).then_inc(s_yf, 1)
                    split(Unit("mix", j + 2, i, 8))
                low(1)
                dve.wait_ge(g["ob"], n)
                dve.wait_ge(g["zs2"], n)
                step(dve.scalar_tensor_tensor(ot[:, :, :], ot[:, :, :], gnorm,
                                              aux[0][:, :].rearrange("p (h t) -> p h t", h=2), ALU.mult, ALU.mult))
                dve.tensor_tensor(ot[:, :, :], ot[:, :, :], zs[:, :, :], ALU.mult).then_inc(s_yf, 1)
                dve.wait_ge(s_yhi, 3 * i + 3)
                dve.tensor_tensor(y4[:, i, :, 1, :], ot[:, :, :], y4[:, i, :, 0, :].bitcast(F32),
                                  ALU.subtract).then_inc(s_ylo, 1)

            MIX_STEPS = 9
            with dve.Fori(0, 4) as i:
                v_.enter(i, MIX_STEPS)
                mix(i)
                v_.leave(4)

            def look(phase, j, i=0, per=4):
                if isinstance(i, int):
                    off = U0[phase] + j + per * i + 2
                    if off >= UNITS:
                        return
                    nk = DN_K if any(U0[x] <= off < U0[x] + N_UNITS[x] for x in ("dn0", "dn1")) else KD
                else:
                    nk = DN_K if phase[:2] == "dn" else KD
                split(Unit(phase, j + 2, i, per), nk)

            def add_square(m, j, b):
                dve.wait_ge(s_msq, 16 * (j - 1) + m + 1)
                dve.wait_ge(s_ssq, 17 * (j - 1) + 1 + m)
                dve.tensor_tensor(ssq[:, :], ssq[:, :], sqd[b][:, :], ALU.add).then_inc(s_ssq, 1)

            def out_phase(phase, jn):
                dve.memset(ssq[:, :], 0.0).then_inc(s_ssq, 1)
                with dve.Fori(0, 4) as i:
                    for j in range(4):
                        add_square(4 * i + j, jn, j % 2)
                        look(phase, j, i)

            def up_phase(phase, layer):
                def pairs(i):
                    for a in range(2):
                        c = 2 * i + a
                        take(Unit(phase, 2 * a, i), Tile(phase, 2 * a, i), cbuf[a][:, 3:3 + S], rstd[:, :])
                        dve.wait_ge(s_silu, 24 + KF * layer + c - 1)
                        conv(cv[a][:, :], cbuf[a][:, 1:3 + S], lambda k: fconv[:, layer, c, k:k + 1], 3, s_conv)
                        look(phase, 2 * a, i)
                        take(Unit(phase, 2 * a + 1, i), Tile(phase, 2 * a + 1, i), up[a][:, :], rstd[:, :])
                        dve.wait_ge(s_silu, 24 + KF * layer + c + 1)
                        after(dve, s_midhi, KF * layer + c - 1)
                        dve.tensor_tensor(mf[a][:, :], sil[a][:, :], up[a][:, :], ALU.mult).then_inc(s_mid, 1)
                        look(phase, 2 * a + 1, i)
                        dve.wait_ge(s_midhi, KF * layer + c + 1)
                        dve.tensor_tensor(mid[:, c, 1, :], mf[a][:, :], mid[:, c, 0, :].bitcast(F32),
                                          ALU.subtract).then_inc(s_midlo, 1)
                dve.wait_ge(s_rs, 2 * layer + 2)
                pairs(0)
                with dve.Fori(1, 21) as i:
                    v_.enter(i, 4, first=1)
                    pairs(i)
                    v_.leave(21)
                pairs(21)

            def down_phase(phase, jn):
                dve.memset(ssq[:, :], 0.0).then_inc(s_ssq, 1)
                def tiles(i):
                    for a in range(2):
                        for q in range(4):
                            if q == 3:
                                add_square(2 * i + a, jn, a)
                            look(phase, 4 * a + q, i, 8)
                with dve.Fori(0, 7) as i:
                    tiles(i)
                tiles(7)

            def junction(j, last):
                diagonal(tiny[:, 2:4], diag[0], s_root, 2 * j, s_pbc2)
                dve.wait_ge(s_pbc, j)
                dve.wait_ge(s_hload, 16 * j)
                dve.wait_ge(s_free, T0[last] + 16)

                def add(q):
                    m4 = mout[:, 4 * q:4 * q + 4, :]
                    step(dve.tensor_tensor(m4, m4, aux[1][:, 0:S].unsqueeze(1).broadcast_to([P, 4, S]), ALU.mult))
                    dve.tensor_tensor(hnew[:, 4 * q:4 * q + 4, :], m4, hold[:, 4 * q:4 * q + 4, :],
                                      ALU.add).then_inc(s_hn, 1)

                for q in range(5):
                    if q < 4:
                        add(q)
                    if q > 0 and j < 4:
                        norm_low(j, q - 1)
                if j < 4:
                    diagonal(tiny[:, 0:2], diag[1], s_root, 2 * j + 1, s_col)

            out_phase("out0", 1)
            junction(1, "out0")
            up_phase("gu0", 0)
            down_phase("dn0", 2)
            junction(2, "dn0")

            dve.wait_ge(s_hstore, 32)
            dve.wait_ge(s_l1c, 16)
            dve.wait_ge(s_rs, 3)
            take(Unit("gate", 0), Tile("gate", 0), gts[:, :], rstd[:, :])
            for name in ("cos", "sin"):
                ins = dve.tensor_tensor(C1[name], C1[name], rstd[:, :], ALU.mult)
            step(ins)
            look("gate", 0)

            def rotary(u, t, b, dst, count):
                dve.wait_ge(ns["swap"], count)
                take(u, t, cv[b][:, :], C1["cos"])
                step(dve.tensor_tensor(up[b][:, :], up[b][:, :], C1["sin"], ALU.mult))
                dve.tensor_tensor(dst, cv[b][:, :], up[b][:, :], ALU.add).then_inc(ns["rope"], 1)

            def kv(i):
                for j in range(8):
                    u, t = Unit("kv", j, i, 8), Tile("kv", j, i, 8)
                    if j < 4:
                        rotary(u, t, j % 2, kt[:, i, j, :], 4 * i + j + 1)
                    else:
                        after(dve, ns["vk_"], 4 * (i - 1) + j - 3)
                        take(u, t, vst[:, j - 4, :], rstd[:, :])
                    look("kv", j, i, 8)
                    if j == 0 and isinstance(i, int):
                        dve.wait_ge(ns["sg"], 1)
                        sg = sig[:, :, :, :].rearrange("p t b h -> p (t b h)")
                        step(dve.tensor_scalar(sg, sg, 1.0, None, ALU.add))
                        step(dve.reciprocal(sg, sg))
                        for t_ in range(TT):
                            dve.tensor_copy(gt[:, :, 2 * t_:2 * t_ + 2], sig[:, t_, 1:3, :].rearrange("p b h -> p h b"))
                            ins = dve.tensor_copy(gt[:, :, 4 + t_:5 + t_], sig[:, t_, 0:1, :].rearrange("p b h -> p h b"))
                        step(ins)

            kv(0)
            for kind in range(2):
                pos = C1["posv" if kind else "posk"].rearrange("p (a b) -> p a b", a=2)
                src = (vst[:, :, :] if kind else kt[:, 0, :, :]).rearrange("p g (w b) -> p g w b", b=16)
                dve.wait_ge(ns["rope"], 4)
                if kind:
                    dve.wait_ge(ns["xcl"], 1)
                for a in range(2):
                    ins = dve.tensor_tensor(xct[:, 16 * a:16 * a + 16, :, :],
                                            src[:, :, a:a + WINS, :].rearrange("p g w b -> p b g w"),
                                            pos[:, a, :].unsqueeze(2).unsqueeze(3).broadcast_to([P, 16, NG, WINS]),
                                            ALU.add)
                ins.then_inc(ns["xcw"], 1)
                dve.wait_ge(ns["xch"], kind + 1)
                dve.tensor_tensor(xc[kind][:, :, 1, :], xct[:, :, :, :].rearrange("p l g c -> p l (g c)"),
                                  xc[kind][:, :, 0, :].bitcast(F32), ALU.subtract).then_inc(ns["xcl"], 1)
            with dve.Fori(1, 3) as i:
                v_.enter(i, 4, first=1)
                kv(i)
                v_.leave(3)
            for kind in range(2):
                for ht in range(2):
                    for q in range(2):
                        if q == 1:
                            t = Tile("cmp", 2 * kind + ht)
                            dve.wait_ge(s_half, 2 * kind + ht + 1)
                            dve.tensor_tensor(h1[:, 2 * kind + ht, :], lin[t.bank][:, 0:CW], half[ht][:, :],
                                              ALU.add).then_inc(s_free, 1)
                        look("cmp", 4 * kind + 2 * ht + q)

            def query(j, i):
                after(dve, ns["sc"], 4 * (i - 1) + j + 1)
                rotary(Unit("q", j, i), Tile("q", j, i, bank=j % 2), j % 2, qs[:, j, :], 12 + 4 * i + j + 1)

            def maxima(h):
                dve.wait_ge(ns["sc"], h + 1)
                after(dve, ns["tp"], h)
                dve.tensor_tensor(smc[:, :, 0:WINS], aux[0][:, S:S + 32].rearrange("p (t c) -> p t c", t=2)[:, :, 0:WINS],
                                  C1["cmask"].rearrange("p (t c) -> p t c", t=2), ALU.add)
                dve.tensor_tensor(sm0[:, :, :], aux[0][:, 0:S].rearrange("p (b k) -> p b k", b=2),
                                  C1["causal"][:, P:S].unsqueeze(1).broadcast_to([P, 2, P]), ALU.add)
                step(dve.tensor_tensor(sm1[:, :, :], aux[1][:, :].rearrange("p (b k) -> p b k", b=2),
                                       C1["causal"][:, 0:S].unsqueeze(1).broadcast_to([P, 2, S]), ALU.add))
                dve.tensor_reduce(soft[:, 0:2], sm0[:, :, :], AX.X, ALU.max)
                dve.tensor_reduce(soft[:, 2:4], sm1[:, :, :], AX.X, ALU.max)
                step(dve.tensor_reduce(soft[:, 4:6], smc[:, :, 0:WINS], AX.X, ALU.max))
                dve.tensor_scalar(soft[:, 8:14], soft[:, 0:6], -SCALE, None, ALU.mult).then_inc(ns["mx"], 1)

            def weigh(h):
                dve.wait_ge(ns["ex"], h + 1)
                step(dve.reciprocal(soft[:, 24:30], soft[:, 16:22]))
                step(dve.tensor_tensor(soft[:, 24:30], soft[:, 24:30], gt[:, h, :], ALU.mult))
                for b in range(2):
                    dve.tensor_scalar(sm0[:, b, :], sm0[:, b, :], soft[:, 24 + b:25 + b], None, ALU.mult)
                    dve.tensor_scalar(sm1[:, b, :], sm1[:, b, :], soft[:, 26 + b:27 + b], None, ALU.mult)
                    ins = dve.scalar_tensor_tensor(smc[:, b, 0:WINS], smc[:, b, 0:WINS], soft[:, 28 + b:29 + b],
                                                   C1["cvalid"].rearrange("p (t c) -> p t c", t=2)[:, b, :],
                                                   ALU.mult, ALU.mult)
                ins.then_inc(ns["p"], 1)

            def low(h, r):
                dve.wait_ge(ns["oc"], h + 1)
                dve.tensor_tensor(yhl[:, h, 1, :], of[r % 2][:, :], yhl[:, h, 0, :].bitcast(F32),
                                  ALU.subtract).then_inc(s_ylo, 1)

            def queries(i):
                for j in range(4):
                    if j > 0 or not isinstance(i, int):
                        maxima(4 * i + j - 1)
                        split(Unit("q", j + 1, i))
                        weigh(4 * i + j - 1)
                    if j > 1 or not isinstance(i, int):
                        low(4 * i + j - 2, (j - 2) % 4)
                    query(j, i)

            queries(0)
            with dve.Fori(1, 4) as i:
                v_.enter(i, 20, first=1)
                queries(i)
                v_.leave(4)
            maxima(15)
            weigh(15)
            split(Unit("q", 17))
            low(14, 2)
            low(15, 3)
            out_phase("out1", 3)
            junction(3, "out1")
            up_phase("gu1", 1)
            down_phase("dn1", 4)
            junction(4, "dn1")

        @block.gpsimd
        def _(pool):
            pool.wait_ge(s_prm, 16)
            pool.wait_ge(s_l0c, 16)
            l_ = level
            with pool.Fori(0, 4) as i:
                n = i + 1
                pool.wait_ge(g["de"], n)
                four = [P, 4, P]
                pool.tensor_tensor(dt_[:, :, :], dt_[:, :, :], triu.unsqueeze(1).broadcast_to(four),
                                   ALU.mult).then_inc(g["dm"], 1)
                pool.wait_ge(g["bc"], 2 * n)
                eye = ident.unsqueeze(1).broadcast_to(four)
                pool.tensor_tensor(X[:, :, :], eye, eye, ALU.mult)
                pool.tensor_tensor(PT[:, :, :], eye, eye, ALU.mult).then_inc(g["xi"], 1)
                pool.wait_ge(g["lt"], n)
                for l in range(LEVELS):
                    if l >= 2:
                        pool.wait_ge(g["y"], i * LEVELS + l - 1)
                    pool.tensor_tensor(nt[l % 2][:, :, :], lt[:, :, :], level[:, l, :].unsqueeze(1).broadcast_to(four),
                                       ALU.mult).then_inc(g["nt"], 1)


def layouts(np, a):
    f = np.float32

    def chunks(v):
        v = v.reshape(v.shape[:-1] + (v.shape[-1] // P, P))
        return np.moveaxis(v, -1, 0)

    def units(w, cols):
        k = w.shape[0] // P
        return np.ascontiguousarray(w.reshape(k, P, w.shape[1])[:, :, cols].reshape(k, P, -1, P).transpose(2, 1, 0, 3))

    r = {}
    r["x"] = np.ascontiguousarray(a["x"][0].T.reshape(KD, P, S).transpose(1, 0, 2))
    w0 = a["ab_w_in"][0]
    ab = np.zeros((D, P), w0.dtype)
    ab[:, 0:8] = w0[:, 4096:4104]
    ab[:, 32:40] = w0[:, 4104:4112]
    cols = list(range(3072))
    z, hb, gb, gc = 3072, 4112, 5136, 6160
    for i in range(4):
        for s_, t in ((z, 0), (z, 1), (hb, 0), (gc, 0), (gb, 0), (hb, 1), (gc, 1), (gb, 1)):
            c = s_ + (2 * i + t) * P
            cols += list(range(c, c + P))
    r["w_in0"] = np.concatenate([units(ab, np.arange(P)), units(w0, np.array(cols))], 0)
    prm = np.zeros((P, N_PARAM), f)

    def put(name, v):
        c, w = PARAM[name]
        prm[:, c:c + w] = v.reshape(P, w)

    put("norm", chunks(a["norm_w"].reshape(8, D)))
    put("gconv", chunks(a["gdn_conv"][0]).transpose(0, 2, 1))
    put("sconv", chunks(a["sc_conv"][0]).transpose(0, 2, 1))
    put("fconv", chunks(a["ffn_conv"]).transpose(0, 1, 3, 2))
    put("gnorm", a["gdn_norm"][0][:, None])
    v = np.zeros((P, 1), f)
    v[0:8, 0] = a["gdn_a_log"][0]
    put("alog", v)
    v = np.zeros((P, 1), f)
    v[0:8, 0] = a["gdn_dt_bias"][0]
    put("dtb", v)
    put("eps", np.full((P, 1), EPS, f))
    oh = np.zeros((P, 8, 2), f)
    for h in range(8):
        oh[h, h, 0] = 1
        oh[32 + h, h, 1] = 1
    put("onehot", oh)
    put("ident", np.eye(P, dtype=f))
    put("ones", np.ones((P, P), f))
    r["params"] = prm
    j, i = np.arange(P)[:, None], np.arange(P)[None, :]
    l0 = [(i >= j).astype(f)]
    for l in range(LEVELS):
        s_ = 1 << l
        l0.append(((i // (2 * s_) == j // (2 * s_)) & (j // s_ % 2 == 0) & (i // s_ % 2 == 1)).astype(f))
    r["l0c"] = np.concatenate(l0, 1)
    every = np.arange(D)
    r["w_out0"] = units(a["ab_w_out"][0], every)
    r["w_out1"] = units(a["nsa_w_out"][0], every)
    for l in range(2):
        gu = a["ffn_w_gu"][l]
        cols = np.arange(2 * FF).reshape(2, KF, P).transpose(1, 0, 2).ravel()
        r[f"w_gu{l}"] = units(gu, cols)
        dn = units(a["ffn_w_down"][l], every)
        r[f"w_dn{l}"] = np.ascontiguousarray(dn.reshape(KD, P, 4, DN_K, P).transpose(0, 2, 1, 3, 4)).reshape(64, P, DN_K, P)
    w1 = a["nsa_w_in"][0]
    gates = np.zeros((D, P), w1.dtype)
    gates[:, 0:48] = w1[:, 5120:5168]
    r["w_in1"] = np.concatenate([units(gates, np.arange(P)), units(w1, np.arange(2048, 5120)), units(w1, every)], 0)
    c = []
    for name in ("cmp_w1_k", "cmp_w1_v"):
        c.append(a[name][0].reshape(2, 16, P, 2, P).transpose(3, 0, 2, 1, 4).reshape(4, P, 16, P))
    r["w_cmp"] = np.ascontiguousarray(np.concatenate(c, 0))
    l1 = np.zeros((P, N_L1C), f)

    def put1(name, v):
        c, w = L1C[name]
        l1[:, c:c + w] = v.reshape(P, w)

    inv = 1.0 / (10000.0 ** (np.arange(0, P, 2, dtype=f) / f(P)))
    ang = (np.arange(S, dtype=f)[:, None] * inv[None, :].astype(f)).astype(f)
    put1("cos", np.concatenate([np.cos(ang).T, np.cos(ang).T], 0))
    put1("sin", np.concatenate([-np.sin(ang).T, np.sin(ang).T], 0))
    causal = np.where(np.arange(P)[None, :] <= np.arange(P)[:, None], 0, NEG).astype(f)
    put1("causal", np.concatenate([np.zeros((P, P), f), causal], 1))
    tok = np.arange(S).reshape(TT, P).T[:, :, None]
    ok = np.arange(WINS)[None, None, :] * 16 + 31 <= tok
    put1("cmask", np.where(ok | (tok < 31), 0, NEG).astype(f))
    put1("cvalid", ok.astype(f))
    put1("posk", a["cmp_pos_k"][0].T)
    put1("posv", a["cmp_pos_v"][0].T)
    for n, k in (("w2k", "cmp_w2_k"), ("w2v", "cmp_w2_v")):
        put1(n, a[k][0].reshape(2, P, P).transpose(1, 0, 2))
    r["l1c"] = l1
    return r



def kernel(**inputs):
    import numpy as np
    import concourse.bacc as bacc
    from concourse.bass_utils import run_bass_kernel_spmd

    nc = bacc.Bacc("TRN2", target_bir_lowering=False, num_devices=1)
    arrays = {"in_" + k: v for k, v in layouts(np, {k: np.asarray(v) for k, v in inputs.items()}).items()}
    A = {k[3:]: nc.dram_tensor(k, v.shape, F32, kind="ExternalInput").ap() for k, v in arrays.items()}
    A["residual"] = nc.dram_tensor("residual", (P, KD, S), F32, kind="Internal").ap()
    out = nc.dram_tensor("out", (P, KD, S), F32, kind="ExternalOutput").ap()
    build(nc, A, out)
    got = run_bass_kernel_spmd(nc, [arrays], core_ids=[0]).results[0]["out"]
    return np.ascontiguousarray(got.transpose(1, 0, 2).reshape(D, S).T[None])
```

```python
from contextlib import ExitStack

import concourse.bass as bass
from concourse import mybir

F32 = mybir.dt.float32
F32R = mybir.dt.float32r
ACT = mybir.ActivationFunctionType
ALU = mybir.AluOpType
AX = mybir.AxisListType

P = 128
S = 256
D = 2048
KD = D // P
FF = 5632
KF = FF // P
DN_K = KF // 4
HEADS = 8
TT = S // P
LEVELS = 7
NG, NR = 4, 4
WINS = S // 16 - 1
CW = NG * WINS
EPS = 1e-6
NEG = -1e30
SCALE = float(P) ** -0.5

PHASES = ["ab", "qkv", "mix", "out0", "gu0", "dn0", "gate", "kv", "cmp", "q", "out1", "gu1", "dn1"]
N_UNITS = dict(ab=1, qkv=24, mix=32, out0=16, gu0=88, dn0=64, gate=1, kv=24, cmp=8, q=16, out1=16, gu1=88, dn1=64)
N_TILES = dict(N_UNITS, dn0=16, dn1=16, cmp=4)
U0, T0 = {}, {}
_u = _t = 0
for _p in PHASES:
    U0[_p], T0[_p] = _u, _t
    _u += N_UNITS[_p]
    _t += N_TILES[_p]
UNITS = _u

PARAM = {}
_c = 0
for _n, _w in [("norm", 8 * KD), ("gconv", 24 * 4), ("sconv", 8 * 3), ("fconv", 2 * KF * 3), ("gnorm", 1),
               ("alog", HEADS), ("dtb", HEADS), ("eps", 1), ("onehot", 2 * HEADS + 4), ("ident", P), ("ones", P)]:
    PARAM[_n] = (_c, _w)
    _c += _w
N_PARAM = _c
L0C = {"triu": (0, P), "level": (P, LEVELS * P)}
N_L0C = P + LEVELS * P
L1C = {}
_c = 0
for _n, _w in [("cos", S), ("sin", S), ("causal", S), ("cmask", TT * WINS), ("cvalid", TT * WINS),
               ("posk", 32), ("posv", 32), ("w2k", 2 * P), ("w2v", 2 * P)]:
    L1C[_n] = (_c, _w)
    _c += _w
N_L1C = _c


class Unit:

    def __init__(self, phase, j, i=0, per=4):
        off = U0[phase] + j
        self.n = off + per * i
        self.raw = off % 4
        self.half = off % 2
        self.loads = 16 * (off // 4 + 1) + 16 * (per // 4) * i


class Tile:

    def __init__(self, phase, j, i=0, per=4, bank=None):
        off = T0[phase] + j
        self.n = off + per * i
        self.bank = off % 4 if bank is None else bank


class Steps:

    def __init__(self, sem):
        self.sem, self.base, self.k, self.i, self.per = sem, 0, 0, None, 0

    def enter(self, i, per, first=0):
        self.base += self.k - first * per
        self.k, self.i, self.per = 0, i, per

    def leave(self, end):
        assert self.k == self.per, (self.k, self.per)
        self.base += end * self.per
        self.k, self.i = 0, None

    def mark(self, ins):
        ins.then_inc(self.sem, 1)
        self.k += 1
        return self.base + self.k + (self.i * self.per if self.i is not None else 0)


def after(eng, sem, value):
    if not isinstance(value, int) or value > 0:
        eng.wait_ge(sem, value)


def build(nc, A, out):
    ctx = ExitStack()
    base0 = (nc.sbuf_base + 63) // 64 * 64

    def at(name, offset, shape, dt=F32):
        return nc.alloc_sbuf_tensor_at(name, shape, dt, offset=base0 + offset)

    KB = 1024
    with ctx:
        def sem(name):
            return ctx.enter_context(nc.semaphore(name))

        raw = [at(f"raw{i}", i * 8 * KB, [P, KD, P]) for i in range(4)]
        hi = [at(f"hi{i}", (32 + 8 * i) * KB, [P, KD, P], F32R) for i in range(2)]
        lo = [at(f"lo{i}", (48 + 8 * i) * KB, [P, KD, P], F32R) for i in range(2)]
        XO = 64 * KB
        xhl = at("xhl", XO, [P, KD, 2, S], F32R)
        mh = at("mh", XO, [P, KD, 2, S])
        mout, hold = mh[:, :, 0, :], mh[:, :, 1, :]
        MO = 96 * KB
        mid = at("mid", MO, [P, KF, 2, S], F32R)
        yhl = at("yhl", MO, [P, KD, 2, S], F32R)
        hnew = at("hnew", MO + 72 * KB, [P, KD, S])
        sq4 = [at(f"sq4_{i}", MO + 40 * KB + 4 * KB * i, [P, 4, S]) for i in range(2)]
        WO = MO + 88 * KB

        qkv = at("qkv", MO + 32 * KB, [P, 3, 4, 2, S])
        G = MO + 56 * KB
        gb_ = at("gb_", G, [P, TT, P])
        gl = at("gl", G + KB, [P, 6, TT, HEADS])
        X = at("X", G, [P, 4, P])
        PT = at("PT", G + 2 * KB, [P, 4, P])
        dt_ = at("dt_", G + 4 * KB, [P, 4, P])
        yb_ = at("yb_", G + 4 * KB, [P, 4, P])
        bc = at("bc", G + 6 * KB, [P, 2, 2, S])
        nt = [at(f"nt{i}", G + 6 * KB + 2 * KB * i, [P, 4, P]) for i in range(2)]
        dqk = at("dqk", G + 10 * KB, [P, 8, P])
        vb = at("vb", G + 10 * KB, [P, 4, P])
        kdec = at("kdec", G + 12 * KB, [P, 2, P])
        kbg = at("kbg", G + 13 * KB, [P, 2, P])
        kb = at("kb", G + 14 * KB, [P, 2, S])
        vn0 = at("vn0", G + 14 * KB, [P, 2, P])
        vn1 = at("vn1", G + 15 * KB, [P, 2, P])
        qn = at("qn", G + 16 * KB, [P, 2, S])
        ot = at("ot", G + 18 * KB, [P, 2, S])
        vw = at("vw", G + 20 * KB, [P, 2, S])
        osq = at("osq", G + 20 * KB, [P, 2, S])
        lt = at("lt", G + 22 * KB, [P, 4, P])
        do_ = at("do_", G + 22 * KB, [P, 4, P])
        kn = at("kn", G + 24 * KB, [P, 2, S])
        wt = at("wt", G + 24 * KB, [P, 2, P])
        s1 = at("s1", G + 25 * KB, [P, 2, P])
        qg = at("qg", G + 26 * KB, [P, 2, P])
        eg = at("eg", G + 27 * KB, [P, 2, P])
        att = at("att", G + 28 * KB, [P, 4, P])
        zs = at("zs", G + 30 * KB, [P, 2, S])

        kt = at("kt", MO + 32 * KB, [P, 3, NG, S])
        vk = at("vk", MO + 44 * KB, [P, 3, NG, TT, P])
        l1c = at("l1c", MO + 56 * KB, [P, N_L1C])
        xf = [at(f"xf{k}", MO + 16 * KB * k, [P, 31 * 2 * CW + 256], F32R) for k in range(2)]
        xc = [t[:, 0:64 * CW].rearrange("p (k l c) -> p k l c", l=2, c=CW) for t in xf]
        assert N_L1C * 4 <= 7 * KB
        B1 = MO + 63 * KB
        h1 = at("h1", B1, [P, 4, CW])
        kc_ = at("kc_", B1 + 1024, [P, NG, WINS])
        vc_ = at("vc_", B1 + 1280, [P, NG, P])
        sig = at("sig", B1 + 3328, [P, TT, 3, 16])
        gt = at("gt", B1 + 3712, [P, 16, 6])
        B2 = MO + 68 * KB
        vst = at("vst", B2, [P, NG, S])
        xct = at("xct", B2 + 4 * KB, [P, 32, NG, WINS])
        gts = at("gts", B2 + 12 * KB, [P, S])
        qs = at("qs", B2, [P, NR, S])
        sm1 = at("sm1", B2 + 4 * KB, [P, 2, S])
        sm0 = at("sm0", B2 + 6 * KB, [P, 2, P])
        smc = at("smc", B2 + 7 * KB, [P, TT, 16])
        soft = at("soft", B2 + 7 * KB + 128, [P, 32])
        pt = at("pt", B2 + 8 * KB, [P, 2, 3 * P])
        ptc = at("ptc", B2 + 11 * KB, [P, S])
        vs = at("vs", B2 + 12 * KB, [P, 2, TT, P])
        vcs = at("vcs", B2 + 14 * KB, [P, P])
        of = [at(f"of{k}", B2 + 15 * KB + KB * k, [P, S]) for k in range(2)]
        C1 = {n: l1c[:, c:c + w] for n, (c, w) in L1C.items()}

        o = WO
        def small(name, shape, dt=F32):
            nonlocal o
            n = 4
            for s_ in shape[1:]:
                n *= s_
            t = at(name, o, shape, dt)
            o += (n + 31) // 32 * 32
            return t

        prm = small("prm", [P, N_PARAM])
        half = [small(f"half{i}", [P, CW]) for i in range(2)]
        cbuf = [small(f"cbuf{i}", [P, 3 + S]) for i in range(2)]
        cv = [small(f"cv{i}", [P, S]) for i in range(2)]
        up = [small(f"up{i}", [P, S]) for i in range(2)]
        ssq = small("ssq", [P, S])
        acc = ssq
        sqd = [small(f"sqd{i}", [P, S]) for i in range(2)]
        rstd = small("rstd", [P, S])
        tiny = small("tiny", [P, 160])
        diag = [x[:, :].rearrange("p (t j) -> p t j", t=TT) for x in sqd]
        wend = o
        sil = [small(f"sil{i}", [P, S]) for i in range(2)]
        mf = [small(f"mf{i}", [P, S]) for i in range(2)]
        o = wend
        l0c = small("l0c", [P, N_L0C])
        R = small("R", [P, S])
        abf = small("abf", [P, S])
        sel = small("sel", [P, 4, P])
        sqt = [sqd[1], small("sqt", [P, S])]
        gcol = tiny[:, 8:24].rearrange("p (t i a) -> p t i a", t=TT, a=2)
        bcol = tiny[:, 24:40].rearrange("p (t i a) -> p t i a", t=TT, a=2)
        bge = tiny[:, 40:48].rearrange("p (i a) -> p i a", a=2)
        rc = tiny[:, 80:120]

        def prm_(name, *dims):
            c, w = PARAM[name]
            return prm[:, c:c + w]

        normw = prm_("norm").rearrange("p (l c) -> p l c", l=8)
        norm1 = prm_("norm").rearrange("p (l c o) -> p l c o", l=8, o=1)
        gconv = prm_("gconv").rearrange("p (c k) -> p c k", k=4)
        sconv = prm_("sconv").rearrange("p (i a k) -> p i a k", a=2, k=3)
        fconv = prm_("fconv").rearrange("p (l c k) -> p l c k", l=2, k=3)
        onehot = prm_("onehot").rearrange("p (i a) -> p i a", a=4)
        gnorm, alog, dtb, eps = prm_("gnorm"), prm_("alog"), prm_("dtb"), prm_("eps")
        ident, ones = prm_("ident"), prm_("ones")
        triu = l0c[:, 0:P]
        level = l0c[:, P:].rearrange("p (l j) -> p l j", l=LEVELS)

        lin = [ctx.enter_context(nc.psum_tensor(f"lin{i}", [P, 512], F32)) for i in range(4)]
        aux = [ctx.enter_context(nc.psum_tensor(f"aux{i}", [P, 512], F32)) for i in range(4)]

        s_prm = sem("s_prm")
        s_l0c = sem("s_l0c")
        s_w = [sem(f"s_w{i}") for i in range(4)]
        s_hi = sem("s_hi")
        s_lo = sem("s_lo")
        s_wh = sem("s_wh")
        s_unit = sem("s_unit")
        s_half = sem("s_half")
        s_free = sem("s_free")
        v_ = Steps(sem("s_dve"))
        a_ = Steps(sem("s_act"))
        s_hload = sem("s_hload")
        s_out = sem("s_out")
        s_hstore = sem("s_hstore")
        s_hn = sem("s_hn")
        s_sq4 = sem("s_sq4")
        s_acc = sem("s_acc")
        p_ = Steps(sem("s_pool"))
        s_nps = sem("s_nps")
        s_root = sem("s_root")
        s_x = [sem(f"s_x{i}") for i in range(4)]
        s_col = sem("s_col")
        s_bc = sem("s_bc")
        s_rs = sem("s_rs")
        s_xhi = sem("s_xhi")
        s_xlo = sem("s_xlo")
        s_msq = sem("s_msq")
        s_ssq = sem("s_ssq")
        s_conv = sem("s_conv")
        s_silu = sem("s_silu")
        s_mid = sem("s_mid")
        s_midhi = sem("s_midhi")
        s_midlo = sem("s_midlo")
        s_yf = sem("s_yf")
        s_yhi = sem("s_yhi")
        s_ylo = sem("s_ylo")
        attention_steps = dict(
            gates_turned="columns of the gate logits",
            gate_exps="their exponentials",
            halves_swapped="a head's halves exchanged",
            rotated="rotated keys and queries",
            values_turned="values, [token, channel], in PSUM",
            values_kept="in SBUF",
            windows="windows with positions",
            windows_high="high parts",
            windows_low="low parts",
            hidden="compression's hidden, of a kind",
            compressed="compressed keys and values",
            compressed_kept="in SBUF",
            group_values="a group's values in their fixed places",
            scores="a head's scores",
            maxima="their maxima, scaled",
            exps="exponentials and sums",
            probs="probabilities times gate over sum",
            probs_turned="transposed, in PSUM",
            probs_taken="in SBUF",
            output="a head's output",
            output_taken="in SBUF",
        )
        ns = {name: sem("n_" + name) for name in attention_steps}
        s_l1c = sem("s_l1c")
        s_post = sem("s_post")
        s_pdiag = sem("s_pdiag")
        s_pbc = sem("s_pbc")
        deltanet_steps = dict(
            ab_turned="columns of the gate logits",
            gate_sums="a + dt_bias",
            decay_exps="exponentials of decays (the gates' first)",
            gate_logs="logarithms of the decays",
            cumulated="summed over the tokens",
            gates_placed="decays and beta as columns",
            rows_turned="and as rows, in PSUM",
            rows_ready="rows in SBUF",
            g_exps="exp(g) of the second tile",
            qk_squares="squares of q and k tiles",
            qk_sums="their column sums",
            qk_roots="their roots",
            qk_columns="1 / norm",
            selector="a head pair's rows of R",
            spread="its g and beta over all partitions",
            spread_taken="in SBUF",
            qk_diag="norms on diagonals",
            qk_factors="norms over all partitions",
            v_placed="v in its fixed place",
            k_normed="k",
            k_beta="k times beta (and q)",
            decay_logs="differences of g",
            decays="their exponentials",
            decays_masked="causal",
            q_decayed="q of the second tile",
            kv_turned="k and v, [token, channel]",
            v_scaled="v and k with their factors",
            grams="k k and k q products",
            lt_ready="L transposed",
            att_ready="masked scores",
            level_0_masked="L's part of the first level",
            level_masked="and of the others",
            pt_begun="PT's first level",
            y_product="first product of a level",
            y_taken="in SBUF",
            z_product="second products",
            inverse_step="X and PT of a level",
            first_v="products of the first tile",
            first_v_taken="in SBUF",
            state="state after the first tile",
            state_taken="in SBUF",
            second_v="products of the second tile",
            second_v_taken="in SBUF",
            outputs="outputs",
            outputs_taken="and their squares in SBUF",
            output_sums="column sums",
            output_roots="roots",
            output_diag="on diagonals",
            output_factors="over all partitions",
            z_silu="silu(z)",
        )
        g = {name: sem("g_" + name) for name in deltanet_steps}

        block = ctx.enter_context(nc.Block())

        @block.sync
        def _(sp):
            sp.dma_start(prm[:, :], A["params"]).then_inc(s_prm, 16)

            def x_group(q):
                sp.dma_start(hnew[:, 4 * q:4 * q + 4, :], A["x"][:, 4 * q:4 * q + 4, :]).then_inc(s_x[q], 16)

            x_group(0)

            def load(u, src, nk=KD):
                after(sp, s_lo, u.n - 3)
                sp.dma_start(raw[u.raw][:, 0:nk, :], src).then_inc(s_w[u.raw], 16)

            w = A["w_in0"]
            load(Unit("ab", 0), w[0])
            for q in range(1, 4):
                x_group(q)
            for j in range(1, 4):
                load(Unit("ab", j), w[j])
            sp.dma_start(l0c[:, :], A["l0c"]).then_inc(s_l0c, 16)
            load(Unit("ab", 4), w[4])
            with sp.Fori(0, 13) as i:
                for j in range(4):
                    load(Unit("ab", 5 + j, i), w[i * 4 + 5 + j])

            def loads(phase, w, nk=KD):
                with sp.Fori(1, N_UNITS[phase] // 4) as i:
                    for j in range(4):
                        load(Unit(phase, j, i), w[i * 4 + j], nk)

            def first(phase, w, nk=KD):
                for j in range(4):
                    load(Unit(phase, j), w[j], nk)

            def residual(j, phase):
                sp.wait_ge(s_unit, U0[phase])
                if j > 1:
                    sp.wait_ge(s_hstore, 16 * (j - 1))
                sp.dma_start(hold, A["x"] if j == 1 else A["residual"]).then_inc(s_hload, 16)

            def store(j):
                sp.wait_ge(s_hn, 4 * j)
                sp.wait_ge(s_hload, 16 * j)
                sp.dma_start(A["residual"], hnew[:, :, :]).then_inc(s_hstore, 16)

            first("out0", A["w_out0"])
            loads("out0", A["w_out0"])
            residual(1, "out0")
            first("gu0", A["w_gu0"])
            store(1)
            loads("gu0", A["w_gu0"])
            first("dn0", A["w_dn0"], DN_K)
            loads("dn0", A["w_dn0"], DN_K)
            residual(2, "dn0")
            w = A["w_in1"]
            for j in range(4):
                load(Unit("gate", j), w[j])
            sp.wait_ge(s_unit, U0["gate"])
            sp.dma_start(l1c[:, :], A["l1c"]).then_inc(s_l1c, 16)
            store(2)
            load(Unit("gate", 4), w[4])
            with sp.Fori(0, 5) as i:
                for j in range(4):
                    load(Unit("gate", 5 + j, i), w[i * 4 + 5 + j])
            for j in range(8):
                load(Unit("cmp", j), A["w_cmp"][j])
            for j in range(16):
                load(Unit("q", j), w[25 + j])
            first("out1", A["w_out1"])
            loads("out1", A["w_out1"])
            residual(3, "out1")
            first("gu1", A["w_gu1"])
            store(3)
            loads("gu1", A["w_gu1"])
            first("dn1", A["w_dn1"], DN_K)
            loads("dn1", A["w_dn1"], DN_K)
            residual(4, "dn1")
            for q in range(4):
                sp.wait_ge(s_hn, 16 - 3 + q)
                sp.dma_start(out[:, 4 * q:4 * q + 4, :], hnew[:, 4 * q:4 * q + 4, :]).then_inc(s_out, 16)
            sp.wait_ge(s_out, 64)

        @block.tensor
        def _(pe):
            def passes(u, bank, hi_, lo_, nk, start, stop, ready=None, slot=None):
                pe.wait_ge(s_hi, u.n + 1)
                for k in range(nk):
                    if ready is not None:
                        ready(k)
                    pe.matmul(bank[:, 0:S], hi[u.half][:, k, :], hi_(k), start=start and k == 0, stop=False,
                              skip_group_check=True)
                    m = pe.matmul(bank[:, 0:S], hi[u.half][:, k, :], lo_(k), start=False, stop=False,
                                  skip_group_check=True)
                    if k == nk - 1:
                        m.then_inc(s_wh, 1)
                    if slot is not None:
                        slot(k)
                pe.wait_ge(s_lo, u.n + 1)
                for k in range(nk):
                    m = pe.matmul(bank[:, 0:S], lo[u.half][:, k, :], hi_(k), start=False, stop=stop and k == nk - 1,
                                  skip_group_check=True)
                m.then_inc(s_unit, 1)
                if slot is not None:
                    slot(nk)

            def x_unit(u, t, slot=None, last=3):
                after(pe, s_free, t.n - last)
                passes(u, lin[t.bank], lambda k: xhl[:, k, 0, :], lambda k: xhl[:, k, 1, :], KD, True, True, slot=slot)

            def x_pair(units, tiles, norm):
                after(pe, s_free, tiles[1].n - 3)

                def product(e, w, x, q, done=None):
                    if q == 0:
                        pe.wait_ge(s_lo if w else s_hi, units[e].n + 1)
                    for k in range(4 * q, 4 * q + 4):
                        m = pe.matmul(lin[tiles[e].bank][:, 0:S], (lo if w else hi)[units[e].half][:, k, :],
                                      xhl[:, k, x, :], start=w == 0 and x == 0 and k == 0,
                                      stop=w == 1 and k == KD - 1, skip_group_check=True)
                    if done is not None:
                        m.then_inc(done, 1)

                for q in range(5):
                    if q > 0:
                        product(1, 0, 0, q - 1)
                        product(1, 0, 1, q - 1, done=s_wh if q == 4 else None)
                        product(1, 1, 0, q - 1, done=s_unit if q == 4 else None)
                    if q < 4:
                        pe.wait_ge(s_xhi, 4 * norm + q + 1)
                        product(0, 0, 0, q)
                        if q < 3:
                            product(0, 1, 0, q)
                        pe.wait_ge(s_xlo, 4 * norm + q + 1)
                        product(0, 0, 1, q, done=s_wh if q == 3 else None)
                        if q == 3:
                            product(0, 1, 0, q, done=s_unit)

            def factors(norm, k):
                if k == 3:
                    sum_squares(norm)
                if k != KD - 1:
                    return
                pe.wait_ge(s_col, norm + 1)
                pe.matmul(aux[0][:, 0:S], ones, diag[1], start=True, stop=True).then_inc(s_bc, 1)

            def sum_squares(norm):
                pe.wait_ge(s_acc, 4 * norm + 4)
                for t in range(TT):
                    m = pe.matmul(aux[0][:, t:t + 1], acc[:, t * P:(t + 1) * P], ones[:, 0:1],
                                  start=True, stop=True, skip_group_check=True)
                m.then_inc(s_nps, 1)

            pe.wait_ge(s_prm, 16)
            x_pair([Unit("ab", 0), Unit("qkv", 0)], [Tile("ab", 0), Tile("qkv", 0)], 0)

            def qkv_unit(j, i, slot):
                x_unit(Unit("qkv", j, i), Tile("qkv", j, i, bank=(j + 1) % 2 if isinstance(i, int) and i == 5 else None),
                       slot=slot, last=1 if isinstance(i, int) and i == 5 else 3)

            def column_sums(c, b):
                pe.wait_ge(g["qk_squares"], c + 1)
                for t in range(TT):
                    m = pe.matmul(aux[1][:, bass.ds(2 * c + t, 1)], sqt[b][:, t * P:(t + 1) * P],
                                  ones[:, 0:1], start=True, stop=True, skip_group_check=True)
                m.then_inc(g["qk_sums"], 1)

            def turn_ab():
                pe.wait_ge(s_free, T0["ab"] + 1)
                for t in range(TT):
                    m = pe.transpose(aux[2][:, t * P:(t + 1) * P], abf[:, t * P:(t + 1) * P], ident)
                m.then_inc(g["ab_turned"], 1)

            def cumulate():
                pe.wait_ge(g["gate_logs"], 1)
                pe.wait_ge(s_l0c, 16)
                pe.matmul(aux[3][:, 0:TT * HEADS], triu, gl[:, 2, :, :], start=True,
                        stop=True).then_inc(g["cumulated"], 1)

            def gate_rows():
                pe.wait_ge(g["gates_placed"], 1)
                for t in range(TT):
                    m = pe.transpose(aux[2][:, t * P:(t + 1) * P], gb_[:, t, :], ident)
                m.then_inc(g["rows_turned"], 1)

            def spread(n):
                pe.wait_ge(g["selector"], n + 1)
                for k in range(2):
                    for h in range(2):
                        m = pe.matmul(aux[1 + k][:, h * S:(h + 1) * S], sel[:, 2 * h + k, :], R[:, :],
                                      start=True, stop=True, skip_group_check=True)
                m.then_inc(g["spread"], 1)

            def norms(n):
                pe.wait_ge(g["qk_diag"], n + 1)
                for k in range(2):
                    m = pe.matmul(lin[2 + k][:, :], ones, dqk[:, 4 * k:4 * k + 4, :], start=True, stop=True)
                m.then_inc(g["qk_factors"], 1)

            for j in range(1, 4):
                plan = {(1, 3): lambda: factors(0, 3), (1, 15): lambda: factors(0, 15), (2, 15): turn_ab,
                        (2, KD): lambda: column_sums(0, 0), (3, KD): lambda: column_sums(1, 1)}
                qkv_unit(j, 0, lambda k, j=j: plan[j, k]() if (j, k) in plan else None)
            with pe.Fori(1, 4) as i:
                for j in range(4):
                    qkv_unit(j, i, lambda k, j=j: column_sums(4 * i + j - 2, j % 2) if k == KD else None)
            for j in range(4):
                plan = {(1, 7): cumulate, (0, KD): lambda: column_sums(14, 0), (1, KD): lambda: column_sums(15, 1),
                        (3, 7): gate_rows}
                qkv_unit(j, 4, lambda k, j=j: plan[j, k]() if (j, k) in plan else None)
            first = {(1, 7): spread, (3, 7): norms}
            for j in range(4):
                qkv_unit(j, 5, lambda k, j=j: first[j, k](0) if (j, k) in first else None)

            def mix(i):
                n = i + 1

                def turn():
                    pe.wait_ge(g["k_normed"], n)
                    pe.wait_ge(g["v_placed"], n)
                    for q in range(4):
                        pe.transpose(aux[2][:, q * P:(q + 1) * P], kn[:, q // 2, (q % 2) * P:(q % 2 + 1) * P], ident)
                    for q in range(4):
                        m = pe.transpose(aux[3][:, q * P:(q + 1) * P], vw[:, q // 2, (q % 2) * P:(q % 2 + 1) * P], ident)
                    m.then_inc(g["kv_turned"], 1)

                def grams():
                    pe.wait_ge(g["k_beta"], n)
                    for bank, rhs in ((aux[0], kb), (aux[1], qn)):
                        for q in range(4):
                            sl = slice((q % 2) * P, (q % 2 + 1) * P)
                            m = pe.matmul(bank[:, q * P:(q + 1) * P], kn[:, q // 2, sl], rhs[:, q // 2, sl],
                                          start=True, stop=True, skip_group_check=True)
                    m.then_inc(g["grams"], 1)

                def level_0():
                    pe.wait_ge(g["level_0_masked"], n)
                    for q in range(4):
                        m = pe.transpose(aux[3][:, q * P:(q + 1) * P], nt[0][:, q, :], ident)
                    m.then_inc(g["z_product"], 1)

                def inv_a(l):
                    pe.wait_ge(g["level_masked"], i * (LEVELS - 1) + l)
                    if l == 1:
                        pe.wait_ge(g["pt_begun"], n)
                        pe.wait_ge(g["v_scaled"], n)
                    pe.wait_ge(g["inverse_step"], i * LEVELS + l)
                    for q in range(4):
                        m = pe.matmul(aux[2][:, q * P:(q + 1) * P], nt[l % 2][:, q, :], X[:, q, :],
                                      start=True, stop=True, skip_group_check=True)
                    m.then_inc(g["y_product"], 1)

                def inv_b(l):
                    pe.wait_ge(g["y_taken"], i * (LEVELS - 1) + l)
                    s_ = 1 << l
                    for q in range(4):
                        yq = yb_[:, q, :].rearrange("p (b h s) -> p b h s", h=2, s=s_)
                        pq = PT[:, q, :].rearrange("p (b h s) -> p b h s", h=2, s=s_)
                        pe.matmul(aux[3][:, q * 64:(q + 1) * 64], PT[:, q, :], yq[:, :, 0, :],
                                  start=True, stop=True, skip_group_check=True)
                        m = pe.matmul(aux[3][:, 256 + q * 64:256 + (q + 1) * 64], yb_[:, q, :], pq[:, :, 1, :],
                                      start=True, stop=True, skip_group_check=True)
                    m.then_inc(g["z_product"], 1)

                def first_v():
                    pe.wait_ge(g["inverse_step"], (i + 1) * LEVELS)
                    pe.wait_ge(g["att_ready"], n)
                    for h in range(2):
                        pe.matmul(aux[0][:, h * P:(h + 1) * P], PT[:, 2 * h, :], vb[:, 2 * h, :],
                                  start=True, stop=True, skip_group_check=True)
                        m = pe.matmul(aux[0][:, 256 + h * P:256 + (h + 1) * P], kbg[:, h, :], PT[:, 2 * h + 1, :],
                                      start=True, stop=True, skip_group_check=True)
                    m.then_inc(g["first_v"], 1)

                def state():
                    pe.wait_ge(g["first_v_taken"], n)
                    for h in range(2):
                        m = pe.matmul(aux[1][:, h * P:(h + 1) * P], kdec[:, h, :], vn0[:, h, :],
                                      start=True, stop=True, skip_group_check=True)
                    m.then_inc(g["state"], 1)

                def second_v():
                    pe.wait_ge(g["state_taken"], n)
                    for h in range(2):
                        pe.matmul(aux[2][:, h * P:(h + 1) * P], PT[:, 2 * h + 1, :], vb[:, 2 * h + 1, :],
                                  start=True, stop=False, skip_group_check=True)
                        m = pe.matmul(aux[2][:, h * P:(h + 1) * P], wt[:, h, :], s1[:, h, :],
                                      start=False, stop=True, skip_group_check=True)
                    m.then_inc(g["second_v"], 1)

                def outputs():
                    pe.wait_ge(g["second_v_taken"], n)
                    pe.wait_ge(g["q_decayed"], n)
                    for h in range(2):
                        pe.matmul(aux[3][:, h * S:h * S + P], vn0[:, h, :], att[:, 2 * h, :],
                                  start=True, stop=True, skip_group_check=True)
                        pe.matmul(aux[3][:, h * S + P:(h + 1) * S], vn1[:, h, :], att[:, 2 * h + 1, :],
                                  start=True, stop=False, skip_group_check=True)
                        m = pe.matmul(aux[3][:, h * S + P:(h + 1) * S], s1[:, h, :], qg[:, h, :],
                                      start=False, stop=True, skip_group_check=True)
                    m.then_inc(g["outputs"], 1)

                def out_norm():
                    pe.wait_ge(g["outputs_taken"], n)
                    for q in range(4):
                        m = pe.matmul(aux[0][:, q:q + 1], osq[:, q // 2, (q % 2) * P:(q % 2 + 1) * P], ones[:, 0:1],
                                      start=True, stop=True, skip_group_check=True)
                    m.then_inc(g["output_sums"], 1)

                def out_scale():
                    pe.wait_ge(g["output_diag"], n)
                    pe.matmul(aux[0][:, :], ones, do_[:, :, :], start=True,
                            stop=True).then_inc(g["output_factors"], 1)

                plan = {0: [turn], 1: [grams], 15: [first_v], 16: [state], 17: [second_v], 18: [outputs],
                        19: [out_norm], 20: [out_scale], 22: [lambda: spread(n)], 23: [lambda: norms(n)]}
                plan[2] = [level_0]
                for l in range(1, LEVELS):
                    plan[1 + 2 * l] = [lambda l=l: inv_a(l)]
                    plan[2 + 2 * l] = [lambda l=l: inv_b(l)]
                for j in range(8):
                    x_unit(Unit("mix", j, i, 8), Tile("mix", j, i, 8, bank=(j + 1) % 2), last=1,
                           slot=lambda k, j=j: [f() for f in plan.get(3 * j + {7: 0, 15: 1, 16: 2}.get(k, 99), [])])

            with pe.Fori(0, 4) as i:
                mix(i)

            def out_phase(phase):
                def tiles(i):
                    for j in range(4):
                        peeled = isinstance(i, int)

                        def ready(k):
                            if peeled and j == 0 and k in (0, 6, 14, 15):
                                pe.wait_ge(s_ylo, {0: 9, 6: 11, 14: 11, 15: 12}[k])
                        if peeled and phase == "out1" and j < 2:
                            continue
                        t = Tile(phase, j, i, bank=j if phase == "out1" else None)
                        after(pe, s_free, t.n - (1 if phase == "out0" and peeled and j == 0 else 3))
                        passes(Unit(phase, j, i), lin[t.bank], lambda k: yhl[:, k, 0, :],
                               lambda k: yhl[:, k, 1, :], KD, True, True, ready=ready if phase == "out0" else None)
                tiles(0)
                with pe.Fori(1, 4) as i:
                    tiles(i)

            def up_phase(phase, norm):
                x_pair([Unit(phase, j) for j in range(2)], [Tile(phase, j) for j in range(2)], norm)
                x_unit(Unit(phase, 2), Tile(phase, 2), slot=lambda k: factors(norm, k))
                x_unit(Unit(phase, 3), Tile(phase, 3))
                with pe.Fori(1, 22) as i:
                    for j in range(4):
                        x_unit(Unit(phase, j, i), Tile(phase, j, i))

            def down_phase(phase, layer):
                with pe.Fori(0, 8) as i:
                    for a in range(2):
                        t = Tile(phase, a, i, 2)
                        pe.wait_ge(s_free, t.n - 1)
                        for q in range(4):
                            pe.wait_ge(s_midlo, KF * layer + DN_K * (q + 1))
                            passes(Unit(phase, 4 * a + q, i, 8), lin[t.bank],
                                   lambda k: mid[:, DN_K * q + k, 0, :], lambda k: mid[:, DN_K * q + k, 1, :],
                                   DN_K, q == 0, q == 3)

            def junction(j):
                pe.wait_ge(s_ssq, 17 * j)
                for t in range(TT):
                    m = pe.matmul(aux[1][:, t:t + 1], ssq[:, t * P:(t + 1) * P], ones[:, 0:1],
                                  start=True, stop=True, skip_group_check=True)
                m.then_inc(s_post, 1)
                pe.wait_ge(s_pdiag, j)
                pe.matmul(aux[1][:, 0:S], ones, diag[0], start=True, stop=True).then_inc(s_pbc, 1)

            out_phase("out0")
            junction(1)
            up_phase("gu0", 1)
            down_phase("dn0", 0)
            junction(2)

            x_pair([Unit("gate", 0), Unit("kv", 0)], [Tile("gate", 0), Tile("kv", 0)], 2)

            def kv(i):
                for j in range(8):
                    peeled = isinstance(i, int)
                    if not peeled or j > 0:
                        x_unit(Unit("kv", j, i, 8), Tile("kv", j, i, 8),
                               slot=lambda k, now=peeled and j == 1: factors(2, k) if now else None)
                    if j == 2 and peeled:
                        pe.wait_ge(s_free, T0["gate"] + 1)
                        for t in range(TT):
                            m = pe.transpose(aux[1][:, t * P:(t + 1) * P], gts[:, t * P:(t + 1) * P], ident)
                        m.then_inc(ns["gates_turned"], 1)
                    if j >= 5:
                        turn_v(i, j - 5)
                turn_v(i, 3)

            def turn_v(i, g_):
                pe.wait_ge(s_free, Tile("kv", 4 + g_, i, 8).n + 1)
                after(pe, ns["values_kept"], 4 * i + g_ - 1)
                for t in range(TT):
                    m = pe.transpose(aux[2 + g_ % 2][:, t * P:(t + 1) * P], vst[:, g_, t * P:(t + 1) * P], ident)
                m.then_inc(ns["values_turned"], 1)

            kv(0)
            with pe.Fori(1, 3) as i:
                kv(i)
            for kind in range(2):
                pe.wait_ge(ns["windows_low"], kind + 1)

                def window(k):
                    return xf[kind][:, 2 * CW * k:2 * CW * k + S]

                for ht in range(2):
                    t = Tile("cmp", 2 * kind + ht)
                    pe.wait_ge(s_free, t.n - 3)
                    for q in range(2):
                        u = Unit("cmp", 4 * kind + 2 * ht + q)
                        pe.wait_ge(s_hi, u.n + 1)
                        for k in range(KD):
                            m = pe.matmul(lin[t.bank][:, 0:S], hi[u.half][:, k, :], window(16 * q + k),
                                          start=q == 0 and k == 0, stop=False, skip_group_check=True)
                        m.then_inc(s_wh, 1)
                        pe.wait_ge(s_lo, u.n + 1)
                        for k in range(KD):
                            m = pe.matmul(lin[t.bank][:, 0:S], lo[u.half][:, k, :], window(16 * q + k),
                                          start=False, stop=q == 1 and k == KD - 1, skip_group_check=True)
                        m.then_inc(s_unit, 1)
            def compressed():
                pe.wait_ge(ns["hidden"], 2)
                for ht in range(2):
                    pe.matmul(aux[0][:, 0:CW], C1["w2k"].rearrange("p (a d) -> p a d", a=2)[:, ht, :],
                              h1[:, ht, :], start=ht == 0, stop=ht == 1)
                for g_ in range(NG):
                    for ht in range(2):
                        m = pe.matmul(aux[1][0:WINS, g_ * P:(g_ + 1) * P], h1[:, 2 + ht, g_ * WINS:(g_ + 1) * WINS],
                                      C1["w2v"].rearrange("p (a d) -> p a d", a=2)[:, ht, :],
                                      start=ht == 0, stop=ht == 1, skip_group_check=True)
                m.then_inc(ns["compressed"], 1)
                pe.wait_ge(ns["compressed_kept"], 1)

            def scores(h, g_, r):
                pe.wait_ge(ns["rotated"], 12 + h + 1)
                after(pe, ns["maxima"], h)
                for t in range(TT):
                    pe.matmul(aux[0][:, S + 16 * t:S + 16 * t + WINS], qs[:, r, t * P:(t + 1) * P], kc_[:, g_, :],
                              start=True, stop=True, skip_group_check=True)
                pe.matmul(aux[0][:, 0:S], qs[:, r, 0:P], kt[:, 1:3, g_, 0:P], start=True, stop=True,
                          skip_group_check=True)
                pe.matmul(aux[1][:, :], qs[:, r, P:S], kt[:, 1:3, g_, :], start=True,
                        stop=True).then_inc(ns["scores"], 1)

            def turn_p(h):
                pe.wait_ge(ns["probs"], h + 1)
                after(pe, ns["probs_taken"], h)
                for b in range(2):
                    pe.transpose(aux[2][:, b * P:(b + 1) * P], sm0[:, b, :], ident)
                for t in range(TT):
                    pe.transpose(aux[2][0:WINS, (2 + t) * P:(3 + t) * P], smc[:, t, 0:WINS], ident)
                for b in range(2):
                    for k in range(2):
                        m = pe.transpose(aux[3][:, (2 * b + k) * P:(2 * b + k + 1) * P], sm1[:, b, k * P:(k + 1) * P],
                                         ident)
                m.then_inc(ns["probs_turned"], 1)

            def values(h, g_, r):
                pe.wait_ge(ns["probs_taken"], h + 1)
                pe.wait_ge(ns["group_values"], g_ + 1)
                after(pe, ns["output_taken"], h - 1)
                o_ = lin[2 + r % 2]
                for b in range(2):
                    pe.matmul(o_[:, 0:S], vs[:, b, 0, :], pt[:, b, 0:S], start=b == 0, stop=False, skip_group_check=True)
                    pe.matmul(o_[:, P:S], vs[:, b, 1, :], pt[:, b, S:S + P], start=False, stop=False,
                              skip_group_check=True)
                pe.matmul(o_[:, 0:S], vcs[0:WINS, :], ptc[0:WINS, :], start=False, stop=True,
                          skip_group_check=True).then_inc(ns["output"], 1)

            def queries(i):
                for j in range(4):
                    def slot(k, j=j):
                        if k == 5 and (j > 1 or not isinstance(i, int)):
                            turn_p(4 * i + j - 2)
                        if k == 8 and (j > 0 or not isinstance(i, int)):
                            scores(4 * i + j - 1, i if j > 0 else i - 1, (j - 1) % 4)
                        if k == 13 and (j > 1 or not isinstance(i, int)):
                            values(4 * i + j - 2, i if j > 1 else i - 1, (j - 2) % 4)
                    t = Tile("q", j, i, bank=j % 2)
                    pe.wait_ge(s_free, t.n - 1)
                    passes(Unit("q", j, i), lin[t.bank], lambda k: xhl[:, k, 0, :], lambda k: xhl[:, k, 1, :],
                           KD, True, True, slot=slot)
                    if j == 0 and isinstance(i, int):
                        compressed()

            queries(0)
            with pe.Fori(1, 4) as i:
                queries(i)

            done = 12

            def out_part(j, w, x, chunks, signal=None):
                for k in chunks:
                    m = pe.matmul(lin[j][:, 0:S], (lo if w else hi)[Unit("out1", j).half][:, k, :], yhl[:, k, x, :],
                                  start=w == 0 and x == 0 and k == 0, stop=w == 1 and k == KD - 1, skip_group_check=True)
                if signal is not None:
                    m.then_inc(signal, 1)

            early, late = range(done), range(done, KD)
            pe.wait_ge(s_free, T0["q"] + 15)
            pe.wait_ge(s_ylo, 12 + done)
            pe.wait_ge(s_hi, U0["out1"] + 1)
            out_part(0, 0, 0, early)
            turn_p(14)
            out_part(0, 0, 1, early)
            scores(15, 3, 3)
            pe.wait_ge(s_lo, U0["out1"] + 1)
            out_part(0, 1, 0, early)
            values(14, 3, 2)
            pe.wait_ge(s_free, T0["q"] + 16)
            pe.wait_ge(s_hi, U0["out1"] + 2)
            out_part(1, 0, 0, early)
            out_part(1, 0, 1, early)
            turn_p(15)
            pe.wait_ge(s_lo, U0["out1"] + 2)
            out_part(1, 1, 0, early)
            values(15, 3, 3)
            pe.wait_ge(s_ylo, 28)
            for j in range(2):
                out_part(j, 0, 0, late)
                out_part(j, 0, 1, late, s_wh)
                out_part(j, 1, 0, late, s_unit)
            out_phase("out1")
            junction(3)
            up_phase("gu1", 3)
            down_phase("dn1", 1)
            junction(4)

        @block.scalar
        def _(act):
            def split(u, nk=KD):
                act.wait_ge(s_w[u.raw], u.loads)
                after(act, s_wh, u.n - 1)
                after(act, s_lo, u.n - 1)
                act.activation(hi[u.half][:, 0:nk, :], raw[u.raw][:, 0:nk, :], ACT.Copy).then_inc(s_hi, 1)

            def norm(nn, group, then):
                w = normw[:, 2 * nn, :]
                for q in range(4):
                    group(q)
                    for c in range(4 * q, 4 * q + 4):
                        m = act.activation(xhl[:, c, 0, :], hnew[:, c, :], ACT.Copy, scale=w[:, c:c + 1])
                    m.then_inc(s_xhi, 1)
                    after(act, s_acc, 4 * nn + q - 1)
                    act.activation(sq4[q % 2][:, :, :], hnew[:, 4 * q:4 * q + 4, :], ACT.Square).then_inc(s_sq4, 1)
                then()
                act.wait_ge(s_nps, nn + 1)
                act.activation(tiny[:, 0:2], aux[0][:, 0:2], ACT.Sqrt, bias=eps, scale=1.0 / D).then_inc(s_root, 1)

            def factors(nn):
                act.wait_ge(s_bc, nn + 1)
                act.activation(rstd[:, :], aux[0][:, 0:S], ACT.Copy).then_inc(s_rs, 1)

            act.wait_ge(s_prm, 16)
            split(Unit("ab", 0))

            def x_group(q):
                if q == 2:
                    split(Unit("ab", 1))
                act.wait_ge(s_x[q], 16)

            norm(0, x_group, lambda: split(Unit("ab", 2)))
            factors(0)

            def qkv_tiles(i, squares=True, also=None):
                for j in range(4):
                    split(Unit("qkv", j + 2, i))
                    c = i * 4 + j
                    square = c > 0 if isinstance(i, int) and i == 0 else squares or (i == 4 and j == 0)
                    if square:
                        act.wait_ge(s_silu, c)
                        after(act, g["qk_sums"], c - 2)
                    act.wait_ge(s_conv, c + 1)
                    tiles = qkv[:, :, :, :, :].rearrange("p a b c t -> p (a b c) t")
                    act.activation(tiles[:, c, :], cv[j % 2][:, :], ACT.Silu).then_inc(s_silu, 1)
                    if square:
                        act.activation(sqt[(j + 1) % 2][:, :], tiles[:, c - 1, :],
                                ACT.Square).then_inc(g["qk_squares"], 1)
                    if also is not None and j in also:
                        also[j]()

            def gate_logs():
                act.wait_ge(g["gate_sums"], 1)
                r = a_.mark(act.activation(gl[:, 1, :, :], gl[:, 0, :, :], ACT.Abs))
                act.wait_ge(a_.sem, r)
                r = a_.mark(act.activation(gl[:, 1, :, :], gl[:, 1, :, :], ACT.Exp, scale=-1.0))
                act.activation(gl[:, 5, :, :], aux[2][:, 0:S].rearrange("p (t c) -> p t c", t=TT)[:, :, 32:40],
                               ACT.Exp, scale=-1.0)
                act.activation(tiny[:, 64:72], alog, ACT.Exp)
                return r

            def gate_ln(r):
                act.wait_ge(a_.sem, r)
                act.activation(gl[:, 2, :, :], gl[:, 1, :, :], ACT.Ln, bias=1.0).then_inc(g["decay_exps"], 1)

            def gate_rows():
                act.wait_ge(g["rows_turned"], 1)
                act.activation(R[:, :], aux[2][:, 0:S], ACT.Copy).then_inc(g["rows_ready"], 1)
                act.activation(tiny[:, 40:48], tiny[:, 16:24], ACT.Exp).then_inc(g["g_exps"], 1)

            def roots():
                act.wait_ge(g["qk_sums"], 16)
                act.activation(tiny[:, 120:152], aux[1][:, 0:32], ACT.Sqrt, bias=eps).then_inc(g["qk_roots"], 1)

            def take_spread(n):
                act.wait_ge(g["spread"], n + 1)
                act.activation(bc[:, 0, :, :], aux[1][:, :], ACT.Copy)
                act.activation(bc[:, 1, :, :], aux[2][:, :], ACT.Copy).then_inc(g["spread_taken"], 1)

            r_exp = []
            qkv_tiles(0, also={1: lambda: r_exp.append(gate_logs()), 3: lambda: gate_ln(r_exp[0])})
            with act.Fori(1, 4) as i:
                qkv_tiles(i)
            qkv_tiles(4, False, {2: roots, 3: gate_rows})
            qkv_tiles(5, False, {1: lambda: take_spread(0)})

            def mix(i):
                n = i + 1
                act.activation(vw[:, :, :], qkv[:, 2, i, :, :], ACT.Copy).then_inc(g["v_placed"], 1)

                def exps():
                    act.wait_ge(g["decay_logs"], n)
                    act.activation(dt_[:, :, :], dt_[:, :, :], ACT.Exp).then_inc(g["decays"], 1)
                    act.activation(eg[:, :, :], bc[:, 0, :, P:S], ACT.Exp)
                    act.activation(tiny[:, 50:52], tiny[:, 48:50], ACT.Exp).then_inc(g["decay_exps"], 1)

                def zsilu():
                    act.wait_ge(s_free, Tile("mix", 1, i, 8).n + 1)
                    act.activation(zs[:, :, :], zs[:, :, :], ACT.Silu).then_inc(g["z_silu"], 1)

                def yev(l):
                    if l == 1:
                        act.wait_ge(g["att_ready"], n)
                    act.wait_ge(g["y_product"], i * (LEVELS - 1) + l)
                    act.activation(yb_[:, :, :], aux[2][:, :], ACT.Copy).then_inc(g["y_taken"], 1)

                def v0():
                    act.wait_ge(g["first_v"], n)
                    act.activation(vn0[:, :, :], aux[0][:, 0:256], ACT.Copy)
                    act.activation(wt[:, :, :], aux[0][:, 256:512], ACT.Copy,
                            scale=-1.0).then_inc(g["first_v_taken"], 1)

                def s1c():
                    act.wait_ge(g["state"], n)
                    act.activation(s1[:, :, :], aux[1][:, 0:256], ACT.Copy).then_inc(g["state_taken"], 1)

                def v1():
                    act.wait_ge(g["second_v"], n)
                    act.activation(vn1[:, :, :], aux[2][:, 0:256], ACT.Copy).then_inc(g["second_v_taken"], 1)

                def oev():
                    act.wait_ge(g["outputs"], n)
                    act.activation(ot[:, :, :], aux[3][:, :], ACT.Copy)
                    act.activation(osq[:, :, :], aux[3][:, :], ACT.Square).then_inc(g["outputs_taken"], 1)

                def oroot():
                    act.wait_ge(g["output_sums"], n)
                    act.activation(tiny[:, 72:76], aux[0][:, 0:4], ACT.Sqrt, bias=eps,
                            scale=1.0 / P).then_inc(g["output_roots"], 1)

                def high(a):
                    act.wait_ge(s_yf, 3 * i + 2 * a + 1)
                    act.activation(y4[:, i + 4, a, 0, :], cv[a][:, :], ACT.Copy).then_inc(s_yhi, 1)

                def out_high():
                    act.wait_ge(s_yf, 3 * i + 2)
                    act.activation(y4[:, i, :, 0, :], ot[:, :, :], ACT.Copy).then_inc(s_yhi, 1)

                plan = {0: [exps], 7: [zsilu], 15: [v0], 16: [lambda: high(0), s1c], 17: [v1], 18: [oev], 19: [oroot],
                        23: [lambda: take_spread(n), out_high]}
                for l in range(1, LEVELS):
                    plan.setdefault(1 + 2 * l, []).append(lambda l=l: yev(l))
                for j in range(8):
                    for s_ in range(3):
                        for f in plan.get(3 * j + s_, []):
                            f()
                    split(Unit("mix", j + 2, i, 8))
                high(1)

            y4 = yhl[:, :, :, :].rearrange("p (i a) l t -> p i a l t", a=2)
            n_last = 4
            with act.Fori(0, n_last) as i:
                mix(i)

            def look(phase, j, i=0, per=4):
                if isinstance(i, int):
                    off = U0[phase] + j + per * i + 2
                    if off >= UNITS:
                        return
                    nk = DN_K if any(U0[x] <= off < U0[x] + N_UNITS[x] for x in ("dn0", "dn1")) else KD
                else:
                    nk = DN_K if phase[:2] == "dn" else KD
                split(Unit(phase, j + 2, i, per), nk)

            def take_out(t, u, m, j, b):
                act.wait_ge(s_unit, u.n + 1)
                act.wait_ge(s_ssq, 17 * (j - 1) + 1 + m)
                act.activation(sqd[b][:, :], lin[t.bank][:, 0:S], ACT.Square).then_inc(s_msq, 1)
                act.activation(mout[:, m, :], lin[t.bank][:, 0:S], ACT.Copy,
                        scale=norm1[:, 2 * j - 1, m, :]).then_inc(s_free, 1)

            def out_phase(phase, jn):
                def tiles(i):
                    for j in range(4):
                        u, t = Unit(phase, j, i), Tile(phase, j, i, bank=j if phase == "out1" else None)
                        take_out(t, u, 4 * i + j, jn, j % 2)
                        if not isinstance(i, int) or j < 3:
                            look(phase, j, i)
                with act.Fori(0, 3) as i:
                    tiles(i)
                tiles(3)

            def up_phase(phase, layer):
                def pairs(i):
                    for a in range(2):
                        c = 2 * i + a
                        begin = isinstance(i, int) and i == 0 and a == 0
                        look(phase, 1 if begin else 2 * a, i)
                        act.wait_ge(s_conv, 24 + KF * layer + c + 1)
                        after(act, s_mid, KF * layer + c - 1)
                        act.activation(sil[a][:, :], cv[a][:, :], ACT.Silu).then_inc(s_silu, 1)
                        if not begin:
                            look(phase, 2 * a + 1, i)
                        act.wait_ge(s_mid, KF * layer + c + 1)
                        act.activation(mid[:, c, 0, :], mf[a][:, :], ACT.Copy).then_inc(s_midhi, 1)
                factors(2 * layer + 1)
                act.wait_ge(s_hstore, 16 * (2 * layer + 1))
                pairs(0)
                with act.Fori(1, 21) as i:
                    pairs(i)
                pairs(21)

            def down_phase(phase, jn):
                def tiles(i):
                    for a in range(2):
                        for q in range(4):
                            j = 4 * a + q
                            u, t = Unit(phase, j, i, 8), Tile(phase, a, i, 2)
                            if q == 3:
                                take_out(t, u, 2 * i + a, jn, a)
                            if not isinstance(i, int) or j < 7:
                                look(phase, j, i, 8)
                with act.Fori(0, 7) as i:
                    tiles(i)
                tiles(7)

            def junction(j, u=None):
                act.wait_ge(s_post, j)
                act.activation(tiny[:, 2:4], aux[1][:, 0:2], ACT.Sqrt, bias=eps, scale=1.0 / D).then_inc(s_root, 1)
                if j < 4:
                    split(Unit(u, 1))
                    norm(j, lambda q: act.wait_ge(s_hn, 4 * (j - 1) + q + 1), lambda: split(Unit(u, 2)))

            out_phase("out0", 1)
            junction(1, "gu0")
            up_phase("gu0", 0)
            down_phase("dn0", 2)
            junction(2, "gate")

            factors(2)

            def swap(t, u, b):
                act.wait_ge(s_unit, u.n + 1)
                act.activation(up[b][0:64, :], lin[t.bank][64:128, 0:S], ACT.Copy)
                act.activation(up[b][64:128, :], lin[t.bank][0:64, 0:S], ACT.Copy).then_inc(ns["halves_swapped"], 1)

            def kv(i):
                for j in range(8):
                    if j < 4:
                        after(act, ns["rotated"], 4 * i + j - 1)
                        swap(Tile("kv", j, i, 8), Unit("kv", j, i, 8), j % 2)
                    look("kv", j, i, 8)
                    if j == 6 and isinstance(i, int):
                        windows_high(0)
                    if j >= 5:
                        out_v(i, j - 5)
                    if j == 3 and isinstance(i, int):
                        act.wait_ge(ns["gates_turned"], 1)
                        act.activation(sig[:, :, :, :].rearrange("p t b h -> p t (b h)"),
                                       aux[1][:, 0:S].rearrange("p (t c) -> p t c", t=TT)[:, :, 0:48],
                                       ACT.Exp, scale=-1.0).then_inc(ns["gate_exps"], 1)
                out_v(i, 3)

            def out_v(i, g_):
                act.wait_ge(ns["values_turned"], 4 * i + g_ + 1)
                act.activation(vk[:, i, g_, :, :], aux[2 + g_ % 2][:, 0:S], ACT.Copy).then_inc(ns["values_kept"], 1)

            def windows_high(kind):
                act.wait_ge(ns["windows"], kind + 1)
                act.activation(xc[kind][:, :, 0, :], xct[:, :, :, :].rearrange("p l g c -> p l (g c)"),
                               ACT.Copy).then_inc(ns["windows_high"], 1)

            kv(0)
            windows_high(1)
            with act.Fori(1, 3) as i:
                kv(i)
            for kind in range(2):
                for ht in range(2):
                    for q in range(2):
                        j = 4 * kind + 2 * ht + q
                        if q == 1:
                            t = Tile("cmp", 2 * kind + ht)
                            act.wait_ge(s_unit, U0["cmp"] + j + 1)
                            act.activation(half[ht][:, :], lin[t.bank][:, CW:2 * CW], ACT.Copy).then_inc(s_half, 1)
                        look("cmp", j)
                act.wait_ge(s_free, T0["cmp"] + 2 * kind + 2)
                act.activation(h1[:, 2 * kind:2 * kind + 2, :], h1[:, 2 * kind:2 * kind + 2, :],
                               ACT.Gelu_apprx_tanh).then_inc(ns["hidden"], 1)

            def query(j, i):
                act.wait_ge(ns["rotated"], 12 + 4 * i + j - 1)
                swap(Tile("q", j, i, bank=j % 2), Unit("q", j, i), j % 2)

            def exps(h):
                act.wait_ge(ns["maxima"], h + 1)
                for b in range(2):
                    act.activation(sm0[:, b, :], sm0[:, b, :], ACT.Exp, bias=soft[:, 8 + b:9 + b], scale=SCALE,
                                   accum_out=soft[:, 16 + b:17 + b])
                    act.activation(sm1[:, b, :], sm1[:, b, :], ACT.Exp, bias=soft[:, 10 + b:11 + b], scale=SCALE,
                                   accum_out=soft[:, 18 + b:19 + b])
                    m = act.activation(smc[:, b, 0:WINS], smc[:, b, 0:WINS], ACT.Exp, bias=soft[:, 12 + b:13 + b],
                                       scale=SCALE, accum_out=soft[:, 20 + b:21 + b])
                m.then_inc(ns["exps"], 1)

            def take_p(h):
                act.wait_ge(ns["probs_turned"], h + 1)
                act.activation(pt[:, :, 0:P], aux[2][:, 0:S].rearrange("p (b t) -> p b t", b=2), ACT.Copy)
                act.activation(ptc[0:WINS, :], aux[2][0:WINS, S:2 * S], ACT.Copy)
                act.activation(pt[:, :, P:3 * P], aux[3][:, :].rearrange("p (b t) -> p b t", b=2),
                               ACT.Copy).then_inc(ns["probs_taken"], 1)

            def take_o(h, r):
                act.wait_ge(ns["output"], h + 1)
                after(act, s_ylo, 12 + h - 1)
                act.activation(of[r % 2][:, :], lin[2 + r % 2][:, 0:S], ACT.Copy)
                act.activation(yhl[:, h, 0, :], lin[2 + r % 2][:, 0:S], ACT.Copy).then_inc(ns["output_taken"], 1)

            def group(g_):
                after(act, ns["output"], 4 * g_)
                act.activation(vs[:, :, :, :], vk[:, 1:3, g_, :, :], ACT.Copy)
                act.activation(vcs[0:WINS, :], vc_[0:WINS, g_, :], ACT.Copy).then_inc(ns["group_values"], 1)

            def queries(i):
                for j in range(4):
                    if j > 1 or not isinstance(i, int):
                        take_p(4 * i + j - 2)
                    if j > 0 or not isinstance(i, int):
                        split(Unit("q", j + 1, i))
                        exps(4 * i + j - 1)
                    if j > 1 or not isinstance(i, int):
                        take_o(4 * i + j - 2, (j - 2) % 4)
                    if j == 1:
                        group(i)
                    query(j, i)
                    if j == 0 and isinstance(i, int):
                        act.wait_ge(ns["compressed"], 1)
                        act.activation(kc_[:, :, :], aux[0][:, 0:CW], ACT.Copy)
                        act.activation(vc_[0:WINS, :, :], aux[1][0:WINS, :],
                                ACT.Copy).then_inc(ns["compressed_kept"], 1)

            queries(0)
            with act.Fori(1, 4) as i:
                queries(i)
            take_p(14)
            split(Unit("q", 17))
            exps(15)
            take_o(14, 2)
            take_p(15)
            take_o(15, 3)
            out_phase("out1", 3)
            junction(3, "gu1")
            up_phase("gu1", 1)
            down_phase("dn1", 4)
            junction(4)

        @block.vector
        def _(dve):
            def split(u, nk=KD):
                dve.wait_ge(s_hi, u.n + 1)
                after(dve, s_unit, u.n - 1)
                dve.tensor_tensor(lo[u.half][:, 0:nk, :], raw[u.raw][:, 0:nk, :],
                                  hi[u.half][:, 0:nk, :].bitcast(F32), ALU.subtract).then_inc(s_lo, 1)

            def take(u, t, dst, factor):
                dve.wait_ge(s_unit, u.n + 1)
                dve.tensor_tensor(dst, lin[t.bank][:, 0:S], factor, ALU.mult).then_inc(s_free, 1)
                dve.wait_ge(s_free, t.n + 1)

            def step(ins):
                dve.wait_ge(v_.sem, v_.mark(ins))

            def norm_low(nn, q):
                w = normw[:, 2 * nn, :]
                dve.wait_ge(s_xhi, 4 * nn + q + 1)
                for c in range(4 * q, 4 * q + 4):
                    ins = dve.scalar_tensor_tensor(xhl[:, c, 1, :], hnew[:, c, :], w[:, c:c + 1],
                                                   xhl[:, c, 0, :].bitcast(F32), ALU.mult, ALU.subtract)
                ins.then_inc(s_xlo, 1)

            def diagonal(cols, dst, roots, count, done):
                dve.wait_ge(roots, count)
                step(dve.reciprocal(cols, cols))
                for t in range(dst.shape[1]):
                    ins = dve.tensor_scalar(dst[:, t, :], ident, cols[:, t:t + 1], None, ALU.mult)
                ins.then_inc(done, 1)

            for b in range(2):
                dve.memset(cbuf[b][:, :], 0.0)
            step(dve.memset(R[:, :], 0.0))
            dve.wait_ge(s_prm, 16)
            for q in range(4):
                dve.wait_ge(s_x[q], 16)
                norm_low(0, q)
                if q in (0, 2):
                    split(Unit("ab", q // 2))
            split(Unit("ab", 2))
            diagonal(tiny[:, 0:2], diag[1], s_root, 1, s_col)
            dve.wait_ge(s_rs, 1)
            take(Unit("ab", 0), Tile("ab", 0), abf[:, :], rstd[:, :])
            step(dve.tensor_tensor(sqd[0][:, :], rstd[:, :], rstd[:, :], ALU.mult))

            def conv(dst, src, w, taps, last):
                step(dve.tensor_scalar(dst, src[:, 0:S], w(0), None, ALU.mult))
                for k in range(1, taps):
                    ins = dve.scalar_tensor_tensor(dst, src[:, k:k + S], w(k), dst, ALU.mult, ALU.add)
                    if k < taps - 1:
                        step(ins)
                    elif last is not None:
                        ins.then_inc(last, 1)
                    else:
                        step(ins)

            def qkv_tiles(i, also=None):
                for j in range(4):
                    t = Tile("qkv", j, i, bank=(j + 1) % 2 if isinstance(i, int) and i == 5 else None)
                    c = i * 4 + j
                    if also is not None and j in also:
                        also[j]()
                    take(Unit("qkv", j, i), t, cbuf[j % 2][:, 3:3 + S], rstd[:, :])
                    after(dve, s_silu, c - 1)
                    conv(cv[j % 2][:, :], cbuf[j % 2], lambda k: gconv[:, c, k:k + 1], 4, s_conv)
                    if not isinstance(i, int) or i < 5 or j < 3:
                        split(Unit("qkv", j + 2, i))

            def gates_first():
                logits = aux[2][:, 0:S].rearrange("p (t c) -> p t c", t=TT)
                dve.wait_ge(g["ab_turned"], 1)
                dve.tensor_tensor(gl[:, 0, :, :], logits[:, :, 0:8], dtb.unsqueeze(1).broadcast_to([P, TT, HEADS]),
                                  ALU.add).then_inc(g["gate_sums"], 1)

            def gates_second():
                a0, a1, a2, a3, a4, a5 = [gl[:, k, :, :] for k in range(6)]
                dve.wait_ge(g["decay_exps"], 1)
                step(dve.tensor_scalar(a3, a1, 1.0, None, ALU.add))
                dve.tensor_scalar(a5, a5, 1.0, None, ALU.add)
                step(dve.scalar_tensor_tensor(a4, a3, -1.0, a1, ALU.add, ALU.subtract))
                dve.reciprocal(bcol.rearrange("p t i a -> p t (i a)"), a5)
                step(dve.reciprocal(a3, a3))
                step(dve.tensor_tensor(a4, a4, a3, ALU.mult))
                step(dve.tensor_tensor(a2, a2, a4, ALU.subtract))
                step(dve.scalar_tensor_tensor(a2, a0, 0.0, a2, ALU.max, ALU.add))
                dve.scalar_tensor_tensor(a2, a2, -1.0, tiny[:, 64:72].unsqueeze(1).broadcast_to([P, TT, HEADS]),
                                         ALU.mult, ALU.mult).then_inc(g["gate_logs"], 1)

            def gates_third():
                dve.tensor_copy(gb_[:, :, 32:40], bcol.rearrange("p t i a -> p t (i a)"))
                dve.wait_ge(g["cumulated"], 1)
                cum = aux[3][:, 0:TT * HEADS].rearrange("p (t h) -> p t h", t=TT)
                dve.tensor_copy(gcol.rearrange("p t i a -> p t (i a)"), cum)
                dve.tensor_copy(gb_[:, :, 0:8], cum).then_inc(g["gates_placed"], 1)

            def norm_columns():
                dve.wait_ge(g["qk_roots"], 1)
                dve.reciprocal(rc[:, 0:32].rearrange("p (i k c) -> p k i c", k=2, c=4),

                                                                     tiny[:, 120:152].rearrange("p (k i c) -> p k i c", k=2, c=4)).then_inc(g["qk_columns"], 1)

            def exp_beta():
                dve.wait_ge(g["g_exps"], 1)
                dve.tensor_tensor(bge, bge, bcol[:, 1, :, :], ALU.mult)

            dve.memset(gb_[:, :, :], 0.0)
            dve.memset(rc[:, 32:40], 0.0)
            qkv_tiles(0, {2: gates_first})
            with dve.Fori(1, 4) as i:
                v_.enter(i, 12, first=1)
                qkv_tiles(i)
                v_.leave(4)
            qkv_tiles(4, {0: gates_second, 2: gates_third, 3: norm_columns})
            qkv_tiles(5, {1: exp_beta})

            y4 = yhl[:, :, :, :].rearrange("p (i a) l t -> p i a l t", a=2)

            def mix(i):
                n = i + 1
                def qk_norm():
                    dve.wait_ge(g["qk_factors"], n)
                    dve.tensor_tensor(kn[:, :, :], qkv[:, 1, i, :, :], lin[3][:, :].rearrange("p (h t) -> p h t", h=2),
                                      ALU.mult).then_inc(g["k_normed"], 1)
                    dve.wait_ge(g["spread_taken"], n)
                    for t in range(2):
                        for h in range(2):
                            dve.tensor_scalar(dt_[:, 2 * h + t, :], bc[:, 0, h, t * P:(t + 1) * P],
                                              gcol[:, t, i, h:h + 1], 0.0, ALU.subtract, ALU.min)
                    for h in range(2):
                        ins = dve.tensor_scalar(tiny[:, 48 + h:49 + h], bc[:, 0, h, P - 1:P],
                                                gcol[:, 0, i, h:h + 1], None, ALU.subtract)
                    ins.then_inc(g["decay_logs"], 1)
                    dve.scalar_tensor_tensor(qn[:, :, :], qkv[:, 0, i, :, :], SCALE,
                                             lin[2][:, :].rearrange("p (h t) -> p h t", h=2), ALU.mult, ALU.mult)
                    dve.wait_ge(g["k_normed"], n)
                    dve.tensor_tensor(kb[:, :, :], kn[:, :, :], bc[:, 1, :, :], ALU.mult).then_inc(g["k_beta"], 1)
                    split(Unit("mix", 1, i, 8))
                    dve.wait_ge(g["k_beta"], n)
                    dve.wait_ge(g["decay_exps"], n + 1)
                    dve.tensor_tensor(qg[:, :, :], qn[:, :, P:S], eg[:, :, :], ALU.mult).then_inc(g["q_decayed"], 1)

                def vbs():
                    dve.wait_ge(g["kv_turned"], n)
                    for h in range(2):
                        for t in range(2):
                            q = 2 * h + t
                            dve.tensor_scalar(vb[:, q, :], aux[3][:, q * P:(q + 1) * P], bcol[:, t, i, h:h + 1],
                                              None, ALU.mult)
                        dve.tensor_scalar(kdec[:, h, :], aux[2][:, 2 * h * P:(2 * h + 1) * P],
                                          tiny[:, 50 + h:51 + h], None, ALU.mult)
                        ins = dve.tensor_scalar(kbg[:, h, :], aux[2][:, (2 * h + 1) * P:(2 * h + 2) * P],
                                                bge[:, i, h:h + 1], None, ALU.mult)
                    ins.then_inc(g["v_scaled"], 1)

                def masks():
                    dve.wait_ge(g["grams"], n)
                    dve.wait_ge(g["decays_masked"], n)
                    dve.tensor_tensor(lt[:, :, :], aux[0][:, :].rearrange("p (q j) -> p q j", q=4), dt_[:, :, :],
                                      ALU.mult).then_inc(g["lt_ready"], 1)
                    dve.wait_ge(g["lt_ready"], n)
                    dve.tensor_tensor(nt[0][:, :, :], lt[:, :, :], level[:, 0, :].unsqueeze(1).broadcast_to([P, 4, P]),
                                      ALU.mult).then_inc(g["level_0_masked"], 1)
                    dve.tensor_tensor(att[:, :, :], aux[1][:, :].rearrange("p (q j) -> p q j", q=4), dt_[:, :, :],
                                      ALU.mult).then_inc(g["att_ready"], 1)

                def level_0():
                    dve.wait_ge(g["z_product"], i * LEVELS + 1)
                    dve.tensor_tensor(X[:, :, :], ident.unsqueeze(1).broadcast_to([P, 4, P]),
                                      aux[3][:, :].rearrange("p (q j) -> p q j", q=4),
                                              ALU.subtract).then_inc(g["inverse_step"], 1)

                def inv(l):
                    dve.wait_ge(g["z_product"], i * LEVELS + l + 1)
                    s_ = 1 << l
                    for k, m in ((0, X), (1, PT)):
                        v = m[:, :, :].rearrange("p q (b h s) -> p (q b) h s", h=2, s=s_)[:, :, k, :]
                        z = aux[3][:, 256 * k:256 * (k + 1)].rearrange("p (b s) -> p b s", s=s_)
                        ins = dve.tensor_tensor(v, v, z, ALU.subtract)
                    ins.then_inc(g["inverse_step"], 1)

                def out_diag():
                    diagonal(tiny[:, 72:76], do_, g["output_roots"], n, g["output_diag"])

                def low(a):
                    dve.wait_ge(s_yhi, 3 * i + 2 * a + 1)
                    dve.tensor_tensor(y4[:, i + 4, a, 1, :], cv[a][:, :], y4[:, i + 4, a, 0, :].bitcast(F32),
                                      ALU.subtract).then_inc(s_ylo, 1)

                def out_scaled():
                    dve.wait_ge(g["output_factors"], n)
                    dve.wait_ge(g["z_silu"], n)
                    step(dve.scalar_tensor_tensor(ot[:, :, :], ot[:, :, :], gnorm,
                                                  aux[0][:, :].rearrange("p (h t) -> p h t", h=2), ALU.mult, ALU.mult))
                    dve.tensor_tensor(ot[:, :, :], ot[:, :, :], zs[:, :, :], ALU.mult).then_inc(s_yf, 1)

                def out_low():
                    dve.wait_ge(s_yhi, 3 * i + 2)
                    dve.tensor_tensor(y4[:, i, :, 1, :], ot[:, :, :], y4[:, i, :, 0, :].bitcast(F32),
                                      ALU.subtract).then_inc(s_ylo, 1)

                plan = {0: [qk_norm, vbs], 1: [masks], 2: [level_0], 17: [lambda: low(0)], 19: [out_diag],
                        22: [out_scaled]}
                for l in range(1, LEVELS):
                    plan.setdefault(2 + 2 * l, []).append(lambda l=l: inv(l))
                for j in range(8):
                    for s_ in range(3):
                        for f in plan.get(3 * j + s_, []):
                            f()
                    u, t = Unit("mix", j, i, 8), Tile("mix", j, i, 8, bank=(j + 1) % 2)
                    a, w = (j - 2) // 3, (j - 2) % 3
                    if j < 2:
                        take(u, t, zs[:, j, :], rstd[:, :])
                    elif w == 0:
                        take(u, t, up[0][:, :], sqd[0][:, :])
                    elif w == 1:
                        take(u, t, cbuf[a][:, 3:3 + S], up[0][:, :])
                        conv(cv[a][:, :], cbuf[a][:, 1:3 + S], lambda k: sconv[:, i, a, k:k + 1], 3, None)
                    else:
                        take(u, t, up[0][:, :], rstd[:, :])
                        dve.tensor_tensor(cv[a][:, :], cv[a][:, :], up[0][:, :], ALU.mult).then_inc(s_yf, 1)
                    if j < 7:
                        split(Unit("mix", j + 2, i, 8))
                out_low()
                low(1)

            MIX_STEPS = 8
            with dve.Fori(0, 4) as i:
                v_.enter(i, MIX_STEPS)
                mix(i)
                v_.leave(4)
            split(Unit("out0", 1))

            def look(phase, j, i=0, per=4):
                if isinstance(i, int):
                    off = U0[phase] + j + per * i + 2
                    if off >= UNITS:
                        return
                    nk = DN_K if any(U0[x] <= off < U0[x] + N_UNITS[x] for x in ("dn0", "dn1")) else KD
                else:
                    nk = DN_K if phase[:2] == "dn" else KD
                split(Unit(phase, j + 2, i, per), nk)

            def add_square(m, j, b):
                dve.wait_ge(s_msq, 16 * (j - 1) + m + 1)
                dve.wait_ge(s_ssq, 17 * (j - 1) + 1 + m)
                dve.tensor_tensor(ssq[:, :], ssq[:, :], sqd[b][:, :], ALU.add).then_inc(s_ssq, 1)

            def out_phase(phase, jn):
                dve.memset(ssq[:, :], 0.0).then_inc(s_ssq, 1)
                def tiles(i):
                    for j in range(4):
                        add_square(4 * i + j, jn, j % 2)
                        if not isinstance(i, int) or j < 3:
                            look(phase, j, i)
                with dve.Fori(0, 3) as i:
                    tiles(i)
                tiles(3)

            def up_phase(phase, layer):
                def pairs(i):
                    for a in range(2):
                        c = 2 * i + a
                        take(Unit(phase, 2 * a, i), Tile(phase, 2 * a, i), cbuf[a][:, 3:3 + S], rstd[:, :])
                        dve.wait_ge(s_silu, 24 + KF * layer + c - 1)
                        conv(cv[a][:, :], cbuf[a][:, 1:3 + S], lambda k: fconv[:, layer, c, k:k + 1], 3, s_conv)
                        begin = isinstance(i, int) and i == 0 and a == 0
                        look(phase, 1 if begin else 2 * a, i)
                        take(Unit(phase, 2 * a + 1, i), Tile(phase, 2 * a + 1, i), up[a][:, :], rstd[:, :])
                        dve.wait_ge(s_silu, 24 + KF * layer + c + 1)
                        after(dve, s_midhi, KF * layer + c - 1)
                        dve.tensor_tensor(mf[a][:, :], sil[a][:, :], up[a][:, :], ALU.mult).then_inc(s_mid, 1)
                        if not begin:
                            look(phase, 2 * a + 1, i)
                        dve.wait_ge(s_midhi, KF * layer + c + 1)
                        dve.tensor_tensor(mid[:, c, 1, :], mf[a][:, :], mid[:, c, 0, :].bitcast(F32),
                                          ALU.subtract).then_inc(s_midlo, 1)
                dve.wait_ge(s_rs, 2 * layer + 2)
                pairs(0)
                with dve.Fori(1, 21) as i:
                    v_.enter(i, 4, first=1)
                    pairs(i)
                    v_.leave(21)
                pairs(21)

            def down_phase(phase, jn):
                dve.memset(ssq[:, :], 0.0).then_inc(s_ssq, 1)
                def tiles(i):
                    for a in range(2):
                        for q in range(4):
                            if q == 3:
                                add_square(2 * i + a, jn, a)
                            if not isinstance(i, int) or 4 * a + q < 7:
                                look(phase, 4 * a + q, i, 8)
                with dve.Fori(0, 7) as i:
                    tiles(i)
                tiles(7)

            def junction(j, last, u=None):
                diagonal(tiny[:, 2:4], diag[0], s_root, 2 * j, s_pdiag)
                dve.wait_ge(s_pbc, j)
                dve.wait_ge(s_hload, 16 * j)
                dve.wait_ge(s_free, T0[last] + 16)

                def add(q):
                    m4 = mout[:, 4 * q:4 * q + 4, :]
                    step(dve.tensor_tensor(m4, m4, aux[1][:, 0:S].unsqueeze(1).broadcast_to([P, 4, S]), ALU.mult))
                    dve.tensor_tensor(hnew[:, 4 * q:4 * q + 4, :], m4, hold[:, 4 * q:4 * q + 4, :],
                                      ALU.add).then_inc(s_hn, 1)

                for q in range(5):
                    if q < 4:
                        add(q)
                    if q > 0 and j < 4:
                        norm_low(j, q - 1)
                    if q == 1 and j < 4:
                        split(Unit(u, 1))
                if j < 4:
                    split(Unit(u, 2))
                    diagonal(tiny[:, 0:2], diag[1], s_root, 2 * j + 1, s_col)

            out_phase("out0", 1)
            junction(1, "out0", "gu0")
            up_phase("gu0", 0)
            down_phase("dn0", 2)
            junction(2, "dn0", "gate")

            dve.wait_ge(s_hstore, 32)
            dve.wait_ge(s_l1c, 16)
            dve.wait_ge(s_rs, 3)
            take(Unit("gate", 0), Tile("gate", 0), gts[:, :], rstd[:, :])
            for name in ("cos", "sin"):
                ins = dve.tensor_tensor(C1[name], C1[name], rstd[:, :], ALU.mult)
            step(ins)

            def rotary(u, t, b, dst, count):
                dve.wait_ge(ns["halves_swapped"], count)
                take(u, t, cv[b][:, :], C1["cos"])
                step(dve.tensor_tensor(up[b][:, :], up[b][:, :], C1["sin"], ALU.mult))
                dve.tensor_tensor(dst, cv[b][:, :], up[b][:, :], ALU.add).then_inc(ns["rotated"], 1)

            def kv(i):
                for j in range(8):
                    u, t = Unit("kv", j, i, 8), Tile("kv", j, i, 8)
                    if j < 4:
                        rotary(u, t, j % 2, kt[:, i, j, :], 4 * i + j + 1)
                    else:
                        after(dve, ns["values_turned"], 4 * (i - 1) + j - 3)
                        take(u, t, vst[:, j - 4, :], rstd[:, :])
                    look("kv", j, i, 8)
                    if j == 5 and isinstance(i, int):
                        windows(0)
                    if j == 7 and isinstance(i, int):
                        windows_low(0)
                    if j == 4 and isinstance(i, int):
                        dve.wait_ge(ns["gate_exps"], 1)
                        sg = sig[:, :, :, :].rearrange("p t b h -> p (t b h)")
                        step(dve.tensor_scalar(sg, sg, 1.0, None, ALU.add))
                        step(dve.reciprocal(sg, sg))
                        for t_ in range(TT):
                            dve.tensor_copy(gt[:, :, 2 * t_:2 * t_ + 2], sig[:, t_, 1:3, :].rearrange("p b h -> p h b"))
                            ins = dve.tensor_copy(gt[:, :, 4 + t_:5 + t_], sig[:, t_, 0:1, :].rearrange("p b h -> p h b"))
                        step(ins)

            def windows(kind):
                pos = C1["posv" if kind else "posk"].rearrange("p (a b) -> p a b", a=2)
                src = (vst[:, :, :] if kind else kt[:, 0, :, :]).rearrange("p g (w b) -> p g w b", b=16)
                dve.wait_ge(ns["rotated"], 4)
                if kind:
                    dve.wait_ge(ns["windows_low"], 1)
                for a in range(2):
                    ins = dve.tensor_tensor(xct[:, 16 * a:16 * a + 16, :, :],
                                            src[:, :, a:a + WINS, :].rearrange("p g w b -> p b g w"),
                                            pos[:, a, :].unsqueeze(2).unsqueeze(3).broadcast_to([P, 16, NG, WINS]),
                                            ALU.add)
                ins.then_inc(ns["windows"], 1)
                dve.memset(xf[kind][:, 64 * CW:].bitcast(F32), 0.0)

            def windows_low(kind):
                dve.wait_ge(ns["windows_high"], kind + 1)
                dve.tensor_tensor(xc[kind][:, :, 1, :], xct[:, :, :, :].rearrange("p l g c -> p l (g c)"),
                                  xc[kind][:, :, 0, :].bitcast(F32), ALU.subtract).then_inc(ns["windows_low"], 1)

            kv(0)
            windows(1)
            windows_low(1)
            with dve.Fori(1, 3) as i:
                v_.enter(i, 4, first=1)
                kv(i)
                v_.leave(3)
            for kind in range(2):
                for ht in range(2):
                    for q in range(2):
                        if q == 1:
                            t = Tile("cmp", 2 * kind + ht)
                            dve.wait_ge(s_half, 2 * kind + ht + 1)
                            dve.tensor_tensor(h1[:, 2 * kind + ht, :], lin[t.bank][:, 0:CW], half[ht][:, :],
                                              ALU.add).then_inc(s_free, 1)
                        look("cmp", 4 * kind + 2 * ht + q)

            def query(j, i):
                after(dve, ns["scores"], 4 * (i - 1) + j + 1)
                rotary(Unit("q", j, i), Tile("q", j, i, bank=j % 2), j % 2, qs[:, j, :], 12 + 4 * i + j + 1)

            def maxima(h):
                dve.wait_ge(ns["scores"], h + 1)
                after(dve, ns["probs_turned"], h)
                dve.tensor_tensor(smc[:, :, 0:WINS], aux[0][:, S:S + 32].rearrange("p (t c) -> p t c", t=2)[:, :, 0:WINS],
                                  C1["cmask"].rearrange("p (t c) -> p t c", t=2), ALU.add)
                dve.tensor_tensor(sm0[:, :, :], aux[0][:, 0:S].rearrange("p (b k) -> p b k", b=2),
                                  C1["causal"][:, P:S].unsqueeze(1).broadcast_to([P, 2, P]), ALU.add)
                step(dve.tensor_tensor(sm1[:, :, :], aux[1][:, :].rearrange("p (b k) -> p b k", b=2),
                                       C1["causal"][:, 0:S].unsqueeze(1).broadcast_to([P, 2, S]), ALU.add))
                dve.tensor_reduce(soft[:, 0:2], sm0[:, :, :], AX.X, ALU.max)
                dve.tensor_reduce(soft[:, 2:4], sm1[:, :, :], AX.X, ALU.max)
                step(dve.tensor_reduce(soft[:, 4:6], smc[:, :, 0:WINS], AX.X, ALU.max))
                dve.tensor_scalar(soft[:, 8:14], soft[:, 0:6], -SCALE, None, ALU.mult).then_inc(ns["maxima"], 1)

            def weigh(h):
                dve.wait_ge(ns["exps"], h + 1)
                step(dve.reciprocal(soft[:, 24:30], soft[:, 16:22]))
                step(dve.tensor_tensor(soft[:, 24:30], soft[:, 24:30], gt[:, h, :], ALU.mult))
                for b in range(2):
                    dve.tensor_scalar(sm0[:, b, :], sm0[:, b, :], soft[:, 24 + b:25 + b], None, ALU.mult)
                    dve.tensor_scalar(sm1[:, b, :], sm1[:, b, :], soft[:, 26 + b:27 + b], None, ALU.mult)
                    ins = dve.scalar_tensor_tensor(smc[:, b, 0:WINS], smc[:, b, 0:WINS], soft[:, 28 + b:29 + b],
                                                   C1["cvalid"].rearrange("p (t c) -> p t c", t=2)[:, b, :],
                                                   ALU.mult, ALU.mult)
                ins.then_inc(ns["probs"], 1)

            def low(h, r):
                dve.wait_ge(ns["output_taken"], h + 1)
                dve.tensor_tensor(yhl[:, h, 1, :], of[r % 2][:, :], yhl[:, h, 0, :].bitcast(F32),
                                  ALU.subtract).then_inc(s_ylo, 1)

            def queries(i):
                for j in range(4):
                    if j > 0 or not isinstance(i, int):
                        maxima(4 * i + j - 1)
                        split(Unit("q", j + 1, i))
                        weigh(4 * i + j - 1)
                    if j > 1 or not isinstance(i, int):
                        low(4 * i + j - 2, (j - 2) % 4)
                    query(j, i)

            queries(0)
            with dve.Fori(1, 4) as i:
                v_.enter(i, 20, first=1)
                queries(i)
                v_.leave(4)
            maxima(15)
            split(Unit("q", 17))
            weigh(15)
            low(14, 2)
            low(15, 3)
            out_phase("out1", 3)
            junction(3, "out1", "gu1")
            up_phase("gu1", 1)
            down_phase("dn1", 4)
            junction(4, "dn1")

        @block.gpsimd
        def _(pool):
            def add_squares(norm):
                def step(ins):
                    pool.wait_ge(p_.sem, p_.mark(ins))

                for q in range(4):
                    pool.wait_ge(s_sq4, 4 * norm + q + 1)
                    sq = sq4[q % 2]
                    step(pool.tensor_tensor(sq[:, 0:2, :], sq[:, 0:2, :], sq[:, 2:4, :], ALU.add))
                    if q > 0:
                        step(pool.tensor_tensor(sq[:, 0, :], sq[:, 0, :], sq[:, 1, :], ALU.add))
                    pool.tensor_tensor(acc[:, :], acc[:, :] if q > 0 else sq[:, 1, :], sq[:, 0, :],
                                       ALU.add).then_inc(s_acc, 1)
                    if q < 3:
                        pool.wait_ge(s_acc, 4 * norm + q + 1)

            add_squares(0)
            pool.wait_ge(s_prm, 16)
            pool.wait_ge(s_l0c, 16)

            def select(n):
                pool.tensor_tensor(sel[:, :, :], ones.unsqueeze(1).broadcast_to([P, 4, P]),
                                   onehot[:, n, :].unsqueeze(2).broadcast_to([P, 4, P]),
                                           ALU.mult).then_inc(g["selector"], 1)

            def diagonals(n):
                pool.tensor_tensor(dqk[:, :, :], ident.unsqueeze(1).broadcast_to([P, 8, P]),
                                   rc[:, bass.ds(8 * n, 8)].unsqueeze(2).broadcast_to([P, 8, P]),
                                   ALU.mult).then_inc(g["qk_diag"], 1)

            pool.wait_ge(g["rows_ready"], 1)
            select(0)
            pool.wait_ge(g["qk_columns"], 1)
            diagonals(0)
            with pool.Fori(0, 4) as i:
                n = i + 1
                pool.wait_ge(g["decays"], n)
                four = [P, 4, P]
                pool.tensor_tensor(dt_[:, :, :], dt_[:, :, :], triu.unsqueeze(1).broadcast_to(four),
                                   ALU.mult).then_inc(g["decays_masked"], 1)
                pool.wait_ge(g["lt_ready"], n)
                for l in range(1, LEVELS):
                    if l >= 3:
                        pool.wait_ge(g["y_product"], i * (LEVELS - 1) + l - 2)
                    if l == 2:
                        pool.wait_ge(g["z_product"], i * LEVELS + 1)
                        pool.wait_ge(g["pt_begun"], n)
                    pool.tensor_tensor(nt[l % 2][:, :, :], lt[:, :, :], level[:, l, :].unsqueeze(1).broadcast_to(four),
                                       ALU.mult).then_inc(g["level_masked"], 1)
                    if l == 1:
                        pool.wait_ge(g["level_0_masked"], n)
                        pool.tensor_tensor(PT[:, :, :], ident.unsqueeze(1).broadcast_to(four), nt[0][:, :, :],
                                           ALU.subtract).then_inc(g["pt_begun"], 1)
                select(n)
                pool.wait_ge(g["second_v"], n)
                diagonals(n)
            for norm in range(1, 4):
                add_squares(norm)


def layouts(np, a):
    f = np.float32

    def chunks(v):
        v = v.reshape(v.shape[:-1] + (v.shape[-1] // P, P))
        return np.moveaxis(v, -1, 0)

    def units(w, cols):
        k = w.shape[0] // P
        return np.ascontiguousarray(w.reshape(k, P, w.shape[1])[:, :, cols].reshape(k, P, -1, P).transpose(2, 1, 0, 3))

    r = {}
    r["x"] = np.ascontiguousarray(a["x"][0].T.reshape(KD, P, S).transpose(1, 0, 2))
    w0 = a["ab_w_in"][0]
    ab = np.zeros((D, P), w0.dtype)
    ab[:, 0:8] = w0[:, 4096:4104]
    ab[:, 32:40] = w0[:, 4104:4112]
    cols = list(range(3072))
    z, hb, gb, gc = 3072, 4112, 5136, 6160
    for i in range(4):
        for s_, t in ((z, 0), (z, 1), (hb, 0), (gc, 0), (gb, 0), (hb, 1), (gc, 1), (gb, 1)):
            c = s_ + (2 * i + t) * P
            cols += list(range(c, c + P))
    r["w_in0"] = np.concatenate([units(ab, np.arange(P)), units(w0, np.array(cols))], 0)
    prm = np.zeros((P, N_PARAM), f)

    def put(name, v):
        c, w = PARAM[name]
        prm[:, c:c + w] = v.reshape(P, w)

    put("norm", chunks(a["norm_w"].reshape(8, D)))
    put("gconv", chunks(a["gdn_conv"][0]).transpose(0, 2, 1))
    put("sconv", chunks(a["sc_conv"][0]).transpose(0, 2, 1))
    put("fconv", chunks(a["ffn_conv"]).transpose(0, 1, 3, 2))
    put("gnorm", a["gdn_norm"][0][:, None])
    put("alog", np.broadcast_to(a["gdn_a_log"][0], (P, HEADS)))
    put("dtb", np.broadcast_to(a["gdn_dt_bias"][0], (P, HEADS)))
    put("eps", np.full((P, 1), EPS, f))
    oh = np.zeros((P, HEADS + 2, 2), f)
    for h in range(8):
        oh[h, h, 0] = 1
        oh[32 + h, h, 1] = 1
    put("onehot", oh)
    put("ident", np.eye(P, dtype=f))
    put("ones", np.ones((P, P), f))
    r["params"] = prm
    j, i = np.arange(P)[:, None], np.arange(P)[None, :]
    l0 = [(i >= j).astype(f)]
    for l in range(LEVELS):
        s_ = 1 << l
        l0.append(((i // (2 * s_) == j // (2 * s_)) & (j // s_ % 2 == 0) & (i // s_ % 2 == 1)).astype(f))
    r["l0c"] = np.concatenate(l0, 1)
    every = np.arange(D)
    r["w_out0"] = units(a["ab_w_out"][0], every)
    r["w_out1"] = units(a["nsa_w_out"][0], every)
    for l in range(2):
        gu = a["ffn_w_gu"][l]
        cols = np.arange(2 * FF).reshape(2, KF, P).transpose(1, 0, 2).ravel()
        r[f"w_gu{l}"] = units(gu, cols)
        dn = units(a["ffn_w_down"][l], every)
        r[f"w_dn{l}"] = np.ascontiguousarray(dn.reshape(KD, P, 4, DN_K, P).transpose(0, 2, 1, 3, 4)).reshape(64, P, DN_K, P)
    w1 = a["nsa_w_in"][0]
    gates = np.zeros((D, P), w1.dtype)
    gates[:, 0:48] = w1[:, 5120:5168]
    r["w_in1"] = np.concatenate([units(gates, np.arange(P)), units(w1, np.arange(2048, 5120)), units(w1, every)], 0)
    c = []
    for name in ("cmp_w1_k", "cmp_w1_v"):
        c.append(a[name][0].reshape(2, 16, P, 2, P).transpose(3, 0, 2, 1, 4).reshape(4, P, 16, P))
    r["w_cmp"] = np.ascontiguousarray(np.concatenate(c, 0))
    l1 = np.zeros((P, N_L1C), f)

    def put1(name, v):
        c, w = L1C[name]
        l1[:, c:c + w] = v.reshape(P, w)

    inv = 1.0 / (10000.0 ** (np.arange(0, P, 2, dtype=f) / f(P)))
    ang = (np.arange(S, dtype=f)[:, None] * inv[None, :].astype(f)).astype(f)
    put1("cos", np.concatenate([np.cos(ang).T, np.cos(ang).T], 0))
    put1("sin", np.concatenate([-np.sin(ang).T, np.sin(ang).T], 0))
    causal = np.where(np.arange(P)[None, :] <= np.arange(P)[:, None], 0, NEG).astype(f)
    put1("causal", np.concatenate([np.zeros((P, P), f), causal], 1))
    tok = np.arange(S).reshape(TT, P).T[:, :, None]
    ok = np.arange(WINS)[None, None, :] * 16 + 31 <= tok
    put1("cmask", np.where(ok | (tok < 31), 0, NEG).astype(f))
    put1("cvalid", ok.astype(f))
    put1("posk", a["cmp_pos_k"][0].T)
    put1("posv", a["cmp_pos_v"][0].T)
    for n, k in (("w2k", "cmp_w2_k"), ("w2v", "cmp_w2_v")):
        put1(n, a[k][0].reshape(2, P, P).transpose(1, 0, 2))
    r["l1c"] = l1
    return r



def kernel(**inputs):
    import numpy as np
    import concourse.bacc as bacc
    from concourse.bass_utils import run_bass_kernel_spmd

    nc = bacc.Bacc("TRN2", target_bir_lowering=False, num_devices=1)
    arrays = {"in_" + k: v for k, v in layouts(np, {k: np.asarray(v) for k, v in inputs.items()}).items()}
    A = {k[3:]: nc.dram_tensor(k, v.shape, F32, kind="ExternalInput").ap() for k, v in arrays.items()}
    A["residual"] = nc.dram_tensor("residual", (P, KD, S), F32, kind="Internal").ap()
    out = nc.dram_tensor("out", (P, KD, S), F32, kind="ExternalOutput").ap()
    build(nc, A, out)
    got = run_bass_kernel_spmd(nc, [arrays], core_ids=[0]).results[0]["out"]
    return np.ascontiguousarray(got.transpose(1, 0, 2).reshape(D, S).T[None])
```
